# Optimizing a Trainium2 kernel written in Bass

```python
import math, functools
import jax, jax.numpy as jnp
from jax import lax
import numpy as np

D_MODEL = 1024
BATCH = 1
SEQ = 512
DEPTH = 1
DEC_BATCH = 8
DEC_SEQ = 1
PAST_LEN = 1024
PAGE_SIZE = 128

N_META = 16
RW_HEADS = 8
RW_DH = 64
RW_W = RW_HEADS * RW_DH
DECAY_LORA = 64
AAA_LORA = 64
GATE_LORA = 128
RW_COLS = 3 * RW_W + DECAY_LORA + AAA_LORA + GATE_LORA
RW_SPLITS = (RW_W, 2 * RW_W, 3 * RW_W, 3 * RW_W + DECAY_LORA, 3 * RW_W + DECAY_LORA + AAA_LORA)
LNX_EPS = 64e-5
DF_HEADS = 4
DF_DK = 64
DF_DV = 2 * DF_DK
DF_W = DF_HEADS * DF_DV
DF_COLS = 3 * DF_W
MIX_W = RW_W + DF_W
IN_COLS = RW_COLS + DF_COLS
ROPE_THETA = 10000.0
Q_BLOCK = 128
SUBLN_EPS = 1e-5
LN_EPS = 1e-5
PK_HEADS = 8
N_KEYS = 128
N_EXPERTS = N_KEYS * N_KEYS
PK_DQ = 128
PK_TOPK = 16
PEER_BLOCK = 256
DEEP_ALPHA = (2 * DEPTH) ** 0.25
DEEP_BETA = (8 * DEPTH) ** -0.25

kernel_name = 'hymba_rwkv7_diffattn_peer_decode_step'

def layer_norm(x, w, b):
    xf = x.astype(jnp.float32)
    mu = xf.mean(-1, keepdims=True)
    var = jnp.mean(jnp.square(xf - mu), -1, keepdims=True)
    return ((xf - mu) * lax.rsqrt(var + LN_EPS) * w.astype(jnp.float32) + b.astype(jnp.float32)).astype(x.dtype)

def rope(x, pos):
    half = x.shape[-1] // 2
    inv = ROPE_THETA ** (-jnp.arange(half, dtype=jnp.float32) / half)
    ang = pos.astype(jnp.float32)[:, None] * inv[None, :]
    ang = ang.reshape(ang.shape[:1] + (1,) * (x.ndim - 3) + (half,))
    cos, sin = jnp.cos(ang), jnp.sin(ang)
    xf = x.astype(jnp.float32)
    x1, x2 = xf[..., :half], xf[..., half:]
    return jnp.concatenate([x1 * cos - x2 * sin, x1 * sin + x2 * cos], -1).astype(x.dtype)

def wkv_scan(S0, r, w, k, v, kk, a):
    def step(S, inp):
        r_t, w_t, k_t, v_t, kk_t, a_t = inp
        sa = jnp.einsum('bhvk,bhk->bhv', S, -kk_t)
        S = (S * w_t[:, :, None, :] + sa[..., None] * (kk_t * a_t)[:, :, None, :]
             + v_t[..., None] * k_t[:, :, None, :])
        return S, jnp.einsum('bhvk,bhk->bhv', S, r_t)
    xs = tuple(jnp.moveaxis(t, 1, 0) for t in (r, w, k, v, kk, a))
    S, ys = lax.scan(step, S0, xs)
    return S, jnp.moveaxis(ys, 0, 1)

def rwkv7_group(cols, shift0, wkv0, lw):
    B, T, _ = cols.shape
    f32 = lambda t: t.astype(jnp.float32)
    prev = jnp.concatenate([shift0[:, None].astype(cols.dtype), cols[:, :-1]], axis=1)
    mixed = f32(cols + (prev - cols) * lw['mu_shift'])
    r, k, v, xw, xa, xg = jnp.split(mixed, RW_SPLITS, axis=-1)
    log_w = -jnp.exp(-jax.nn.softplus(-(f32(lw['w0']) + jnp.tanh(xw) @ f32(lw['w2_decay']))) - 0.5)
    decay = jnp.exp(log_w)
    a = jax.nn.sigmoid(f32(lw['a0']) + xa @ f32(lw['a2']))
    g = jax.nn.sigmoid(xg) @ f32(lw['g2'])
    kk = k * f32(lw['k_k'])
    k = k * (1.0 + (a - 1.0) * f32(lw['k_a']))
    hs = lambda t: t.reshape(B, T, RW_HEADS, RW_DH)
    r, k, v, kk, a, decay = (hs(t) for t in (r, k, v, kk, a, decay))
    kk = kk / jnp.maximum(jnp.sqrt(jnp.sum(kk * kk, -1, keepdims=True)), 1e-12)
    S, y = wkv_scan(f32(wkv0), r, decay, k, v, kk, a)
    mu = y.mean(-1, keepdims=True)
    var = jnp.mean(jnp.square(y - mu), -1, keepdims=True)
    yn = ((y - mu) * lax.rsqrt(var + LNX_EPS) * f32(lw['lnx_w']).reshape(RW_HEADS, RW_DH)
          + f32(lw['lnx_b']).reshape(RW_HEADS, RW_DH))
    bonus = jnp.sum(r * k * f32(lw['r_k']), -1, keepdims=True) * v
    out = (yn + bonus).reshape(B, T, RW_W) * g
    return out.astype(cols.dtype), S

def diff_combine(q, k, v, mask, lam):
    s = jnp.einsum('bqhcd,bkhcd->bchqk', q, k).astype(jnp.float32) * (DF_DK ** -0.5)
    s = jnp.where(mask, s, -jnp.inf)
    p = jax.nn.softmax(s, axis=-1)
    att = p[:, 0] - lam.astype(jnp.float32) * p[:, 1]
    return jnp.einsum('bhqk,bkhd->bqhd', att.astype(v.dtype), v)

def diff_attn_prompt(q, k, v, lam):
    B, T, H = q.shape[:3]
    Tp = -(-T // Q_BLOCK) * Q_BLOCK
    pw = Tp - T
    qp = jnp.pad(q, ((0, 0), (0, pw), (0, 0), (0, 0), (0, 0)))
    kp = jnp.pad(k, ((0, 0), (0, pw), (0, 0), (0, 0), (0, 0)))
    vp = jnp.pad(v, ((0, 0), (0, pw), (0, 0), (0, 0)))
    nb = Tp // Q_BLOCK
    qb = jnp.moveaxis(qp.reshape(B, nb, Q_BLOCK, H, 2, DF_DK), 1, 0)
    kpos = jnp.arange(Tp)

    def block(args):
        qblk, start = args
        qpos = start + jnp.arange(Q_BLOCK)
        return diff_combine(qblk, kp, vp, kpos[None, :] <= qpos[:, None], lam)

    out = lax.map(block, (qb, jnp.arange(nb) * Q_BLOCK))
    return jnp.moveaxis(out, 0, 1).reshape(B, Tp, H, DF_DV)[:, :T]

def diff_attn_sample(q, k, v, lam, cache_k, cache_v, page_table):
    B, T = q.shape[:2]
    k_past = cache_k[page_table]
    k_past = k_past.reshape((B, -1) + k_past.shape[3:])
    v_past = cache_v[page_table].reshape(B, -1, DF_HEADS, DF_DV)
    past = k_past.shape[1]
    keys = jnp.concatenate([k_past.astype(k.dtype), k], axis=1)
    vals = jnp.concatenate([v_past.astype(v.dtype), v], axis=1)
    kpos = jnp.arange(past + T)
    qpos = past + jnp.arange(T)
    return diff_combine(q, keys, vals, kpos[None, :] <= qpos[:, None], lam)

def peer(x, wq, subkeys, U, V):
    n = x.shape[0]
    blk = min(PEER_BLOCK, n)
    n_pad = -(-n // blk) * blk
    xb = jnp.pad(x, ((0, n_pad - n), (0, 0))).reshape(n_pad // blk, blk, D_MODEL)

    def block(xt):
        q = (xt @ wq).reshape(blk, PK_HEADS, 2, PK_DQ // 2)
        s = jnp.einsum('thcd,hckd->thck', q, subkeys).astype(jnp.float32)
        s1, i1 = lax.top_k(s[:, :, 0], PK_TOPK)
        s2, i2 = lax.top_k(s[:, :, 1], PK_TOPK)
        cand_s = (s1[..., :, None] + s2[..., None, :]).reshape(blk, PK_HEADS, PK_TOPK * PK_TOPK)
        cand_i = (i1[..., :, None] * N_KEYS + i2[..., None, :]).reshape(blk, PK_HEADS, PK_TOPK * PK_TOPK)
        top_s, sel = lax.top_k(cand_s, PK_TOPK)
        idx = jnp.take_along_axis(cand_i, sel, axis=-1)
        gate = jax.nn.softmax(top_s, axis=-1)
        act = jax.nn.gelu(jnp.einsum('thed,td->the', U[idx], xt).astype(jnp.float32), approximate=False)
        return jnp.einsum('the,thed->td', (gate * act).astype(V.dtype), V[idx])

    return lax.map(block, xb).reshape(n_pad, D_MODEL)[:n]

def trunk_layer(x, pos, wkv0, shift0, attend, lw, lam_init):
    B, T, _ = x.shape
    cols = x @ lw['w_in']
    rw_cols, df_cols = cols[..., :RW_COLS], cols[..., RW_COLS:]
    rw_out, S = rwkv7_group(rw_cols, shift0, wkv0, lw)
    q = rope(df_cols[..., :DF_W].reshape(B, T, DF_HEADS, 2, DF_DK), pos)
    k = rope(df_cols[..., DF_W:2 * DF_W].reshape(B, T, DF_HEADS, 2, DF_DK), pos)
    v = df_cols[..., 2 * DF_W:].reshape(B, T, DF_HEADS, DF_DV)
    f32 = lambda t: t.astype(jnp.float32)
    lam = (jnp.exp(jnp.sum(f32(lw['lam_q1']) * f32(lw['lam_k1'])))
           - jnp.exp(jnp.sum(f32(lw['lam_q2']) * f32(lw['lam_k2']))) + lam_init)
    o = f32(attend(q, k, v, lam))
    o = o * lax.rsqrt(jnp.mean(o * o, -1, keepdims=True) + SUBLN_EPS)
    o = o * f32(lw['subln_w']).reshape(DF_HEADS, DF_DV) * (1.0 - lam_init)
    mix = jnp.concatenate([rw_out, o.reshape(B, T, DF_W).astype(x.dtype)], -1) @ lw['w_out']
    x = layer_norm(DEEP_ALPHA * x + mix, lw['ln1_w'], lw['ln1_b'])
    ch = peer(x.reshape(B * T, D_MODEL), lw['pk_wq'], lw['pk_subkeys'], lw['peer_u'], lw['peer_v'])
    x = layer_norm(DEEP_ALPHA * x + ch.reshape(B, T, D_MODEL), lw['ln2_w'], lw['ln2_b'])
    return x, k, v, S, rw_cols[:, -1]

def setup_inputs(seed: int = 0) -> dict:
    key = jax.random.key(seed)
    ks = iter(jax.random.split(key, 40))
    nrm = lambda shape, s=1.0: s * jax.random.normal(next(ks), shape, jnp.float32)
    uni = lambda shape, lo, hi: jax.random.uniform(next(ks), shape, jnp.float32, lo, hi)
    n_pages = PAST_LEN // PAGE_SIZE
    n_used = DEC_BATCH * n_pages
    n_pool = n_used + max(1, n_used // 4)
    L = DEPTH
    x_prompt = nrm((BATCH, SEQ, D_MODEL))
    x_sample = nrm((DEC_BATCH, DEC_SEQ, D_MODEL))
    cache_k = nrm((L, n_pool, PAGE_SIZE, DF_HEADS, 2, DF_DK))
    cache_v = nrm((L, n_pool, PAGE_SIZE, DF_HEADS, DF_DV))
    page_table = jax.random.permutation(next(ks), n_pool)[:n_used].reshape(DEC_BATCH, n_pages).astype(jnp.int32)
    state_wkv = nrm((L, DEC_BATCH, RW_HEADS, RW_DH, RW_DH), 0.3)
    state_shift = nrm((L, DEC_BATCH, RW_COLS))
    return {
        'x_prompt': x_prompt,
        'x_sample': x_sample,
        'cache_k': cache_k,
        'cache_v': cache_v,
        'page_table': page_table,
        'state_wkv': state_wkv,
        'state_shift': state_shift,
        'meta_tokens': nrm((N_META, D_MODEL)),
        'w_in': nrm((L, D_MODEL, IN_COLS), D_MODEL ** -0.5),
        'mu_shift': uni((L, RW_COLS), 0.0, 1.0),
        'w0': uni((L, RW_W), -2.0, 1.0),
        'w2_decay': nrm((L, DECAY_LORA, RW_W), 0.1),
        'a0': nrm((L, RW_W), 0.1),
        'a2': nrm((L, AAA_LORA, RW_W), 0.5 * AAA_LORA ** -0.5),
        'g2': nrm((L, GATE_LORA, RW_W), GATE_LORA ** -0.5),
        'k_k': 0.85 + nrm((L, RW_W), 0.05),
        'k_a': 1.0 + nrm((L, RW_W), 0.05),
        'r_k': nrm((L, RW_HEADS, RW_DH), 0.1),
        'lnx_w': 1.0 + nrm((L, RW_W), 0.05),
        'lnx_b': nrm((L, RW_W), 0.01),
        'lam_q1': nrm((L, DF_DK), 0.1),
        'lam_k1': nrm((L, DF_DK), 0.1),
        'lam_q2': nrm((L, DF_DK), 0.1),
        'lam_k2': nrm((L, DF_DK), 0.1),
        'subln_w': 1.0 + nrm((L, DF_W), 0.05),
        'w_out': nrm((L, MIX_W, D_MODEL), DEEP_BETA * MIX_W ** -0.5),
        'ln1_w': 1.0 + nrm((L, D_MODEL), 0.05),
        'ln1_b': nrm((L, D_MODEL), 0.01),
        'pk_wq': nrm((L, D_MODEL, PK_HEADS * PK_DQ), D_MODEL ** -0.5),
        'pk_subkeys': nrm((L, PK_HEADS, 2, N_KEYS, PK_DQ // 2), (PK_DQ // 2) ** -0.5),
        'peer_u': nrm((L, N_EXPERTS, D_MODEL), D_MODEL ** -0.5),
        'peer_v': nrm((L, N_EXPERTS, D_MODEL), DEEP_BETA),
        'ln2_w': 1.0 + nrm((L, D_MODEL), 0.05),
        'ln2_b': nrm((L, D_MODEL), 0.01),
    }

def reference(x_prompt, x_sample, cache_k, cache_v, page_table, state_wkv, state_shift,
              meta_tokens, w_in, mu_shift, w0, w2_decay, a0, a2, g2, k_k, k_a, r_k, lnx_w, lnx_b,
              lam_q1, lam_k1, lam_q2, lam_k2, subln_w, w_out, ln1_w, ln1_b,
              pk_wq, pk_subkeys, peer_u, peer_v, ln2_w, ln2_b):
    B = x_prompt.shape[0]
    meta = jnp.broadcast_to(meta_tokens[None].astype(x_prompt.dtype), (B, N_META, D_MODEL))
    xp = jnp.concatenate([meta, x_prompt], axis=1)
    xs = x_sample
    pos_p = jnp.arange(xp.shape[1])
    past = page_table.shape[1] * cache_k.shape[2]
    pos_s = past + jnp.arange(xs.shape[1])
    wkv0_p = jnp.zeros((B, RW_HEADS, RW_DH, RW_DH), jnp.float32)
    shift0_p = jnp.zeros((B, RW_COLS), xp.dtype)
    kp_l, vp_l, sp_l, hp_l, ks_l, vs_l, ss_l, hs_l = [], [], [], [], [], [], [], []
    for l in range(DEPTH):
        lw = {
            'w_in': w_in[l], 'mu_shift': mu_shift[l], 'w0': w0[l], 'w2_decay': w2_decay[l],
            'a0': a0[l], 'a2': a2[l], 'g2': g2[l], 'k_k': k_k[l], 'k_a': k_a[l], 'r_k': r_k[l],
            'lnx_w': lnx_w[l], 'lnx_b': lnx_b[l], 'lam_q1': lam_q1[l], 'lam_k1': lam_k1[l],
            'lam_q2': lam_q2[l], 'lam_k2': lam_k2[l], 'subln_w': subln_w[l], 'w_out': w_out[l],
            'ln1_w': ln1_w[l], 'ln1_b': ln1_b[l], 'pk_wq': pk_wq[l], 'pk_subkeys': pk_subkeys[l],
            'peer_u': peer_u[l], 'peer_v': peer_v[l], 'ln2_w': ln2_w[l], 'ln2_b': ln2_b[l],
        }
        lam_init = 0.8 - 0.6 * math.exp(-0.3 * l)
        xp, kp, vp, sp, hp = trunk_layer(xp, pos_p, wkv0_p, shift0_p, diff_attn_prompt, lw, lam_init)
        sample_attend = functools.partial(diff_attn_sample, cache_k=cache_k[l], cache_v=cache_v[l],
                                          page_table=page_table)
        xs, ksn, vsn, ssn, hsn = trunk_layer(xs, pos_s, state_wkv[l], state_shift[l], sample_attend, lw, lam_init)
        kp_l.append(kp); vp_l.append(vp); sp_l.append(sp); hp_l.append(hp)
        ks_l.append(ksn); vs_l.append(vsn); ss_l.append(ssn); hs_l.append(hsn)
    y_prompt = xp[:, N_META:]
    y_sample = xs
    return (y_prompt, y_sample,
            jnp.stack(kp_l), jnp.stack(vp_l), jnp.stack(sp_l), jnp.stack(hp_l),
            jnp.stack(ks_l), jnp.stack(vs_l), jnp.stack(ss_l), jnp.stack(hs_l))


_drawn_inputs = setup_inputs


def setup_inputs(seed=0):
    import zlib

    import numpy as np

    out = dict(_drawn_inputs(seed))
    spreads = {}
    factors = {'k_k': 4.224, 'lnx_b': 3.136, 'lam_k2': 8.0, 'ln2_b': 5.682}
    for name, (base, spread) in spreads.items():
        noise = np.random.default_rng([zlib.crc32(name.encode()), seed]).standard_normal(out[name].shape)
        drawn = base * np.exp(spread * noise) if base else spread * noise
        out[name] = __import__('jax').numpy.asarray(drawn.astype(out[name].dtype))
    for name, factor in factors.items():
        out[name] = (out[name] * factor).astype(out[name].dtype)
    return out
```

```python
import math

import numpy as np
import concourse.bass as bass
from concourse import mybir
from concourse.alu_op_type import AluOpType as ALU
from contextlib import ExitStack

F32 = mybir.dt.float32
I32 = mybir.dt.int32
U32 = mybir.dt.uint32
ACT = mybir.ActivationFunctionType
AX = mybir.AxisListType

P = 128
D = 1024
KT = D // P
NMETA, SEQ, NB = 16, 512, 8
NT = SEQ // P
TP = NMETA + SEQ
TA = TP + NB
SM = NB + NMETA
RWW, RWC = 512, 1792
NCH = RWC // P
HP = 4
DH = 64
NH, DV = 4, 128
PAST, PAGE = 1024, 128
NPG = PAST // PAGE
PKH, NKEY, TOPK = 8, 128, 16
NEXP = NKEY * NKEY
SLOTS = PKH * TOPK
CH = 64
LAM_INIT = 0.8 - 0.6 * math.exp(-0.3 * 0)
ALPHA = 2.0 ** 0.25
BIG = 1.0e30


class Link:

    def __init__(self, eng, own):
        self.eng, self.own, self.n = eng, own, {}

    def __call__(self, ins, sem=None):
        s = sem if sem is not None else self.own
        k = s.name
        self.n[k] = self.n.get(k, 0) + 1
        ins.then_inc(s, 1)
        self.eng.wait_ge(s, self.n[k])


def constant_table():
    t, s = np.arange(P)[:, None], np.arange(P)[None, :]
    same = (t // CH) == (s // CH)
    parts = {}
    parts["ident"] = (t == s)
    strict_up = same & (t < s)
    incl_up = same & (t <= s)
    parts["mask4"] = np.concatenate([strict_up, incl_up, strict_up, incl_up], 1)

    def level(l):
        return (t // (2 * l) == s // (2 * l)) & ((t // l) % 2 == 1) & ((s // l) % 2 == 0)

    parts["first"] = level(1)
    parts["firstT"] = level(1).T
    for l in (2, 4, 8, 16, 32):
        parts[f"lev{l}"] = level(l)
    parts["heads"] = (t // DH == s // DH)
    parts["half"] = (t // DH == np.arange(2)[None, :])
    parts["diag64"] = (t % DH == np.arange(DH)[None, :])
    parts["causal"] = np.where(s > t, -BIG, 0.0)
    parts["one8"] = (t == np.arange(NB)[None, :])
    parts["spread"] = (t == s // TOPK)
    parts["gather"] = (t // TOPK == np.arange(NB)[None, :])
    parts["iota16"] = np.broadcast_to(np.arange(16)[None, :], (P, 16))
    parts["rowid"] = t
    parts["map"] = np.concatenate([t % 2 == 0, t % 2 == 1], 1)
    half = 32
    inv = (np.float32(10000.0) ** (-np.arange(half, dtype=np.float32) / np.float32(half))).astype(np.float32)
    pos = np.zeros((P, NT + 1), np.float32)
    for tt in range(NT):
        pos[:, tt] = NMETA + P * tt + np.arange(P)
    pos[:NB, NT] = PAST
    pos[NB:SM, NT] = np.arange(NMETA)
    ang = pos[:, :, None] * inv[None, None, :]
    c, sn = np.cos(ang), np.sin(ang)
    parts["cos"] = np.concatenate([c, c], 2).reshape(P, -1)
    parts["sin"] = np.concatenate([-sn, sn], 2).reshape(P, -1)
    start = np.ones((P, TA))
    start[:, 0] = 0
    start[:, NMETA:TP:CH] = 0
    start[:, TP:] = 0
    parts["start"] = start
    keep = ("ident", "spread", "gather", "iota16")
    where, tables = {}, []
    for which in (True, False):
        at, here = 0, []
        for n, a in parts.items():
            if (n in keep) == which:
                where[n] = (len(tables), at, a.shape[1])
                at += a.shape[1]
                here.append(np.asarray(a, np.float32))
        tables.append(np.concatenate(here, 1))
    return where, tables


WHERE, TABLES = constant_table()
PAR = {}
_at = 0
for _n, _c in (("mu", NCH), ("w0", HP), ("a0", HP), ("k_k", HP), ("k_a", HP), ("r_k", HP)):
    PAR[_n] = _at
    _at += _c
NPAR = _at


def phase_project(nc, io, m):
    ctx = ExitStack()
    with ctx:
        sb = lambda n, s, dt=F32: ctx.enter_context(nc.sbuf_tensor(n, s, dt))
        sem = lambda n: ctx.enter_context(nc.semaphore(n))
        ps = m.ps
        xT = sb("xT", [P, KT, TA])
        wr = sb("w_ring", [P, 2, KT, 512])
        cols = sb("cols", [P, 2, TA + 1])
        diff = sb("diff", [P, 2, TA])
        rraw = m.ar[:, :, 1, :]
        kraw = m.kt
        xwa = sb("xwa", [P, TA])
        xg = sb("xg", [P, TA])
        kk = sb("kk", [P, TA])
        kk2 = sb("kk2", [P, TA])
        sgm = sb("sgm", [P, TA])
        am = sb("am", [P, TA])
        L = sb("L", [P, TA])
        E = sb("E", [P, TA])
        Ei = sb("Ei", [P, TA])
        Lp = sb("Lp", [P, TA])
        rot = sb("rot", [P, 3, 512])
        rtmp = sb("rtmp", [P, 512])
        rtmp2 = sb("rtmp2", [P, 512])
        c = m.c
        par = m.par

        s_const = sem("s_const")
        s_x = sem("s_x")
        s_w = [sem(f"s_w{i}") for i in range(2)]
        s_item = sem("s_item")
        s_cols = sem("s_cols")
        s_mixed = sem("s_mixed")
        s_rope = sem("s_rope")
        s_val = sem("s_val")
        s_tr = sem("s_tr")
        s_trc = sem("s_trc")
        s_rot_out = [sem(f"s_rot_out{i}") for i in range(3)]
        s_tanh = sem("s_tanh")
        s_sq = sem("s_sq")
        s_lora = sem("s_lora")
        s_sig = sem("s_sig")
        s_ss = sem("s_ss")
        s_rn = sem("s_rn")
        s_L = sem("s_L")
        s_E = sem("s_E")
        s_Eu = sem("s_Eu")
        s_v = sem("s_v")
        s_a = sem("s_a")
        s_out = sem("s_out")

        NG = 7
        GW = [4, 4, 4, 2, 4, 4, 4]
        chan = list(range(NCH))
        done_group = [4, 8, 12, 14, 19, 24, 29]

        block = ctx.enter_context(nc.Block())

        @block.sync
        def _(sp):
            for n in m.consts:
                sp.dma_start(n[0], n[1]).then_inc(s_const, 16)
            sp.dma_start(xT[:, :, :], io["xT"].rearrange("(k p) n -> p k n", p=P)).then_inc(s_x, 16)
            for g in range(NG):
                if g >= 2:
                    sp.wait_ge(s_item, done_group[g - 2])
                w = GW[g] * P
                sp.dma_start(wr[:, g % 2, :, 0:w],
                             io["w_in"][:, g * 512 - (256 if g > 3 else 0):][:, 0:w].rearrange("(k p) n -> p k n", p=P)
                             ).then_inc(s_w[g % 2], 16)
            n_out = 0
            for n in range(10):
                tt = n % 5
                if n >= 5:
                    sp.wait_ge(s_rope, n + 1)
                    if tt < NT:
                        sp.dma_start(io["k_out"][tt * P:(tt + 1) * P, :], rot[:, n % 3, :]).then_inc(s_rot_out[n % 3], 16)
                    else:
                        sp.dma_start(io["k_out"][SEQ:, :], m.qks[0:SM, 1, :]).then_inc(s_out, 16)
                        n_out += 1
            sp.wait_ge(s_val, 4)
            sp.dma_start(io["v_out"][0:SEQ, :].rearrange("(t p) n -> p t n", p=P), m.vtok[:, 0:NT, :]).then_inc(s_out, 16)
            sp.wait_ge(s_val, 5)
            sp.dma_start(io["v_out"][SEQ:, :], m.vtok[0:SM, NT, :]).then_inc(s_out, 16)
            sp.dma_start(m.vmeta[:, :], m.vtok[NB:SM, NT, :]).then_inc(s_out, 16)
            sp.wait_ge(s_mixed, NCH)
            sp.dma_start(io["shift_out"], m.shout[:, :, :]).then_inc(s_out, 16)
            n_out += 4
            sp.wait_ge(s_out, 16 * n_out)
            for i, k in ((0, 1), (1, 1), (2, 2)):
                sp.wait_ge(s_rot_out[i], 16 * sum(1 for n in range(5, 9) if n % 3 == i))

        @block.tensor
        def _(pe):
            pe.wait_ge(s_const, 16 * len(m.consts))
            pe.wait_ge(s_x, 16)

            def arrived(g):
                pe.wait_ge(s_w[g % 2], 16 * (g // 2 + 1))

            def channel_tiles(g):
                arrived(g)
                for mt in range(GW[g]):
                    ct = 4 * g + mt
                    if ct >= 2:
                        pe.wait_ge(s_cols, ct - 1)
                    for k in range(KT):
                        w = wr[:, g % 2, k, mt * P:(mt + 1) * P]
                        pe.matmul(ps[:, ct % 2, :], w, xT[:, k, 0:SEQ], start=(k == 0), stop=(k == KT - 1))
                        mm = pe.matmul(ps[:, 2 + ct % 2, 0:SM], w, xT[:, k, SEQ:TA], start=(k == 0), stop=(k == KT - 1))
                    mm.then_inc(s_item, 1)

            def token_tiles(g):
                arrived(g)
                for tt in range(NT + 1):
                    n = 5 * (g - 4) + tt
                    rows = P if tt < NT else SM
                    if n >= 2:
                        pe.wait_ge(s_rope, min(n - 1, 10))
                        if n - 1 > 10:
                            pe.wait_ge(s_val, n - 11)
                    for k in range(KT):
                        mm = pe.matmul(ps[0:rows, 4 + n % 2, :], xT[:, k, tt * P:tt * P + rows], wr[:, g % 2, k, :],
                                       start=(k == 0), stop=(k == KT - 1))
                    mm.then_inc(s_item, 1)
                    if 1 <= n <= 10:
                        transposes(n - 1)

            def transposes(n):
                rows = P if n % 5 < NT else SM
                src = rot[:, n % 3, :] if n % 5 < NT else m.qks[0:SM, n // 5, :]
                pe.wait_ge(s_rope, n + 1)
                if n >= 2:
                    pe.wait_ge(s_trc, n - 1)
                for h in range(NH):
                    mm = pe.transpose(ps[:, 6 + n % 2, h * P:h * P + rows], src[:, h * P:(h + 1) * P], c("ident")[0:rows, 0:rows])
                mm.then_inc(s_tr, 1)

            def lora(i):
                pe.wait_ge(s_tanh, 1)
                if i >= 1:
                    pe.wait_ge(s_rn, i)
                    pe.wait_ge(s_sig, 2 * i)
                else:
                    pe.wait_ge(s_cols, NCH)
                for a, b in ((0, 512), (512, TA)):
                    pe.matmul(ps[:, a // 512, 0:b - a], m.w2a2[0:DH, i * P:(i + 1) * P], xwa[0:DH, a:b], start=True, stop=True)
                for a, b in ((0, 512), (512, TA)):
                    mm = pe.matmul(ps[:, 2 + a // 512, 0:b - a], m.w2a2[DH:P, i * P:(i + 1) * P], xwa[DH:P, a:b], start=True, stop=True)
                mm.then_inc(s_lora, 1)
                pe.wait_ge(s_sq, i + 1)
                pe.wait_ge(s_sig, 2 * i + 1)
                for a, b in ((0, 512), (512, TA)):
                    mm = pe.matmul(ps[:, a // 512, 0:b - a], c("heads"), kk2[:, a:b], start=True, stop=True)
                mm.then_inc(s_ss, 1)

            for g in range(4):
                channel_tiles(g)
            token_tiles(4)
            lora(0)
            token_tiles(5)
            lora(1)
            token_tiles(6)
            lora(2)
            lora(3)

        @block.scalar
        def _(act):
            link = Link(act, s_a)
            act.wait_ge(s_const, 16 * len(m.consts))
            for ct in range(NCH):
                act.wait_ge(s_item, ct + 1)
                if ct == 0:
                    act.wait_ge(s_v, 1)
                if ct >= 2:
                    act.wait_ge(s_mixed, ct - 1)
                buf = cols[:, ct % 2, :]
                act.activation(buf[:, 1 + NMETA:1 + TP], ps[:, ct % 2, :], ACT.Copy)
                act.activation(buf[:, 1:1 + NMETA], ps[:, 2 + ct % 2, NB:SM], ACT.Copy)
                act.activation(buf[:, 1 + TP:1 + TA], ps[:, 2 + ct % 2, 0:NB], ACT.Copy).then_inc(s_cols, 1)
            act.wait_ge(s_mixed, NCH)
            act.activation(xwa[0:DH, :], xwa[0:DH, :], ACT.Tanh).then_inc(s_tanh, 1)
            act.activation(m.sg[:, :], xg[:, :], ACT.Sigmoid).then_inc(s_tanh, 1)

            def evac_transposes(n):
                act.wait_ge(s_tr, n + 1)
                tt = n % 5
                src = ps[:, 6 + n % 2, :].rearrange("p (h t) -> p h t", h=NH)
                if n < 4:
                    ins = act.activation(m.qT[:, :, tt * P:(tt + 1) * P], src, ACT.Copy)
                elif n == 4:
                    ins = act.activation(m.qTs[:, :, :], src[:, :, 0:NB], ACT.Copy)
                elif tt < NT:
                    ins = act.activation(m.kT[:, :, NMETA + tt * P:NMETA + (tt + 1) * P], src, ACT.Copy)
                else:
                    ins = act.activation(m.kT[:, :, 0:NMETA], src[:, :, NB:SM], ACT.Copy)
                ins.then_inc(s_trc, 1)

            def factors(i):
                act.wait_ge(s_lora, i + 1)
                if i >= 1:
                    act.wait_ge(s_Eu, 2 * i)
                z = ps[:, 0:2, :].rearrange("p a b -> p (a b)")[:, 0:TA]
                za = ps[:, 2:4, :].rearrange("p a b -> p (a b)")[:, 0:TA]
                act.activation(sgm[:, :], z, ACT.Sigmoid, bias=par("w0", i)).then_inc(s_sig, 1)
                act.activation(am[:, :], za, ACT.Sigmoid, bias=par("a0", i)).then_inc(s_sig, 1)
                act.wait_ge(s_ss, i + 1)
                act.activation(kk2[:, :], z, ACT.Sqrt).then_inc(s_rn, 1)
                act.wait_ge(s_L, i + 1)
                act.activation(E[:, :], L[:, :], ACT.Exp)
                act.activation(Ei[:, :], L[:, :], ACT.Exp, scale=-1.0)
                act.activation(Lp[:, :], Lp[:, :], ACT.Exp).then_inc(s_E, 1)

            for n in range(4):
                evac_transposes(n)
            factors(0)
            for n in range(4, 9):
                evac_transposes(n)
            factors(1)
            for tt in range(NT + 1):
                rows = P if tt < NT else SM
                act.wait_ge(s_item, 24 + tt + 1)
                act.activation(m.vtok[0:rows, tt, :], ps[0:rows, 4 + tt % 2, :], ACT.Copy).then_inc(s_val, 1)
                if tt == 0:
                    evac_transposes(9)
            factors(2)
            factors(3)

        @block.vector
        def _(dve):
            link = Link(dve, s_v)
            link(dve.memset(cols[:, :, 0:1], 0.0))
            link(dve.memset(m.zero[:, :], 0.0))
            dve.wait_ge(s_const, 16 * len(m.consts))
            link(dve.tensor_scalar(m.omka[:, :], m.params[:, PAR["k_a"]:PAR["k_a"] + HP], -1.0, 1.0, ALU.mult, ALU.add))
            dests = [rraw[:, i, :] for i in range(HP)] + [kraw[:, i, :] for i in range(HP)] + \
                    [m.vT[:, i, :] for i in range(HP)] + [xwa[:, :], xg[:, :]]
            for ct in range(NCH):
                dve.wait_ge(s_cols, ct + 1)
                buf, d = cols[:, ct % 2, :], diff[:, ct % 2, :]
                dve.tensor_tensor(d[:, 0:TP], buf[:, 0:TP], buf[:, 1:1 + TP], ALU.subtract)
                dve.tensor_copy(m.shout[:, ct, :], buf[:, TP:1 + TA])
                link(dve.tensor_tensor(d[:, TP:TA], m.shift0[:, ct, :], buf[:, 1 + TP:1 + TA], ALU.subtract))
                link(dve.scalar_tensor_tensor(dests[ct], d, par("mu", ct), buf[:, 1:1 + TA], ALU.mult, ALU.add), s_mixed)

            def rope(n):
                tt = n % 5
                rows = P if tt < NT else SM
                dve.wait_ge(s_item, 14 + n + 1)
                if n >= 3:
                    dve.wait_ge(s_tr, n - 2)
                    if n - 3 >= 5 and (n - 3) % 5 < NT:
                        dve.wait_ge(s_rot_out[n % 3], 16 * sum(1 for q in range(5, n - 2) if q % 3 == n % 3 and q % 5 < NT))
                x = ps[0:rows, 4 + n % 2, :].rearrange("p (g f) -> p g f", f=DH)
                out = rot[:, n % 3, :] if tt < NT else m.qks[0:SM, n // 5, :]
                cs = c("cos")[0:rows, tt * DH:(tt + 1) * DH].unsqueeze(1).broadcast_to([rows, 8, DH])
                sn = c("sin")[0:rows, tt * DH:(tt + 1) * DH].unsqueeze(1).broadcast_to([rows, 8, DH])
                t = rtmp[0:rows, :].rearrange("p (g f) -> p g f", f=DH)
                u = rtmp2[0:rows, :].rearrange("p (g f) -> p g f", f=DH)
                dve.tensor_tensor(t, x, cs, ALU.mult)
                dve.tensor_tensor(u[:, :, 0:32], x[:, :, 32:64], sn[:, :, 0:32], ALU.mult)
                link(dve.tensor_tensor(u[:, :, 32:64], x[:, :, 0:32], sn[:, :, 32:64], ALU.mult))
                link(dve.tensor_tensor(out, rtmp[0:rows, :], rtmp2[0:rows, :], ALU.add), s_rope)

            def squares(i):
                if i >= 1:
                    dve.wait_ge(s_ss, i)
                link(dve.tensor_scalar(kk[:, :], kraw[:, i, :], par("k_k", i), None, ALU.mult))
                link(dve.tensor_tensor(kk2[:, :], kk[:, :], kk[:, :], ALU.mult), s_sq)

            def factors(i):
                dve.wait_ge(s_sig, 2 * i + 2)
                link(dve.tensor_scalar(sgm[:, :], sgm[:, :], -math.exp(-0.5), None, ALU.mult))
                link(dve.tensor_tensor_scan(L[:, :], c("start"), sgm[:, :], 0.0, ALU.mult, ALU.add))
                link(dve.tensor_tensor(Lp[:, :], L[:, :], sgm[:, :], ALU.subtract), s_L)
                link(dve.tensor_scalar(sgm[:, :], am[:, :], par("k_a", i), m.omka[:, i:i + 1], ALU.mult, ALU.add))
                link(dve.tensor_tensor(kraw[:, i, :], kraw[:, i, :], sgm[:, :], ALU.mult), s_Eu)
                dve.wait_ge(s_rn, i + 1)
                link(dve.tensor_scalar(kk2[:, :], kk2[:, :], 1e-12, None, ALU.max))
                link(dve.reciprocal(kk2[:, :], kk2[:, :]))
                link(dve.tensor_tensor(kk[:, :], kk[:, :], kk2[:, :], ALU.mult))
                dve.wait_ge(s_E, i + 1)
                link(dve.scalar_tensor_tensor(m.rk[:, i, :], rraw[:, i, :], par("r_k", i), kraw[:, i, :], ALU.mult, ALU.mult))
                dve.tensor_tensor(m.ar[:, i, 1, :], rraw[:, i, :], E[:, :], ALU.mult)
                dve.scalar_tensor_tensor(m.ar[:, i, 0, :], kk[:, :], -1.0, Lp[:, :], ALU.mult, ALU.mult)
                dve.tensor_tensor(m.kt[:, i, :], kraw[:, i, :], Ei[:, :], ALU.mult)
                dve.tensor_copy(m.eend[:, i, 0:9], E[:, NMETA - 1:TP:CH])
                dve.tensor_copy(m.eend[:, i, 9:17], E[:, TP:TA])
                link(dve.tensor_tensor(am[:, :], kk[:, :], am[:, :], ALU.mult))
                link(dve.tensor_tensor(m.bt[:, i, :], am[:, :], Ei[:, :], ALU.mult), s_Eu)

            for n in range(5):
                rope(n)
            squares(0)
            factors(0)
            for n in range(5, 10):
                rope(n)
            squares(1)
            factors(1)
            for i in (2, 3):
                squares(i)
                factors(i)


def phase_rwkv(nc, io, m):
    ctx = ExitStack()
    with ctx:
        sb = lambda n, s, dt=F32: ctx.enter_context(nc.sbuf_tensor(n, s, dt))
        sem = lambda n: ctx.enter_context(nc.semaphore("r_" + n))
        ps, c = m.ps, m.c
        tok = sb("tok", [P, 2, 4, RWW])
        msk = sb("msk", [P, 8, 4, P])
        X = sb("X", [P, 2, HP, P])
        XT = sb("XT", [P, 2, HP, P])
        T1 = sb("T1", [P, 2, HP, P])
        AV = sb("AV", [P, RWW])
        U0 = sb("U0", [P, RWW])
        U = sb("U", [P, RWW])
        WT = sb("WT", [P, HP, P])
        St = sb("St", [P, 10, HP, DH])
        stmp = sb("stmp", [P, HP, DH])
        y = sb("y", [P, RWW])
        sq = sb("sq", [P, RWW])
        stat = sb("stat", [P, 4, 8])
        S0 = sb("S0", [P, NB, HP, DH])
        y2 = msk[0:2, 0:4].rearrange("p a x t -> p (a x t)")
        w1 = msk[:, 4:8].rearrange("p a x t -> p (a x t)").rearrange("p (b i v) -> p b i v", b=NB, i=HP)
        lnw = sb("lnxw", [P, RWW])
        lnb = sb("lnxb", [P, RWW])

        s_ld, s_st = sem("ld"), sem("st")
        s_tr, s_trc = sem("tr"), sem("trc")
        s_A, s_Am = sem("A"), sem("Am")
        s_A0, s_X = sem("A0"), sem("X")
        s_XT0 = sem("XT0")
        s_T, s_Tc, s_XX = sem("T"), sem("Tc"), sem("XX")
        s_AV, s_AVc, s_UW, s_UWc = sem("AV"), sem("AVc"), sem("UW"), sem("UWc")
        s_U, s_Uc, s_N, s_S = sem("U"), sem("Uc"), sem("N"), sem("S")
        s_Y, s_yc, s_var, s_rs = sem("Y"), sem("yc"), sem("var"), sem("rs")
        s_mix, s_mt, s_mtc = sem("mix"), sem("mt"), sem("mtc")
        s_sp, s_sc = sem("sp"), sem("sc")
        s_sr = sem("sr")
        s_y2, s_y2d = sem("y2"), sem("y2d")
        s_v, s_a, s_g = sem("v"), sem("a"), sem("g")

        tiles = [(0, NMETA, (2, 4, 8))] + [(NMETA + P * t, P, (2, 4, 8, 16, 32)) for t in range(NT)]
        NTL = len(tiles)
        levels_before = [sum(len(t[2]) for t in tiles[:i]) for i in range(NTL)]

        block = ctx.enter_context(nc.Block())

        @block.sync
        def _(sp):
            sp.dma_start(lnw[:, :], io["lnx_w"].partition_broadcast(P)).then_inc(s_ld, 16)
            sp.dma_start(lnb[:, :], io["lnx_b"].partition_broadcast(P)).then_inc(s_ld, 16)
            sp.dma_start(S0[:, :, :, :], io["state"]).then_inc(s_ld, 16)
            sp.wait_ge(s_y2, 1)
            for h2 in range(2):
                for b in range(NB):
                    sp.dma_start(y[b:b + 1, :].rearrange("b (i h v) -> b i h v", h=2, v=DH)[:, :, h2, :],
                                 y2[h2:h2 + 1, :].rearrange("o (b i v) -> o b i v", b=NB, v=DH)[:, b]).then_inc(s_y2d, 16)
            sp.wait_ge(s_sc, 3)
            sp.dma_start(io["wkv_s_out"], S0[:, :, :, :]).then_inc(s_st, 16)
            sp.wait_ge(s_S, 9)
            sp.dma_start(io["wkv_p_out"], St[:, 9, :, :]).then_inc(s_st, 16)
            sp.wait_ge(s_st, 32)

        @block.tensor
        def _(pe):
            def prepare(ti):
                p0, n, levels = tiles[ti]
                span = slice(p0, p0 + n)
                for q, src in enumerate((m.ar[:, :, 0], m.bt, m.kt, m.vT)):
                    if 4 * ti + q >= 2:
                        pe.wait_ge(s_trc, 4 * ti + q - 1)
                    if ti >= 1:
                        pe.wait_ge(s_UWc, 2 * ti)
                    for i in range(HP):
                        mm = pe.transpose(ps[0:n, q % 2, i * P:(i + 1) * P], src[:, i, span], c("ident"))
                    mm.then_inc(s_tr, 1)
                pe.wait_ge(s_trc, 4 * ti + 4)
                for hd in range(8):
                    q, i = hd // 4, hd % 4
                    rows = slice(q * DH, (q + 1) * DH)
                    j = 8 * ti + hd
                    if hd >= 2:
                        pe.wait_ge(s_Am, j - 1)
                    for w, src in enumerate((m.bt, m.kt)):
                        mm = pe.matmul(ps[0:n, hd % 2, w * 2 * n:(w + 1) * 2 * n].rearrange("s (x t) -> s x t", x=2),
                                       src[rows, i, span], m.ar[rows, i, :, span], start=True, stop=True)
                    mm.then_inc(s_A, 1)
                for q in range(2):
                    rows = slice(q * DH, (q + 1) * DH)
                    if ti >= 1:
                        pe.wait_ge(s_yc, ti)
                    for i in range(HP):
                        mm = pe.matmul(ps[0:n, 4 + q, i * n:(i + 1) * n], m.ar[rows, i, 0, span], m.bt[rows, i, span],
                                       start=True, stop=True)
                    mm.then_inc(s_A0, 1)
                for l in range(len(levels)):
                    at = 2 * (levels_before[ti] + l)
                    for q in range(2):
                        pe.wait_ge(s_X, at + q + 1 + 2 * ti)
                        if l == 0:
                            pe.wait_ge(s_XT0, 2 * ti + q + 1)
                            pe.wait_ge(s_Am, 8 * ti + 8)
                        for i in range(HP):
                            mm = pe.matmul(ps[0:n, 2 + q, i * n:(i + 1) * n], msk[0:n, 4 * q + i, 0, 0:n], X[0:n, q, i, 0:n],
                                           start=True, stop=True)
                        mm.then_inc(s_T, 1)
                    for q in range(2):
                        pe.wait_ge(s_Tc, at + q + 1)
                        for i in range(HP):
                            if l < len(levels) - 1:
                                pe.matmul(ps[0:n, 4 + q, i * n:(i + 1) * n], XT[0:n, q, i, 0:n], T1[0:n, q, i, 0:n],
                                          start=True, stop=True)
                            mm = pe.matmul(ps[0:n, 6 + q, i * n:(i + 1) * n], T1[0:n, q, i, 0:n], XT[0:n, q, i, 0:n],
                                           start=True, stop=True)
                        mm.then_inc(s_XX, 1)
                for hd in range(8):
                    h = 2 * (hd % 4) + hd // 4
                    mm = pe.matmul(ps[0:n, 0, h * DH:(h + 1) * DH], msk[0:n, hd, 2, 0:n], tok[0:n, ti % 2, 3, h * DH:(h + 1) * DH],
                                   start=True, stop=True)
                mm.then_inc(s_AV, 1)
                pe.wait_ge(s_X, 2 * (levels_before[ti] + len(levels)) + 2 * ti + 2)
                pe.wait_ge(s_AVc, ti + 1)
                for hd in range(8):
                    q, i = hd // 4, hd % 4
                    h = 2 * i + q
                    mm = pe.matmul(ps[0:n, 1, h * DH:(h + 1) * DH], XT[0:n, q, i, 0:n], AV[0:n, h * DH:(h + 1) * DH],
                                   start=True, stop=True)
                    if ti > 0:
                        mm = pe.matmul(ps[q * DH:(q + 1) * DH, 2, i * P:(i + 1) * P], tok[0:n, ti % 2, 0, h * DH:(h + 1) * DH],
                                       XT[0:n, q, i, 0:n], start=True, stop=True)
                mm.then_inc(s_UW, 1)

            def chain(ti):
                pe.wait_ge(s_UWc, 2 * ti + 2)
                for ch in range(2 if ti else 1):
                    n = CH if ti else NMETA
                    k = 2 * ti - 1 + ch if ti else 0
                    r = slice(ch * CH, ch * CH + n)
                    if ti:
                        pe.wait_ge(s_S, k)
                        for hd in range(8):
                            q, i = hd // 4, hd % 4
                            rows = slice(q * DH, (q + 1) * DH)
                            mm = pe.matmul(ps[r, 2 + q, i * DH:(i + 1) * DH], WT[rows, i, r], St[rows, k, i, :],
                                           start=True, stop=True)
                        mm.then_inc(s_U, 1)
                        pe.wait_ge(s_Uc, k)
                    u = U if ti else U0
                    for hd in range(8):
                        q, i = hd // 4, hd % 4
                        h = 2 * i + q
                        hs = slice(h * DH, (h + 1) * DH)
                        out = ps[q * DH:(q + 1) * DH, 4, i * DH:(i + 1) * DH]
                        pe.matmul(out, tok[r, ti % 2, 1, hs], u[r, hs], start=True, stop=False)
                        mm = pe.matmul(out, tok[r, ti % 2, 2, hs], tok[r, ti % 2, 3, hs], start=False, stop=True)
                    mm.then_inc(s_N, 1)

            def outputs(ti):
                p0 = tiles[ti][0]
                for hd in range(8):
                    q, i = hd // 4, hd % 4
                    h = 2 * i + q
                    hs = slice(h * DH, (h + 1) * DH)
                    rows = slice(q * DH, (q + 1) * DH)
                    for ch in range(2):
                        k = 2 * ti - 1 + ch
                        pe.matmul(ps[ch * CH:(ch + 1) * CH, 6 + q, i * DH:(i + 1) * DH],
                                  m.ar[rows, i, 1, p0 + ch * CH:p0 + (ch + 1) * CH], St[rows, k, i, :],
                                  start=True, stop=False, skip_group_check=True)
                    pe.matmul(ps[:, 6 + q, i * DH:(i + 1) * DH], msk[:, hd, 3, :], tok[:, ti % 2, 3, hs],
                              start=False, stop=False, skip_group_check=True)
                    pe.matmul(ps[:, 6 + q, i * DH:(i + 1) * DH], msk[:, hd, 1, :], U[:, hs],
                              start=False, stop=True, skip_group_check=True)
                gate(slice(p0, p0 + P), P)

            def gate(span, n):
                pe.matmul(ps[0:n, 0, :], m.sg[:, span], m.g2[:, :], start=True, stop=True)
                for i in range(HP):
                    mm = pe.matmul(ps[0:n, 1, 2 * i:2 * i + 2], m.rk[:, i, span], c("half"), start=True, stop=True)
                mm.then_inc(s_Y, 1)

            def transpose_mix(ti, n):
                pe.wait_ge(s_mix, ti + 1)
                for i in range(HP):
                    mm = pe.transpose(ps[:, 2, i * P:i * P + n], y[0:n, i * P:(i + 1) * P], c("ident")[0:n, 0:n])
                mm.then_inc(s_mt, 1)

            for ti in range(NTL):
                prepare(ti)
                chain(ti)
                if ti:
                    outputs(ti)
                    transpose_mix(ti - 1, P)
                    pe.wait_ge(s_mtc, ti)

            def sums(step, src):
                pe.wait_ge(s_sr, step)
                for j in range(4):
                    mm = pe.matmul(ps[:, 4 + j, :], c("heads"), src[:, 2 * j:2 * j + 2].rearrange("p a i v -> p (a i v)"),
                                   start=True, stop=True)
                mm.then_inc(s_sp, 1)

            sums(1, w1)
            pe.wait_ge(s_sc, 1)
            sums(2, w1)
            pe.wait_ge(s_sc, 2)
            pe.wait_ge(s_sr, 3)
            for j in range(4):
                mm = pe.matmul(ps[0:2, 4 + j, :], c("half"), w1[:, 2 * j:2 * j + 2].rearrange("p a i v -> p (a i v)"),
                               start=True, stop=True)
            mm.then_inc(s_sp, 1)
            for i in range(HP):
                mm = pe.transpose(ps[0:NB, 3, i * P:(i + 1) * P], m.vT[:, i, TP:TA], c("ident"))
            mm.then_inc(s_sp, 1)
            gate(slice(TP, TA), NB)
            transpose_mix(NT, NB)

        @block.scalar
        def _(act):
            for ti in range(NTL):
                n = tiles[ti][1]
                for q in range(4):
                    act.wait_ge(s_tr, 4 * ti + q + 1)
                    if ti >= 2:
                        act.wait_ge(s_Y, ti - 1)
                    act.activation(tok[0:n, ti % 2, q, :], ps[0:n, q % 2, :], ACT.Copy).then_inc(s_trc, 1)
                act.wait_ge(s_AV, ti + 1)
                act.activation(AV[0:n, :], ps[0:n, 0, :], ACT.Copy).then_inc(s_AVc, 1)
                act.wait_ge(s_UW, ti + 1)
                if ti:
                    act.activation(WT[:, :, :], ps[:, 2, :].rearrange("p (i t) -> p i t", i=HP), ACT.Copy).then_inc(s_UWc, 1)
                    act.wait_ge(s_var, ti)
                    act.activation(stat[:, 2, :], stat[:, 1, :], ACT.Sqrt).then_inc(s_rs, 1)
                    act.wait_ge(s_mt, ti)
                    act.activation(m.mixT[:, 0:HP, (ti - 1) * P:ti * P], ps[:, 2, :].rearrange("p (i t) -> p i t", i=HP),
                                   ACT.Copy).then_inc(s_mtc, 1)
                else:
                    act.activation(stmp[:, 0, 0:1], c("ident")[:, 0:1], ACT.Copy).then_inc(s_UWc, 1)
            act.wait_ge(s_sp, 3)
            act.activation(y2, ps[0:2, 4:8, :].rearrange("p a b -> p (a b)"), ACT.Copy).then_inc(s_y2, 1)
            act.wait_ge(s_var, NT + 1)
            act.activation(stat[0:NB, 2, :], stat[0:NB, 1, :], ACT.Sqrt).then_inc(s_rs, 1)
            act.wait_ge(s_mt, NT + 1)
            act.activation(m.mixT[:, 0:HP, SEQ:SEQ + NB], ps[:, 2, :].rearrange("p (i t) -> p i t", i=HP)[:, :, 0:NB],
                           ACT.Copy).then_inc(s_mtc, 1)

        @block.gpsimd
        def _(pool):
            for ti in range(NTL):
                n = tiles[ti][1]
                for q in range(2):
                    pool.wait_ge(s_Am, 8 * ti + 4 * q + 4)
                    if ti:
                        pool.wait_ge(s_UW, ti)
                    link_n = 4 * ti + 2 * q
                    pool.tensor_tensor(XT[0:n, q, :, 0:n], msk[0:n, 4 * q:4 * q + 4, 0, 0:n],
                                       c("firstT")[0:n, 0:n].unsqueeze(1).broadcast_to([n, 4, n]), ALU.mult).then_inc(s_g, 1)
                    pool.wait_ge(s_g, 2 * ti + q + 1)
                    pool.tensor_tensor(XT[0:n, q, :, 0:n], XT[0:n, q, :, 0:n],
                                       c("ident")[0:n, 0:n].unsqueeze(1).broadcast_to([n, 4, n]), ALU.add).then_inc(s_XT0, 1)

        @block.vector
        def _(dve):
            link = Link(dve, s_v)
            dve.wait_ge(s_ld, 48)

            def four(t):
                return t.unsqueeze(1).broadcast_to([t.shape[0], HP, t.shape[1]])

            def prepare(ti):
                p0, n, levels = tiles[ti]
                for hd in range(8):
                    dve.wait_ge(s_A, 8 * ti + hd + 1)
                    dve.tensor_tensor(msk[0:n, hd, :, 0:n], ps[0:n, hd % 2, 0:4 * n].rearrange("s (x t) -> s x t", x=4),
                                      c("mask4")[0:n].rearrange("s (x t) -> s x t", x=4)[:, :, 0:n], ALU.mult).then_inc(s_Am, 1)
                for q in range(2):
                    dve.wait_ge(s_A0, 2 * ti + q + 1)
                    link(dve.tensor_tensor(X[0:n, q, :, 0:n], ps[0:n, 4 + q, 0:4 * n].rearrange("s (x t) -> s x t", x=4),
                                           four(c("first")[0:n, 0:n]), ALU.mult))
                    link(dve.tensor_tensor(X[0:n, q, :, 0:n], X[0:n, q, :, 0:n], four(c("ident")[0:n, 0:n]), ALU.add), s_X)
                for l, lev in enumerate(levels):
                    at = 2 * (levels_before[ti] + l)
                    for q in range(2):
                        dve.wait_ge(s_T, at + q + 1)
                        link(dve.tensor_tensor(T1[0:n, q, :, 0:n], ps[0:n, 2 + q, 0:4 * n].rearrange("s (x t) -> s x t", x=4),
                                               four(c(f"lev{lev}")[0:n, 0:n]), ALU.mult), s_Tc)
                    for q in range(2):
                        dve.wait_ge(s_XX, at + q + 1)
                        if l < len(levels) - 1:
                            dve.tensor_tensor(X[0:n, q, :, 0:n], ps[0:n, 4 + q, 0:4 * n].rearrange("s (x t) -> s x t", x=4),
                                              X[0:n, q, :, 0:n], ALU.add)
                        link(dve.tensor_tensor(XT[0:n, q, :, 0:n], ps[0:n, 6 + q, 0:4 * n].rearrange("s (x t) -> s x t", x=4),
                                               XT[0:n, q, :, 0:n], ALU.add), s_X)
                dve.wait_ge(s_UW, ti + 1)
                link(dve.tensor_copy(U0[0:n, :], ps[0:n, 1, :]), s_UWc)

            def chain(ti):
                for ch in range(2 if ti else 1):
                    k = 2 * ti - 1 + ch if ti else 0
                    r = slice(ch * CH, (ch + 1) * CH)
                    if ti:
                        dve.wait_ge(s_U, k)
                        view = lambda t: t[r, :].rearrange("s (i h v) -> s h i v", h=2, v=DH)
                        link(dve.tensor_tensor(view(U), ps[r, 2:4, 0:HP * DH].rearrange("s h (i v) -> s h i v", i=HP),
                                               view(U0), ALU.add), s_Uc)
                    dve.wait_ge(s_N, k + 1)
                    new = ps[:, 4, 0:HP * DH].rearrange("p (i v) -> p i v", i=HP)
                    if ti:
                        link(dve.tensor_tensor(stmp[:, :, :], new, St[:, k, :, :], ALU.add))
                        new = stmp[:, :, :]
                    link(dve.tensor_tensor(St[:, k + 1, :, :], new, m.eend[:, :, k:k + 1].broadcast_to([P, HP, DH]), ALU.mult), s_S)

            def finish(ti, n, vals):
                y3, sq3 = (t[0:n, :].rearrange("s (h v) -> s h v", v=DH) for t in (y, sq))
                per = lambda j: stat[0:n, j, :].unsqueeze(2).broadcast_to([n, 8, DH])
                link(dve.tensor_reduce(stat[0:n, 0, :], y3, AX.X, ALU.add))
                link(dve.tensor_scalar(stat[0:n, 0, :], stat[0:n, 0, :], 1.0 / DH, None, ALU.mult))
                link(dve.tensor_tensor(y3, y3, per(0), ALU.subtract))
                link(dve.tensor_tensor(sq[0:n, :], y[0:n, :], y[0:n, :], ALU.mult))
                link(dve.tensor_reduce(stat[0:n, 1, :], sq3, AX.X, ALU.add))
                link(dve.tensor_scalar(stat[0:n, 1, :], stat[0:n, 1, :], 1.0 / DH, 64e-5, ALU.mult, ALU.add), s_var)
                dve.wait_ge(s_rs, ti + 1)
                link(dve.reciprocal(stat[0:n, 3, :], stat[0:n, 2, :]))
                link(dve.tensor_tensor(y3, y3, per(3), ALU.mult))
                link(dve.tensor_tensor(y[0:n, :], y[0:n, :], lnw[0:n, :], ALU.mult))
                link(dve.tensor_tensor(y[0:n, :], y[0:n, :], lnb[0:n, :], ALU.add))
                dve.wait_ge(s_Y, ti + 1)
                link(dve.tensor_copy(stat[0:n, 0, :], ps[0:n, 1, 0:8]))
                link(dve.tensor_tensor(sq3, vals, per(0), ALU.mult))
                link(dve.tensor_tensor(y[0:n, :], y[0:n, :], sq[0:n, :], ALU.add))
                link(dve.tensor_tensor(y[0:n, :], y[0:n, :], ps[0:n, 0, :], ALU.mult), s_mix)

            for ti in range(NTL):
                prepare(ti)
                chain(ti)
                if ti:
                    dve.wait_ge(s_Y, ti)
                    if ti >= 2:
                        dve.wait_ge(s_mt, ti - 1)
                    link(dve.tensor_copy(y[:, :].rearrange("s (i h v) -> s h i v", h=2, v=DH),
                                         ps[:, 6:8, 0:HP * DH].rearrange("s h (i v) -> s h i v", i=HP)), s_yc)
                    finish(ti - 1, P, tok[:, ti % 2, 3, :].rearrange("s (h v) -> s h v", v=DH))
                else:
                    link(dve.memset(stat[:, :, :], 0.0), s_yc)

            def over_v(t):
                return t.rearrange("p i b -> p b i").unsqueeze(3).broadcast_to([P, NB, HP, DH])

            def halves(f):
                for b in range(NB):
                    last = f(b)
                return last

            def col(t, b):
                return t[:, :, b:b + 1].broadcast_to([P, HP, DH])

            al, rr = m.ar[:, :, 0, TP:TA], m.ar[:, :, 1, TP:TA]
            bb, kk, vv = m.bt[:, :, TP:TA], m.kt[:, :, TP:TA], m.vT[:, :, TP:TA]
            dve.wait_ge(s_mt, NT)
            link(halves(lambda b: dve.tensor_tensor(w1[:, b], S0[:, b], col(al, b), ALU.mult)), s_sr)
            dve.wait_ge(s_sp, 1)
            psv = lambda b: ps[:, 4 + b // 2, (b % 2) * HP * DH:(b % 2 + 1) * HP * DH].rearrange("p (i v) -> p i v", i=HP)
            link(halves(lambda b: dve.tensor_tensor(w1[:, b], psv(b), col(bb, b), ALU.mult)))
            link(halves(lambda b: dve.tensor_tensor(S0[:, b], S0[:, b], w1[:, b], ALU.add)), s_sc)
            diag = c("diag64").unsqueeze(1).broadcast_to([P, HP, DH])
            link(halves(lambda b: dve.tensor_tensor(w1[:, b], diag, col(vv, b), ALU.mult)), s_sr)
            dve.wait_ge(s_sp, 2)
            link(halves(lambda b: dve.tensor_tensor(w1[:, b], psv(b), col(kk, b), ALU.mult)), s_sc)
            link(halves(lambda b: dve.tensor_tensor(S0[:, b], S0[:, b], w1[:, b], ALU.add)))
            link(halves(lambda b: dve.tensor_tensor(w1[:, b], S0[:, b], col(rr, b), ALU.mult)), s_sr)
            link(halves(lambda b: dve.tensor_tensor(S0[:, b], S0[:, b], col(m.eend[:, :, 9:17], b), ALU.mult)), s_sc)
            dve.wait_ge(s_sp, 4)
            link(dve.tensor_copy(U0[0:NB, :], ps[0:NB, 3, :]))
            dve.wait_ge(s_y2d, 16 * 2 * NB)
            finish(NT, NB, U0[0:NB, :].rearrange("s (h v) -> s h v", v=DH))


def phase_attention(nc, io, m):
    ctx = ExitStack()
    with ctx:
        sb = lambda n, s, dt=F32: ctx.enter_context(nc.sbuf_tensor("t_" + n, s, dt))
        sem = lambda n: ctx.enter_context(nc.semaphore("t_" + n))
        ps, c = m.ps, m.c
        RING = 3
        SCALE = DH ** -0.5
        ring = sb("ring", [P, RING, NPG + 1, RWW])
        pt = sb("pt", [P, NB * NPG], I32)
        idx = sb("idx", [P, NB * NPG], I32)
        lam4 = sb("lam4", [P, 4, DH])
        lamj = sb("lamj", [P, DH])
        lam2 = sb("lam2", [P, 2])
        nlam = sb("nlam", [P, 1])
        subw = sb("subw", [P, RWW])
        pr = sb("pr", [P, 2, TP])
        att = sb("att", [P, TP])
        attT = sb("attT", [P, NT + 1, P])
        mx = sb("mx", [P, 2])
        Z = sb("Z", [P, 2])
        rz = sb("rz", [P, 2])
        o = sb("o", [P, RWW])
        osq = sb("osq", [P, RWW])
        ost = sb("ost", [P, 3, NH])
        sc = sb("sc", [P, NPG + 1, NB * 8])
        PT = sb("PT", [NB * 8, PAST + 1])
        sst = sb("sst", [NB * 8, 8])
        attS = sb("attS", [P, NPG + 1, NB * NH])
        oT = sb("oT", [P, NH * NB])

        s_ld = sem("ld")
        s_k = [sem(f"k{i}") for i in range(RING)]
        s_kn = [sem(f"kn{i}") for i in range(RING)]
        s_ix = sem("ix")
        s_use = sem("use")
        s_lam, s_lame, s_lamd = sem("lam"), sem("lame"), sem("lamd")
        s_sc, s_mx, s_ex = sem("sc"), sem("mx"), sem("ex")
        s_at, s_tr, s_trc, s_pv = sem("at"), sem("tr"), sem("trc"), sem("pv")
        s_oc, s_ms, s_rs, s_on, s_ot, s_otc = sem("oc"), sem("ms"), sem("rs"), sem("on"), sem("ot"), sem("otc")
        s_qb, s_qbu = sem("qb"), sem("qbu")
        s_ss, s_st, s_smx, s_sex, s_sP, s_sT, s_sA, s_so, s_soc = (sem(n) for n in
            ("ss", "st2", "smx", "sex", "sP", "sT", "sA", "so", "soc"))
        s_v, s_a = sem("v"), sem("a")
        NQ = NT * NH
        width = lambda t: NMETA + P * (t + 1)

        block = ctx.enter_context(nc.Block())

        @block.sync
        def _(sp):
            sp.dma_start(pt[:, :], io["pages"].partition_broadcast(P)).then_inc(s_ld, 16)
            sp.dma_start(lam4[:, :, :], io["lams"].partition_broadcast(P)).then_inc(s_ld, 16)
            sp.dma_start(subw[:, :], io["subln_w"].partition_broadcast(P)).then_inc(s_ld, 16)
            for j in range(2 * NB):
                b = j % NB
                if j >= RING:
                    sp.wait_ge(s_use, j - RING + 1)
                src = m.qks[b:b + 1, 1, :] if j < NB else m.vtok[b:b + 1, NT, :]
                sp.dma_start(ring[0:1, j % RING, NPG, :], src).then_inc(s_kn[j % RING], 16)

        @block.gpsimd
        def _(pool):
            pool.wait_ge(s_ix, 1)
            for j in range(2 * NB):
                b = j % NB
                if j >= RING:
                    pool.wait_ge(s_use, j - RING + 1)
                for g in range(NPG):
                    pool.indirect_dma_start(
                        out=ring[:, j % RING, g, :], out_offset=None,
                        in_=io["cache_k"] if j < NB else io["cache_v"],
                        in_offset=bass.IndirectOffsetOnAxis(ap=idx[:, b * NPG + g:b * NPG + g + 1], axis=0),
                    ).then_inc(s_k[j % RING], 16)

        def landed(eng, j):
            eng.wait_ge(s_k[j % RING], 16 * NPG * (j // RING + 1))
            eng.wait_ge(s_kn[j % RING], 16 * (j // RING + 1))

        @block.tensor
        def _(pe):
            def scores(n):
                t, h = divmod(n, NH)
                w = width(t)
                if n >= 1:
                    pe.wait_ge(s_ex, n)
                for x in range(2):
                    rows = slice(x * DH, (x + 1) * DH)
                    out = ps[:, 2 * x:2 * x + 2, :].rearrange("p a b -> p (a b)")
                    cuts = [(0, min(w, 512))] + ([(512, w)] if w > 512 else [])
                    for a, b in cuts:
                        pe.matmul(out[:, a:b], m.qT[rows, h, t * P:(t + 1) * P], m.kT[rows, h, a:b],
                                  start=True, stop=False)
                        lo = max(a, w - P)
                        mm = pe.matmul(out[:, lo:b], c("ident"), c("causal")[:, lo - (w - P):b - (w - P)],
                                       start=False, stop=True)
                mm.then_inc(s_sc, 1)

            def values(n):
                t, h = divmod(n, NH)
                hs = slice(h * DV, (h + 1) * DV)
                pe.wait_ge(s_at, n + 1)
                if n >= 1:
                    pe.wait_ge(s_trc, n)
                for j in range(t + 1):
                    pe.transpose(ps[:, 4, j * P:(j + 1) * P], att[:, NMETA + j * P:NMETA + (j + 1) * P], c("ident"))
                pe.transpose(ps[0:NMETA, 5, 0:P], att[:, 0:NMETA], c("ident")).then_inc(s_tr, 1)

            def weigh(n):
                t, h = divmod(n, NH)
                hs = slice(h * DV, (h + 1) * DV)
                pe.wait_ge(s_trc, n + 1)
                if h == 0 and t:
                    pe.wait_ge(s_oc, t)
                pe.matmul(ps[:, 6, hs], attT[0:NMETA, NT, :], m.vmeta[:, hs], start=True, stop=False)
                for j in range(t + 1):
                    mm = pe.matmul(ps[:, 6, hs], attT[:, j, :], m.vtok[:, j, hs], start=False, stop=(j == t))
                mm.then_inc(s_pv, 1)

            def transpose_out(t, n):
                pe.wait_ge(s_on, t + 1)
                for i in range(NH):
                    mm = pe.transpose(ps[:, 5, i * P:i * P + n], o[0:n, i * P:(i + 1) * P], c("ident")[0:n, 0:n])
                mm.then_inc(s_ot, 1)

            def query(b):
                if b >= 1:
                    pe.wait_ge(s_qbu, b)
                pe.matmul(ps[:, 7, :], c("one8")[0:NB, b:b + 1].broadcast_to([NB, P]), m.qks[0:NB, 0, :],
                          start=True, stop=True).then_inc(s_qb, 1)

            scores(0)
            for n in range(NQ):
                if n + 1 < NQ:
                    scores(n + 1)
                values(n)
                weigh(n)
                if n % NH == NH - 1:
                    transpose_out(n // NH, P)
                    pe.wait_ge(s_otc, n // NH + 1)
                if n % 2 == 1:
                    query(n // 2)
            pe.wait_ge(s_ss, NB)
            for g in range(NPG):
                pe.transpose(ps[0:NB * 8, g // 4, (g % 4) * P:(g % 4 + 1) * P], sc[:, g, :], c("ident"))
            pe.transpose(ps[0:NB * 8, 2, 0:1], sc[0:1, NPG, :], c("ident")[0:1, 0:1]).then_inc(s_st, 1)
            pe.wait_ge(s_sP, 1)
            for g in range(NPG):
                pe.transpose(ps[:, 3, g * NB * 8:(g + 1) * NB * 8], PT[:, g * P:(g + 1) * P], c("ident")[0:NB * 8, 0:NB * 8])
            pe.transpose(ps[0:1, 4, 0:NB * 8], PT[:, PAST:PAST + 1], c("ident")[0:NB * 8, 0:NB * 8]).then_inc(s_sT, 1)
            pe.wait_ge(s_sA, 1)
            for b in range(NB):
                landed(pe, NB + b)
                slot = (NB + b) % RING
                for h in range(NH):
                    out = ps[:, 6, h * NB + b:h * NB + b + 1]
                    for g in range(NPG):
                        pe.matmul(out, ring[:, slot, g, h * DV:(h + 1) * DV], attS[:, g, b * NH + h:b * NH + h + 1],
                                  start=(g == 0), stop=False)
                    mm = pe.matmul(out, ring[0:1, slot, NPG, h * DV:(h + 1) * DV], attS[0:1, NPG, b * NH + h:b * NH + h + 1],
                                   start=False, stop=True)
                mm.then_inc(s_so, 1)
            pe.wait_ge(s_soc, 1)
            for h in range(NH):
                mm = pe.transpose(ps[0:NB, 7, h * DV:(h + 1) * DV], oT[:, h * NB:(h + 1) * NB], c("ident"))
            mm.then_inc(s_pv, 1)
            transpose_out(NT, NB)

        @block.scalar
        def _(act):
            act.wait_ge(s_lam, 1)
            act.activation(lam2[:, :], lam2[:, :], ACT.Exp).then_inc(s_lame, 1)

            def root(t, n):
                act.wait_ge(s_ms, t + 1)
                act.activation(ost[0:n, 1, :], ost[0:n, 0, :], ACT.Sqrt).then_inc(s_rs, 1)
                act.wait_ge(s_ot, t + 1)
                act.activation(m.mixT[:, HP:2 * HP, t * P:t * P + n], ps[:, 5, :].rearrange("p (i t) -> p i t", i=NH)[:, :, 0:n],
                               ACT.Copy).then_inc(s_otc, 1)

            for n in range(NQ):
                t, h = divmod(n, NH)
                w = width(t)
                act.wait_ge(s_mx, n + 1)
                if n >= 1:
                    act.wait_ge(s_at, n)
                for x in range(2):
                    last = act.activation(pr[:, x, 0:w], ps[:, 2 * x:2 * x + 2, :].rearrange("p a b -> p (a b)")[:, 0:w],
                                          ACT.Exp, bias=mx[:, x:x + 1], scale=SCALE, accum_out=Z[:, x:x + 1])
                last.then_inc(s_ex, 1)
                act.wait_ge(s_tr, n + 1)
                if n >= 1:
                    act.wait_ge(s_pv, n)
                act.activation(attT[:, 0:t + 1, :], ps[:, 4, 0:(t + 1) * P].rearrange("p (j q) -> p j q", q=P), ACT.Copy)
                act.activation(attT[0:NMETA, NT, :], ps[0:NMETA, 5, 0:P], ACT.Copy).then_inc(s_trc, 1)
                if h == NH - 1:
                    root(t, P)
            act.wait_ge(s_smx, 1)
            act.activation(PT[:, 0:PAST], ps[0:NB * 8, 0:2, :].rearrange("p a b -> p (a b)"), ACT.Exp,
                           bias=sst[:, 2:3], scale=SCALE, accum_out=sst[:, 3:4])
            act.activation(PT[:, PAST:PAST + 1], ps[0:NB * 8, 2, 0:1], ACT.Exp, bias=sst[:, 2:3], scale=SCALE).then_inc(s_sex, 1)
            act.wait_ge(s_so, NB)
            act.activation(oT[:, :], ps[:, 6, 0:NH * NB], ACT.Copy).then_inc(s_soc, 1)
            root(NT, NB)

        @block.vector
        def _(dve):
            link = Link(dve, s_v)
            dve.wait_ge(s_ld, 48)
            link(dve.tensor_scalar(idx[:, :], pt[:, :], float(PAGE), c("rowid"), ALU.mult, ALU.add), s_ix)
            for a in range(2):
                link(dve.tensor_tensor(lamj[:, :], lam4[:, 2 * a, :], lam4[:, 2 * a + 1, :], ALU.mult))
                ins = dve.tensor_reduce(lam2[:, a:a + 1], lamj[:, :], AX.X, ALU.add)
                link(ins, s_lam if a else None)
            dve.wait_ge(s_lame, 1)
            link(dve.tensor_tensor(nlam[:, :], lam2[:, 1:2], lam2[:, 0:1], ALU.subtract))
            link(dve.tensor_scalar(nlam[:, :], nlam[:, :], -LAM_INIT, None, ALU.add))
            link(dve.tensor_scalar(subw[:, :], subw[:, :], 1.0 - LAM_INIT, None, ALU.mult))

            def soft(n):
                t, h = divmod(n, NH)
                w = width(t)
                dve.wait_ge(s_sc, n + 1)
                s = ps[:, 0:4, :].rearrange("p (x a) b -> p x (a b)", x=2)[:, :, 0:w]
                link(dve.tensor_reduce(mx[:, :], s, AX.X, ALU.max))
                link(dve.tensor_scalar(mx[:, :], mx[:, :], -SCALE, None, ALU.mult), s_mx)

            def combine(n):
                t, h = divmod(n, NH)
                w = width(t)
                dve.wait_ge(s_ex, n + 1)
                if n >= 1:
                    dve.wait_ge(s_tr, n)
                link(dve.reciprocal(rz[:, :], Z[:, :]))
                link(dve.tensor_tensor(rz[:, 1:2], rz[:, 1:2], nlam[:, :], ALU.mult))
                link(dve.tensor_scalar(pr[:, 1, 0:w], pr[:, 1, 0:w], rz[:, 1:2], None, ALU.mult))
                link(dve.scalar_tensor_tensor(att[:, 0:w], pr[:, 0, 0:w], rz[:, 0:1], pr[:, 1, 0:w], ALU.mult, ALU.add), s_at)

            def finish(t, n, bank):
                dve.wait_ge(s_pv, NH * (t + 1) if t < NT else NQ + 1)
                if t >= 1:
                    dve.wait_ge(s_ot, t)
                o3, q3 = (x[0:n, :].rearrange("p (h v) -> p h v", h=NH) for x in (o, osq))
                link(dve.tensor_copy(o[0:n, :], ps[0:n, bank, :]), s_oc)
                link(dve.tensor_tensor(osq[0:n, :], o[0:n, :], o[0:n, :], ALU.mult))
                link(dve.tensor_reduce(ost[0:n, 0, :], q3, AX.X, ALU.add))
                link(dve.tensor_scalar(ost[0:n, 0, :], ost[0:n, 0, :], 1.0 / DV, 1e-5, ALU.mult, ALU.add), s_ms)
                dve.wait_ge(s_rs, t + 1)
                link(dve.reciprocal(ost[0:n, 2, :], ost[0:n, 1, :]))
                link(dve.tensor_tensor(o3, o3, ost[0:n, 2, :].unsqueeze(2).broadcast_to([n, NH, DV]), ALU.mult))
                link(dve.tensor_tensor(o[0:n, :], o[0:n, :], subw[0:n, :], ALU.mult), s_on)

            def sample_scores(b):
                dve.wait_ge(s_qb, b + 1)
                landed(dve, b)
                slot = b % RING
                k = ring[:, slot, 0:NPG, :]
                dve.tensor_tensor(k, k, ps[:, 7, :].unsqueeze(1).broadcast_to([P, NPG, RWW]), ALU.mult)
                kn = ring[0:1, slot, NPG, :]
                link(dve.tensor_tensor(kn, kn, ps[0:1, 7, :], ALU.mult), s_qbu)
                dve.tensor_reduce(sc[:, 0:NPG, b * 8:(b + 1) * 8], k.rearrange("p g (x d) -> p g x d", d=DH), AX.X, ALU.add)
                link(dve.tensor_reduce(sc[0:1, NPG, b * 8:(b + 1) * 8], kn.rearrange("p (x d) -> p x d", d=DH), AX.X, ALU.add), s_ss)
                dve.engine_nop().then_inc(s_use, 1)

            soft(0)
            for n in range(NQ):
                combine(n)
                if n + 1 < NQ:
                    soft(n + 1)
                if n % NH == NH - 1:
                    finish(n // NH, P, 6)
                if n % 2 == 1:
                    sample_scores(n // 2)
            dve.wait_ge(s_st, 1)
            link(dve.tensor_reduce(sst[:, 0:1], ps[0:NB * 8, 0:2, :].rearrange("p a b -> p (a b)"), AX.X, ALU.max))
            link(dve.tensor_tensor(sst[:, 1:2], sst[:, 0:1], ps[0:NB * 8, 2, 0:1], ALU.max))
            link(dve.tensor_scalar(sst[:, 2:3], sst[:, 1:2], -SCALE, None, ALU.mult), s_smx)
            dve.wait_ge(s_sex, 1)
            link(dve.tensor_tensor(sst[:, 4:5], sst[:, 3:4], PT[:, PAST:PAST + 1], ALU.add))
            link(dve.reciprocal(sst[:, 5:6], sst[:, 4:5]))
            link(dve.scalar_tensor_tensor(sst[:, 6:7], c("map")[0:NB * 8, 1:2], nlam[0:NB * 8, :], c("map")[0:NB * 8, 0:1], ALU.mult, ALU.add))
            link(dve.tensor_tensor(sst[:, 7:8], sst[:, 6:7], sst[:, 5:6], ALU.mult))
            link(dve.tensor_scalar(PT[:, :], PT[:, :], sst[:, 7:8], None, ALU.mult), s_sP)
            dve.wait_ge(s_sT, 1)
            dve.tensor_reduce(attS[:, 0:NPG, :], ps[:, 3, :].rearrange("p (g x y) -> p g x y", g=NPG, y=2), AX.X, ALU.add)
            link(dve.tensor_reduce(attS[0:1, NPG, :], ps[0:1, 4, 0:NB * 8].rearrange("p (x y) -> p x y", y=2), AX.X, ALU.add), s_sA)
            for b in range(NB):
                dve.wait_ge(s_so, b + 1)
                dve.engine_nop().then_inc(s_use, 1)
            finish(NT, NB, 7)


def phase_peer(nc, io, m):
    ctx = ExitStack()
    with ctx:
        sb = lambda n, s, dt=F32: ctx.enter_context(nc.sbuf_tensor("p_" + n, s, dt))
        sem = lambda n: ctx.enter_context(nc.semaphore("p_" + n))
        ps, c = m.ps, m.c
        G = 4
        W2 = 2 * G
        PARTS = 8
        ITERS = SLOTS // W2 // PARTS
        NTT = NT + 1
        w_out = sb("w_out", [P, KT, D])
        wq = sb("wq", [P, KT, D])
        skT = sb("skT", [P, PKH, NKEY])
        ln = sb("ln", [P, 4, D])
        xin = sb("xin", [P, D])
        x1 = sb("x1", [P, 2, D])
        qT = xin[:, :].rearrange("p (k t) -> p k t", k=KT)
        st = sb("st", [P, 8])
        s = sb("s", [P, 2 * PKH, NKEY])
        x1T = s[:, 0:KT, :]
        work = sb("work", [P, 256])
        vals = sb("vals", [P, 2 * PKH, TOPK])
        ix = sb("ix", [P, 2 * PKH, TOPK], U32)
        ixf = sb("ixf", [P, 2 * PKH, TOPK])
        cand = sb("cand", [P, PKH, TOPK, TOPK])
        tv = sb("tv", [P, PKH, TOPK])
        sel = sb("sel", [P, PKH, TOPK], U32)
        sab = sb("sab", [P, 2, SLOTS], U32)
        sabf = sb("sabf", [P, 2, SLOTS])
        ia = sb("ia", [P, 2, SLOTS])
        gs = sb("gs", [P, 2, PKH])
        idx = sb("idx", [P, 2, SLOTS], I32)
        gate = sb("gate", [P, 2, SLOTS])
        Ur = sb("Ur", [P, W2, D])
        Vr = sb("Vr", [P, W2, D])
        idxu = sb("idxu", [P, W2], I32)
        idxv = sb("idxv", [P, W2], I32)
        dot = sb("dot", [P, W2])
        gel = sb("gel", [P, W2])
        wgt = sb("wgt", [P, W2])
        dg = sb("dg", [P, G, P])
        idr = sb("idr", [P, PKH], I32)
        gtr = sb("gtr", [P, PKH])
        wsel = sb("wsel", [P, PKH, NB])
        eq = s[:, :, :].rearrange("p a b -> p (a b)")

        s_ld = sem("ld")
        s_x = sem("x")
        s_op, s_res = sem("op"), sem("res")
        s_cen, s_mean = sem("cen"), sem("mean")
        s_sqs, s_vr, s_rt = sem("sqs"), sem("vr"), sem("rt")
        s_x1, s_tr, s_trc = sem("x1"), sem("tr"), sem("trc")
        s_q, s_qc, s_sc, s_scc = sem("q"), sem("qc"), sem("sc"), sem("scc")
        s_tv, s_ge = sem("tv"), sem("ge")
        s_idx = sem("idx")
        s_u = [sem(f"u{i}") for i in range(W2)]
        s_vv = [sem(f"v{i}") for i in range(W2)]
        s_turn = sem("turn")
        s_iu, s_iv = sem("iu"), sem("iv")
        s_dot = sem("dot")
        s_gel, s_w, s_dg = sem("gel"), sem("w"), sem("dg")
        s_vu = sem("vu")
        s_acc = sem("acc")
        s_y, s_yo = sem("y"), sem("yo")
        s_rs, s_rep, s_repc, s_ws = sem("rs"), sem("rep"), sem("repc"), sem("ws")
        s_v, s_a = sem("v"), sem("a")
        rows_of = lambda t: P if t < NT else NB

        block = ctx.enter_context(nc.Block())

        @block.sync
        def _(sp):
            sp.dma_start(w_out[:, :, :], io["w_out"].rearrange("(k p) n -> p k n", p=P)).then_inc(s_ld, 16)
            for j, n in enumerate(("ln1_w", "ln1_b", "ln2_w", "ln2_b")):
                sp.dma_start(ln[:, j, :], io[n].partition_broadcast(P)).then_inc(s_ld, 16)
            sp.dma_start(skT[:, :, :], io["skT"]).then_inc(s_ld, 16)
            sp.dma_start(wq[:, :, :], io["pk_wq"].rearrange("(k p) n -> p k n", p=P)).then_inc(s_ld, 16)
            for t in range(NTT):
                n = rows_of(t)
                if t:
                    sp.wait_ge(s_sc, t)
                sp.dma_start(xin[0:n, :], io["x_tok"][t * P:t * P + n, :]).then_inc(s_x, 16)
                if t >= 2:
                    sp.wait_ge(s_y, t - 1)
                    sp.dma_start(io["y_out"][(t - 2) * P:(t - 1) * P, :], x1[:, t % 2, :]).then_inc(s_yo, 16)
            sp.wait_ge(s_idx, NTT)
            for b in range(NB):
                sp.dma_start(idr[b * TOPK:(b + 1) * TOPK, :], idx[b:b + 1, NT % 2, :].rearrange("o (w h) -> o w h", h=PKH)
                             ).then_inc(s_rs, 16)
                sp.dma_start(gtr[b * TOPK:(b + 1) * TOPK, :], gate[b:b + 1, NT % 2, :].rearrange("o (w h) -> o w h", h=PKH)
                             ).then_inc(s_rs, 16)
            for t in range(NTT - 2, NTT):
                sp.wait_ge(s_y, t + 1)
                n = rows_of(t)
                sp.dma_start(io["y_out"][t * P:t * P + n, :], x1[0:n, t % 2, :]).then_inc(s_yo, 16)
            sp.wait_ge(s_yo, 16 * NTT)

        @block.gpsimd
        def _(pool):
            def gather(table, dst, at, s_to):
                pool.indirect_dma_start(out=dst, out_offset=None, in_=io[table],
                                        in_offset=bass.IndirectOffsetOnAxis(ap=at, axis=0)).then_inc(s_to, 16)

            for t in range(NT):
                pool.wait_ge(s_idx, t + 1)
                for part in range(PARTS):
                    it0 = ITERS * part
                    with pool.Fori(0, ITERS) as i:
                        done = 2 * (SLOTS // W2 * t + it0)
                        for half in range(2):
                            col = idx[:, t % 2, bass.ds(W2 * i + (W2 * it0 + half * G), G)]
                            hs = slice(half * G, (half + 1) * G)
                            pool.wait_ge(s_dot, 2 * i + (done + half + 1))
                            pool.sem_inc(s_turn, 1)
                            pool.tensor_copy(idxu[:, hs], col).then_inc(s_iu, 1)
                            pool.wait_ge(s_iu, 2 * i + (done + half + 1))
                            pool.sem_inc(s_turn, 1)
                            for q in range(half * G, (half + 1) * G):
                                gather("peer_u", Ur[:, q, :], idxu[:, q:q + 1], s_u[q])
                            pool.wait_ge(s_vu, 2 * i + (done + half + 1))
                            pool.sem_inc(s_turn, 1)
                            pool.tensor_copy(idxv[:, hs], col).then_inc(s_iv, 1)
                            pool.wait_ge(s_iv, 2 * i + (done + half + 1))
                            pool.sem_inc(s_turn, 1)
                            for q in range(half * G, (half + 1) * G):
                                gather("peer_v", Vr[:, q, :], idxv[:, q:q + 1], s_vv[q])
            pool.wait_ge(s_rs, 16 * 2 * NB)
            done = 2 * (SLOTS // W2 * NT)
            for half in range(2):
                pool.wait_ge(s_dot, done + half + 1)
                for h in range(half * G, (half + 1) * G):
                    gather("peer_u", Ur[:, h, :], idr[:, h:h + 1], s_u[h])
                pool.wait_ge(s_vu, done + half + 1)
                for h in range(half * G, (half + 1) * G):
                    gather("peer_v", Vr[:, h, :], idr[:, h:h + 1], s_vv[h])

        @block.tensor
        def _(pe):
            pe.wait_ge(s_ld, 16 * 7)

            def prep(t, part):
                n = rows_of(t)
                if part == 0:
                    if t:
                        pe.wait_ge(s_scc, 4 * t)
                    for a in range(2):
                        for k in range(KT):
                            mm = pe.matmul(ps[0:n, a, :], m.mixT[:, k, t * P:t * P + n], w_out[:, k, a * 512:(a + 1) * 512],
                                           start=(k == 0), stop=(k == KT - 1))
                    mm.then_inc(s_op, 1)
                if part == 1:
                    pe.wait_ge(s_x1, t + 1)
                    for a in range(2):
                        for k in range(4 * a, 4 * a + 4):
                            mm = pe.transpose(ps[:, 2 + a, (k % 4) * P:(k % 4) * P + n], x1[0:n, t % 2, k * P:(k + 1) * P],
                                              c("ident")[0:n, 0:n])
                        mm.then_inc(s_tr, 1)
                    pe.wait_ge(s_trc, 2 * t + 2)
                    for a in range(2):
                        for f in range(4 * a, 4 * a + 4):
                            for k in range(KT):
                                mm = pe.matmul(ps[:, a, (f % 4) * P:(f % 4) * P + n], wq[:, k, f * P:(f + 1) * P], x1T[:, k, 0:n],
                                               start=(k == 0), stop=(k == KT - 1))
                        mm.then_inc(s_q, 1)
                    pe.wait_ge(s_qc, 2 * t + 2)
                    for x in range(2):
                        for h in range(PKH):
                            mm = pe.matmul(ps[0:n, 2 * x + h // 4, (h % 4) * P:(h % 4 + 1) * P], qT[x * DH:(x + 1) * DH, h, 0:n],
                                           skT[x * DH:(x + 1) * DH, h, :], start=True, stop=True)
                    mm.then_inc(s_sc, 1)

            def gather(t, part):
                acc = ps[:, 4 + 2 * (t % 2):6 + 2 * (t % 2), :]
                if part == 0:
                    if t >= 2:
                        pe.wait_ge(s_res, t - 1)
                    for a in range(2):
                        pe.matmul(acc[:, a, :], m.zero[0:1, :], wq[0:1, 0, 0:512], start=True, stop=False, skip_group_check=True)
                it0 = ITERS * part
                done = 2 * (SLOTS // W2 * t + it0)
                with pe.Fori(0, ITERS) as i:
                    for half in range(2):
                        for q in range(half * G, (half + 1) * G):
                            pe.wait_ge(s_dg, W2 * i + (W2 // 2 * done + q + 1))
                            pe.wait_ge(s_vv[q], 16 * i + (8 * done + 16))
                            for a in range(2):
                                mm = pe.matmul(acc[:, a, :], dg[:, q % G, :], Vr[:, q, a * 512:(a + 1) * 512],
                                               start=False, stop=False, skip_group_check=True)
                        mm.then_inc(s_vu, 1)
                if part == PARTS - 1:
                    for a in range(2):
                        mm = pe.matmul(acc[:, a, :], m.zero[0:1, :], wq[0:1, 0, 0:512], start=False, stop=True, skip_group_check=True)
                    mm.then_inc(s_acc, 1)

            for part in range(PARTS):
                prep(0, part)
            for t in range(NT):
                for part in range(PARTS):
                    gather(t, part)
                    prep(t + 1, part)
            for a in range(2):
                pe.wait_ge(s_scc, 4 * NTT)
                mm = pe.matmul(ps[:, a, :], c("spread")[0:NB, :], x1[0:NB, NT % 2, a * 512:(a + 1) * 512], start=True, stop=True)
            mm.then_inc(s_rep, 1)
            pe.wait_ge(s_ws, 1)
            for h in range(PKH):
                pe.wait_ge(s_vv[h], 16 * (SLOTS // W2 * NT + 1))
                for a in range(2):
                    mm = pe.matmul(ps[0:NB, 4 + a, :], wsel[:, h, :], Vr[:, h, a * 512:(a + 1) * 512],
                                   start=(h == 0), stop=(h == PKH - 1), skip_group_check=True)
            mm.then_inc(s_acc, 1)

        @block.scalar
        def _(act):
            norms = [0]

            def norm(x, n):
                norms[0] += 1
                k = norms[0]
                act.wait_ge(s_mean, k)
                act.activation(x, x, ACT.Identity, bias=st[0:n, 1:2]).then_inc(s_cen, 1)
                act.wait_ge(s_cen, k)
                act.activation(cand[0:n, :, :, :].rearrange("p a b c -> p (a b c)")[:, 0:D], x, ACT.Square,
                               accum_out=st[0:n, 2:3]).then_inc(s_sqs, 1)
                act.wait_ge(s_vr, k)
                act.activation(st[0:n, 4:5], st[0:n, 3:4], ACT.Sqrt).then_inc(s_rt, 1)

            def prep(t, part):
                n = rows_of(t)
                if part == 0:
                    norm(x1[0:n, t % 2, :], n)
                if part == 1:
                    if t:
                        act.wait_ge(s_idx, t)
                    for a in range(2):
                        act.wait_ge(s_tr, 2 * t + a + 1)
                        act.activation(x1T[:, 4 * a:4 * a + 4, 0:n], ps[:, 2 + a, :].rearrange("p (k t) -> p k t", k=4)[:, :, 0:n],
                                       ACT.Copy).then_inc(s_trc, 1)
                    for a in range(2):
                        act.wait_ge(s_q, 2 * t + a + 1)
                        act.activation(qT[:, 4 * a:4 * a + 4, 0:n], ps[:, a, :].rearrange("p (k t) -> p k t", k=4)[:, :, 0:n],
                                       ACT.Copy).then_inc(s_qc, 1)
                    act.wait_ge(s_sc, t + 1)
                    for a in range(4):
                        act.activation(s[0:n, 4 * a:4 * a + 4, :], ps[0:n, a, :].rearrange("p (k t) -> p k t", k=4),
                                       ACT.Copy).then_inc(s_scc, 1)
                if part == PARTS - 1:
                    act.wait_ge(s_tv, t + 1)
                    act.activation(tv[0:n], tv[0:n], ACT.Exp).then_inc(s_ge, 1)

            def gather(t, part):
                it0 = ITERS * part
                done = 2 * (SLOTS // W2 * t + it0)
                with act.Fori(0, ITERS) as i:
                    for half in range(2):
                        hs = slice(half * G, (half + 1) * G)
                        act.wait_ge(s_dot, 2 * i + (done + half + 3))
                        act.activation(gel[:, hs], dot[:, hs], ACT.Gelu).then_inc(s_gel, 1)
                    for half in range(2):
                        act.wait_ge(s_w, 2 * i + (done + half + 1))
                        act.wait_ge(s_vu, 2 * i + (done + half + 2))
                        for q in range(half * G, (half + 1) * G):
                            act.activation(dg[:, q % G, :], c("ident"), ACT.Copy, scale=wgt[:, q:q + 1]).then_inc(s_dg, 1)

            for part in range(PARTS):
                prep(0, part)
            for t in range(NT):
                for part in range(PARTS):
                    gather(t, part)
                    prep(t + 1, part)
                norm(x1[:, t % 2, :], P)
            act.wait_ge(s_rep, 1)
            act.activation(xin[:, :], ps[:, 0:2, :].rearrange("p a b -> p (a b)"), ACT.Copy).then_inc(s_repc, 1)
            act.wait_ge(s_dot, 2 * (SLOTS // W2 * NT) + 3)
            act.activation(gel[:, :], dot[:, :], ACT.Gelu).then_inc(s_gel, 1)
            norm(x1[0:NB, NT % 2, :], NB)

        @block.vector
        def _(dve):
            link = Link(dve, s_v)
            dve.wait_ge(s_ld, 16 * 7)
            norms = [0]

            def norm(x, a, b, n):
                norms[0] += 1
                k = norms[0]
                link(dve.tensor_tensor(st[0:n, 0:1], st[0:n, 0:1], st[0:n, 5:6], ALU.add))
                link(dve.tensor_scalar(st[0:n, 1:2], st[0:n, 0:1], -1.0 / D, None, ALU.mult), s_mean)
                dve.wait_ge(s_sqs, k)
                link(dve.tensor_scalar(st[0:n, 3:4], st[0:n, 2:3], 1.0 / D, 1e-5, ALU.mult, ALU.add), s_vr)
                dve.wait_ge(s_rt, k)
                link(dve.reciprocal(st[0:n, 6:7], st[0:n, 4:5]))
                link(dve.scalar_tensor_tensor(x, x, st[0:n, 6:7], ln[0:n, a, :], ALU.mult, ALU.mult))
                return dve.tensor_tensor(x, x, ln[0:n, b, :], ALU.add)

            def top16(val, ind, src, n):
                w = work[0:n, 0:src.shape[1]]
                link(dve.max(val[:, 0:8], src))
                dve.max_index(ind[:, 0:8], val[:, 0:8], src)
                link(dve.match_replace(w, val[:, 0:8], src, -3.0e38))
                link(dve.max(val[:, 8:16], w))
                return dve.max_index(ind[:, 8:16], val[:, 8:16], w)

            def prep(t, part):
                n = rows_of(t)
                if part == 0:
                    dve.wait_ge(s_op, t + 1)
                    dve.wait_ge(s_x, 16 * (t + 1))
                    if t >= 2:
                        dve.wait_ge(s_yo, 16 * (t - 1))
                    for a in range(2):
                        cs = slice(a * 512, (a + 1) * 512)
                        last = dve.scalar_tensor_tensor(x1[0:n, t % 2, cs], xin[0:n, cs], ALPHA, ps[0:n, a, :], ALU.mult, ALU.add,
                                                        accum_out=st[0:n, 5 * a:5 * a + 1])
                    link(last)
                    link(norm(x1[0:n, t % 2, :], 0, 1, n), s_x1)
                if 2 <= part <= 4:
                    dve.wait_ge(s_scc, 4 * t + 4)
                    for u in range(6 * (part - 2), min(6 * (part - 1), 16)):
                        link(top16(vals[0:n, u, :], ix[0:n, u, :], s[0:n, u, :], n))
                if part == 4:
                    link(dve.tensor_copy(ixf[0:n], ix[0:n]))
                    link(dve.tensor_tensor(cand[0:n], vals[0:n, 0:PKH, :].unsqueeze(3).broadcast_to([n, PKH, TOPK, TOPK]),
                                           vals[0:n, PKH:, :].unsqueeze(2).broadcast_to([n, PKH, TOPK, TOPK]), ALU.add))
                if 5 <= part <= 6:
                    for h in range(4 * (part - 5), 4 * (part - 4)):
                        link(top16(tv[0:n, h, :], sel[0:n, h, :], cand[0:n, h].rearrange("p a b -> p (a b)"), n))
                if part == 7:
                    sf = sel[0:n].rearrange("p h w -> p (h w)")
                    link(dve.tensor_copy(gs[0:n, 0, :], tv[0:n, :, 0]))
                    link(dve.tensor_tensor(tv[0:n], tv[0:n], gs[0:n, 0, :].unsqueeze(2).broadcast_to([n, PKH, TOPK]),
                                           ALU.subtract), s_tv)
                    dve.tensor_scalar(sab[0:n, 0, :], sf, 4, None, ALU.logical_shift_right)
                    link(dve.tensor_scalar(sab[0:n, 1, :], sf, 15, None, ALU.bitwise_and))
                    link(dve.tensor_copy(sabf[0:n], sab[0:n]))
                    e3 = eq[0:n, :].rearrange("p (x k) -> p x k", k=TOPK)
                    e4 = eq[0:n, :].rearrange("p (h w k) -> p h w k", h=PKH, k=TOPK)
                    for x in range(2):
                        link(dve.tensor_tensor(e3, sabf[0:n, x, :].unsqueeze(2).broadcast_to([n, SLOTS, TOPK]),
                                               c("iota16")[0:n].unsqueeze(1).broadcast_to([n, SLOTS, TOPK]), ALU.is_equal))
                        link(dve.tensor_tensor(e4, e4, ixf[0:n, x * PKH:(x + 1) * PKH, :].unsqueeze(2).broadcast_to([n, PKH, TOPK, TOPK]),
                                               ALU.mult))
                        link(dve.tensor_reduce(ia[0:n, x, :], e3, AX.X, ALU.add))
                    link(dve.scalar_tensor_tensor(idx[0:n, t % 2, :], ia[0:n, 0, :], float(NKEY), ia[0:n, 1, :], ALU.mult, ALU.add))
                    dve.wait_ge(s_ge, t + 1)
                    link(dve.tensor_reduce(gs[0:n, 1, :], tv[0:n], AX.X, ALU.add))
                    link(dve.reciprocal(gs[0:n, 0, :], gs[0:n, 1, :]))
                    link(dve.tensor_tensor(gate[0:n, t % 2, :].rearrange("p (h w) -> p h w", h=PKH), tv[0:n],
                                           gs[0:n, 0, :].unsqueeze(2).broadcast_to([n, PKH, TOPK]), ALU.mult), s_idx)

            def gather(t, part):
                it0 = ITERS * part
                done = 2 * (SLOTS // W2 * t + it0)
                with dve.Fori(0, ITERS) as i:
                    for half in range(2):
                        for q in range(half * G, (half + 1) * G):
                            dve.wait_ge(s_u[q], 16 * i + (8 * done + 16))
                            ins = dve.tensor_tensor_reduce(Ur[:, q, :], Ur[:, q, :], x1[:, t % 2, :], 1.0, 0.0, ALU.mult, ALU.add,
                                                           dot[:, q:q + 1])
                        ins.then_inc(s_dot, 1)
                    for half in range(2):
                        hs = slice(half * G, (half + 1) * G)
                        dve.wait_ge(s_gel, 2 * i + (done + half + 1))
                        dve.tensor_tensor(wgt[:, hs], gel[:, hs], gate[:, t % 2, bass.ds(W2 * i + (W2 * it0 + half * G), G)],
                                          ALU.mult).then_inc(s_w, 1)

            def finish(t, n, acc):
                dve.wait_ge(s_acc, t + 1)
                for a in range(2):
                    cs = slice(a * 512, (a + 1) * 512)
                    last = dve.scalar_tensor_tensor(x1[0:n, t % 2, cs], x1[0:n, t % 2, cs], ALPHA, acc[0:n, a, :], ALU.mult, ALU.add,
                                                    accum_out=st[0:n, 5 * a:5 * a + 1])
                link(last, s_res)
                link(norm(x1[0:n, t % 2, :], 2, 3, n), s_y)

            dve.engine_nop().then_inc(s_dot, 1)
            dve.engine_nop().then_inc(s_dot, 1)
            dve.engine_nop().then_inc(s_vu, 1)
            dve.engine_nop().then_inc(s_vu, 1)
            for part in range(PARTS):
                prep(0, part)
            for t in range(NT):
                for part in range(PARTS):
                    gather(t, part)
                    prep(t + 1, part)
                finish(t, P, ps[:, 4 + 2 * (t % 2):6 + 2 * (t % 2), :])
            dve.wait_ge(s_repc, 1)
            for h in range(PKH):
                dve.wait_ge(s_u[h], 16 * (SLOTS // W2 * NT + 1))
                ins = dve.tensor_tensor_reduce(Ur[:, h, :], Ur[:, h, :], xin[:, :], 1.0, 0.0, ALU.mult, ALU.add, dot[:, h:h + 1])
            ins.then_inc(s_dot, 1)
            dve.wait_ge(s_gel, 2 * (SLOTS // W2 * NT) + 1)
            dve.wait_ge(s_rs, 16 * 2 * NB)
            link(dve.tensor_tensor(wgt[:, :], gel[:, :], gtr[:, :], ALU.mult))
            link(dve.tensor_tensor(wsel[:, :, :], wgt[:, :].unsqueeze(2).broadcast_to([P, PKH, NB]),
                                   c("gather").unsqueeze(1).broadcast_to([P, PKH, NB]), ALU.mult), s_ws)
            finish(NT, NB, ps[:, 4:6, :])


class Mem:
    pass


def build(nc, io, upto=9, debug=None):
    root = ExitStack()
    with root:
        m = Mem()
        sb0 = lambda n, s, dt=F32: root.enter_context(nc.sbuf_tensor(n, s, dt))
        m.ps = root.enter_context(nc.psum_tensor("ps", [P, 8, 512], F32))
        tables = [sb0("table_long", TABLES[0].shape)]
        m.params = sb0("params", [P, NPAR])
        m.par = lambda n, i: m.params[:, PAR[n] + i:PAR[n] + i + 1]
        m.c = lambda n: tables[WHERE[n][0]][:, WHERE[n][1]:WHERE[n][1] + WHERE[n][2]]
        m.mixT = sb0("mixT", [P, KT, SEQ + NB])
        m.omka = sb0("omka", [P, HP])
        m.zero = sb0("zero", [1, P])
        mid = ExitStack()
        with mid:
            sb = lambda n, s, dt=F32: mid.enter_context(nc.sbuf_tensor(n, s, dt))
            tables.append(sb("table_short", TABLES[1].shape))
            m.w2a2 = sb("w2a2", [P, RWW])
            m.g2 = sb("g2", [P, RWW])
            m.shift0 = sb("shift0", [P, NCH, NB])
            m.shout = sb("shout", [P, NCH, 1 + NB])
            m.qT = sb("qT", [P, NH, SEQ])
            m.qTs = sb("qTs", [P, NH, NB])
            m.kT = sb("kT", [P, NH, TP])
            m.vtok = sb("vtok", [P, NT + 1, RWW])
            m.vmeta = sb("vmeta", [NMETA, RWW])
            m.qks = sb("qks", [SM, 2, RWW])
            m.ar = sb("ar", [P, HP, 2, TA])
            m.bt = sb("bt", [P, HP, TA])
            m.kt = sb("kt", [P, HP, TA])
            m.rk = sb("rk", [P, HP, TA])
            m.vT = sb("vT", [P, HP, TA])
            m.sg = sb("sg", [P, TA])
            m.eend = sb("eend", [P, HP, 17])
            m.consts = [(tables[0][:, :], io["table0"]), (tables[1][:, :], io["table1"]), (m.params[:, :], io["params"]), (m.w2a2[:, :], io["w2a2"]),
                        (m.g2[:, :], io["g2"]), (m.shift0[:, :, :], io["shift0"])]
            phase_project(nc, io, m)
            if debug:
                debug(nc, m, 1)
            if upto <= 1:
                return
            phase_rwkv(nc, io, m)
            if debug:
                debug(nc, m, 2)
            if upto <= 2:
                return
            phase_attention(nc, io, m)
            if debug:
                debug(nc, m, 3)
            if upto <= 3:
                return
        phase_peer(nc, io, m)


def arrange(x):
    a = {}
    chan = lambda v: np.asarray(v).reshape(-1, P).T
    a["table0"], a["table1"] = TABLES
    a["params"] = np.concatenate([chan(x["mu_shift"][0]), chan(x["w0"][0]), chan(x["a0"][0]), chan(x["k_k"][0]),
                                  chan(x["k_a"][0]), chan(x["r_k"][0])], 1)
    a["w2a2"] = np.concatenate([x["w2_decay"][0], x["a2"][0]], 0)
    a["g2"] = x["g2"][0]
    a["shift0"] = np.asarray(x["state_shift"][0]).reshape(NB, NCH, P).transpose(2, 1, 0)
    a["xT"] = np.concatenate([x["x_prompt"][0], x["x_sample"][:, 0], x["meta_tokens"]], 0).T
    a["w_in"] = x["w_in"][0]
    a["lnx_w"], a["lnx_b"] = x["lnx_w"][0], x["lnx_b"][0]
    a["state"] = np.asarray(x["state_wkv"][0]).reshape(NB, HP, 2, DH, DH).transpose(2, 4, 0, 1, 3).reshape(P, NB, HP, DH)
    a["w_out"], a["pk_wq"] = x["w_out"][0], x["pk_wq"][0]
    a["peer_u"], a["peer_v"] = x["peer_u"][0], x["peer_v"][0]
    for n in ("ln1_w", "ln1_b", "ln2_w", "ln2_b"):
        a[n] = x[n][0]
    a["skT"] = np.asarray(x["pk_subkeys"][0]).transpose(1, 3, 0, 2).reshape(P, PKH, NKEY)
    a["x_tok"] = np.concatenate([x["x_prompt"][0], x["x_sample"][:, 0]], 0)
    a["pages"] = np.asarray(x["page_table"]).reshape(-1)
    a["lams"] = np.stack([x["lam_q1"][0], x["lam_k1"][0], x["lam_q2"][0], x["lam_k2"][0]])
    a["subln_w"] = x["subln_w"][0]
    a["cache_k"] = np.asarray(x["cache_k"][0]).reshape(-1, RWW)
    a["cache_v"] = np.asarray(x["cache_v"][0]).reshape(-1, RWW)
    return {k: np.ascontiguousarray(v) for k, v in a.items()}


_OUTS = {
    "y_out": (SEQ + NB, D), "k_out": (TA, RWW), "v_out": (TA, RWW), "shift_out": (P, NCH, 1 + NB),
    "wkv_p_out": (P, HP, DH), "wkv_s_out": (P, NB, HP, DH),
}


def returned(r):
    y = r["y_out"]
    tokens = lambda a: np.concatenate([a[SEQ + NB:], a[:SEQ]], 0)
    k, v = r["k_out"], r["v_out"]
    sh = r["shift_out"].transpose(2, 1, 0).reshape(1 + NB, RWC)
    wp = r["wkv_p_out"].reshape(2, DH, HP, DH).transpose(2, 0, 3, 1).reshape(1, 1, 2 * HP, DH, DH)
    ws = r["wkv_s_out"].reshape(2, DH, NB, HP, DH).transpose(2, 3, 0, 4, 1).reshape(1, NB, 2 * HP, DH, DH)
    out = (y[None, :SEQ], y[SEQ:, None], tokens(k).reshape(1, 1, TP, NH, 2, DH), tokens(v).reshape(1, 1, TP, NH, DV),
           wp, sh[None, 0:1], k[SEQ:SEQ + NB].reshape(1, NB, 1, NH, 2, DH), v[SEQ:SEQ + NB].reshape(1, NB, 1, NH, DV),
           ws, sh[None, 1:])
    return tuple(np.ascontiguousarray(a) for a in out)


def kernel(**inputs):
    import concourse.bacc as bacc
    from concourse.bass_utils import run_bass_kernel_spmd

    nc = bacc.Bacc("TRN2", target_bir_lowering=False, num_devices=1)
    arrays, io = {}, {}
    for n, a in arrange({k: np.asarray(v) for k, v in inputs.items()}).items():
        arrays[f"in_{n}_dram"] = a
        io[n] = nc.dram_tensor(f"in_{n}_dram", a.shape, mybir.dt.from_np(a.dtype), kind="ExternalInput").ap()
    for n, shape in _OUTS.items():
        io[n] = nc.dram_tensor(f"out_{n}_dram", shape, F32, kind="ExternalOutput").ap()
    build(nc, io)
    r = run_bass_kernel_spmd(nc, [arrays], core_ids=[0])
    return returned({n: r.results[0][f"out_{n}_dram"] for n in _OUTS})
```

```python
import math

import numpy as np
import concourse.bass as bass
from concourse import mybir
from concourse.alu_op_type import AluOpType as ALU
from contextlib import ExitStack

F32 = mybir.dt.float32
I32 = mybir.dt.int32
U32 = mybir.dt.uint32
ACT = mybir.ActivationFunctionType
AX = mybir.AxisListType

P = 128
D = 1024
KT = D // P
NMETA, SEQ, NB = 16, 512, 8
NT = SEQ // P
TP = NMETA + SEQ
TA = TP + NB
SM = NB + NMETA
RWW, RWC = 512, 1792
NCH = RWC // P
HP = 4
DH = 64
NH, DV = 4, 128
PAST, PAGE = 1024, 128
NPG = PAST // PAGE
PKH, NKEY, TOPK = 8, 128, 16
NEXP = NKEY * NKEY
SLOTS = PKH * TOPK
CH = 64
LAM_INIT = 0.8 - 0.6 * math.exp(-0.3 * 0)
ALPHA = 2.0 ** 0.25
BIG = 1.0e30


class Link:

    def __init__(self, eng, own):
        self.eng, self.own, self.n = eng, own, {}

    def __call__(self, ins, sem=None):
        s = sem if sem is not None else self.own
        k = s.name
        self.n[k] = self.n.get(k, 0) + 1
        ins.then_inc(s, 1)
        self.eng.wait_ge(s, self.n[k])


def constant_table():
    t, s = np.arange(P)[:, None], np.arange(P)[None, :]
    same = (t // CH) == (s // CH)
    parts = {}
    parts["ident"] = (t == s)
    strict_up = same & (t < s)
    incl_up = same & (t <= s)
    parts["mask4"] = np.concatenate([strict_up, incl_up, strict_up, incl_up], 1)

    def level(l):
        return (t // (2 * l) == s // (2 * l)) & ((t // l) % 2 == 1) & ((s // l) % 2 == 0)

    parts["first"] = level(1)
    parts["firstT"] = level(1).T
    for l in (2, 4, 8, 16, 32):
        parts[f"lev{l}"] = level(l)
    parts["heads"] = (t // DH == s // DH)
    parts["half"] = (t // DH == np.arange(2)[None, :])
    parts["diag64"] = (t % DH == np.arange(DH)[None, :])
    parts["causal"] = np.where(s > t, -BIG, 0.0)
    parts["one8"] = (t == np.arange(NB)[None, :])
    parts["spread"] = (t == s // TOPK)
    parts["gather"] = (t // TOPK == np.arange(NB)[None, :])
    parts["iota16"] = np.broadcast_to(np.arange(16)[None, :], (P, 16))
    parts["rowid"] = t
    parts["map"] = np.concatenate([t % 2 == 0, t % 2 == 1], 1)
    half = 32
    inv = (np.float32(10000.0) ** (-np.arange(half, dtype=np.float32) / np.float32(half))).astype(np.float32)
    pos = np.zeros((P, NT + 1), np.float32)
    for tt in range(NT):
        pos[:, tt] = NMETA + P * tt + np.arange(P)
    pos[:NB, NT] = PAST
    pos[NB:SM, NT] = np.arange(NMETA)
    ang = pos[:, :, None] * inv[None, None, :]
    c, sn = np.cos(ang), np.sin(ang)
    parts["cos"] = np.concatenate([c, c], 2).reshape(P, -1)
    parts["sin"] = np.concatenate([-sn, sn], 2).reshape(P, -1)
    start = np.ones((P, TA))
    start[:, 0] = 0
    start[:, NMETA:TP:CH] = 0
    start[:, TP:] = 0
    parts["start"] = start
    keep = ("ident", "spread", "gather", "iota16")
    where, tables = {}, []
    for which in (True, False):
        at, here = 0, []
        for n, a in parts.items():
            if (n in keep) == which:
                where[n] = (len(tables), at, a.shape[1])
                at += a.shape[1]
                here.append(np.asarray(a, np.float32))
        tables.append(np.concatenate(here, 1))
    return where, tables


WHERE, TABLES = constant_table()
PAR = {}
_at = 0
for _n, _c in (("mu", NCH), ("w0", HP), ("a0", HP), ("k_k", HP), ("k_a", HP), ("r_k", HP)):
    PAR[_n] = _at
    _at += _c
NPAR = _at


def phase_project(nc, io, m):
    ctx = ExitStack()
    with ctx:
        sb = lambda n, s, dt=F32: ctx.enter_context(nc.sbuf_tensor(n, s, dt))
        sem = lambda n: ctx.enter_context(nc.semaphore(n))
        ps = m.ps
        xT = sb("xT", [P, KT, TA])
        wr = sb("w_ring", [P, 2, KT, 512])
        cols = sb("cols", [P, 2, TA + 1])
        diff = sb("diff", [P, 2, TA])
        rraw = m.ar[:, :, 1, :]
        kraw = m.kt
        xwa = sb("xwa", [P, TA])
        xg = sb("xg", [P, TA])
        kk = sb("kk", [P, TA])
        kk2 = sb("kk2", [P, TA])
        sgm = sb("sgm", [P, TA])
        am = sb("am", [P, TA])
        L = sb("L", [P, TA])
        E = sb("E", [P, TA])
        Ei = sb("Ei", [P, TA])
        Lp = sb("Lp", [P, TA])
        lent = m.mixT[:, :, :].rearrange("p k n -> p (k n)")
        rot = lent[:, 0:1536].rearrange("p (a n) -> p a n", a=3)
        rtmp, rtmp2 = lent[:, 1536:2048], lent[:, 2048:2560]
        c = m.c
        par = m.par

        s_const = sem("s_const")
        s_x = sem("s_x")
        s_w = [sem(f"s_w{i}") for i in range(2)]
        s_item = sem("s_item")
        s_cols = sem("s_cols")
        s_mixed = sem("s_mixed")
        s_rope = sem("s_rope")
        s_val = sem("s_val")
        s_tr = sem("s_tr")
        s_trc = sem("s_trc")
        s_rot_out = [sem(f"s_rot_out{i}") for i in range(3)]
        s_tanh = sem("s_tanh")
        s_sq = sem("s_sq")
        s_lora = sem("s_lora")
        s_sig = sem("s_sig")
        s_ss = sem("s_ss")
        s_rn = sem("s_rn")
        s_L = sem("s_L")
        s_E = sem("s_E")
        s_Eu = sem("s_Eu")
        s_v = sem("s_v")
        s_a = sem("s_a")
        s_out = sem("s_out")

        NG = 7
        GW = [4, 4, 4, 2, 4, 4, 4]
        chan = list(range(NCH))
        done_group = [4, 8, 12, 14, 19, 24, 29]

        block = ctx.enter_context(nc.Block())

        @block.sync
        def _(sp):
            for n in m.consts:
                sp.dma_start(n[0], n[1]).then_inc(s_const, 16)
            sp.dma_start(xT[:, :, :], io["xT"].rearrange("(k p) n -> p k n", p=P)).then_inc(s_x, 16)
            for g in range(NG):
                if g >= 2:
                    sp.wait_ge(s_item, done_group[g - 2])
                w = GW[g] * P
                sp.dma_start(wr[:, g % 2, :, 0:w],
                             io["w_in"][:, g * 512 - (256 if g > 3 else 0):][:, 0:w].rearrange("(k p) n -> p k n", p=P)
                             ).then_inc(s_w[g % 2], 16)
            n_out = 0
            for n in range(10):
                tt = n % 5
                if n >= 5:
                    sp.wait_ge(s_rope, n + 1)
                    if tt < NT:
                        sp.dma_start(io["k_out"][tt * P:(tt + 1) * P, :], rot[:, n % 3, :]).then_inc(s_rot_out[n % 3], 16)
                    else:
                        sp.dma_start(io["k_out"][SEQ:, :], m.qks[0:SM, 1, :]).then_inc(s_out, 16)
                        n_out += 1
            sp.wait_ge(s_val, 4)
            sp.dma_start(io["v_out"][0:SEQ, :].rearrange("(t p) n -> p t n", p=P), m.vtok[:, 0:NT, :]).then_inc(s_out, 16)
            sp.wait_ge(s_val, 5)
            sp.dma_start(io["v_out"][SEQ:, :], m.vtok[0:SM, NT, :]).then_inc(s_out, 16)
            sp.dma_start(m.vmeta[:, :], m.vtok[NB:SM, NT, :]).then_inc(s_out, 16)
            sp.wait_ge(s_mixed, NCH)
            sp.dma_start(io["shift_out"], m.shout[:, :, :]).then_inc(s_out, 16)
            n_out += 4
            sp.wait_ge(s_out, 16 * n_out)
            for i, k in ((0, 1), (1, 1), (2, 2)):
                sp.wait_ge(s_rot_out[i], 16 * sum(1 for n in range(5, 9) if n % 3 == i))

        @block.tensor
        def _(pe):
            pe.wait_ge(s_const, 16 * len(m.consts))
            pe.wait_ge(s_x, 16)

            def arrived(g):
                pe.wait_ge(s_w[g % 2], 16 * (g // 2 + 1))

            def channel_tiles(g):
                arrived(g)
                for mt in range(GW[g]):
                    ct = 4 * g + mt
                    if ct >= 2:
                        pe.wait_ge(s_cols, ct - 1)
                    for k in range(KT):
                        w = wr[:, g % 2, k, mt * P:(mt + 1) * P]
                        pe.matmul(ps[:, ct % 2, :], w, xT[:, k, 0:SEQ], start=(k == 0), stop=(k == KT - 1))
                        mm = pe.matmul(ps[:, 2 + ct % 2, 0:SM], w, xT[:, k, SEQ:TA], start=(k == 0), stop=(k == KT - 1))
                    mm.then_inc(s_item, 1)

            def token_tiles(g):
                arrived(g)
                for tt in range(NT + 1):
                    n = 5 * (g - 4) + tt
                    rows = P if tt < NT else SM
                    if n >= 2:
                        pe.wait_ge(s_rope, min(n - 1, 10))
                        if n - 1 > 10:
                            pe.wait_ge(s_val, n - 11)
                    for k in range(KT):
                        mm = pe.matmul(ps[0:rows, 4 + n % 2, :], xT[:, k, tt * P:tt * P + rows], wr[:, g % 2, k, :],
                                       start=(k == 0), stop=(k == KT - 1))
                    mm.then_inc(s_item, 1)
                    if 1 <= n <= 10:
                        transposes(n - 1)

            def transposes(n):
                rows = P if n % 5 < NT else SM
                src = rot[:, n % 3, :] if n % 5 < NT else m.qks[0:SM, n // 5, :]
                pe.wait_ge(s_rope, n + 1)
                if n >= 2:
                    pe.wait_ge(s_trc, n - 1)
                for h in range(NH):
                    mm = pe.transpose(ps[:, 6 + n % 2, h * P:h * P + rows], src[:, h * P:(h + 1) * P], c("ident")[0:rows, 0:rows])
                mm.then_inc(s_tr, 1)

            def lora(i):
                pe.wait_ge(s_tanh, 1)
                if i >= 1:
                    pe.wait_ge(s_rn, i)
                    pe.wait_ge(s_sig, 2 * i)
                else:
                    pe.wait_ge(s_cols, NCH)
                for a, b in ((0, 512), (512, TA)):
                    pe.matmul(ps[:, a // 512, 0:b - a], m.w2a2[0:DH, i * P:(i + 1) * P], xwa[0:DH, a:b], start=True, stop=True)
                for a, b in ((0, 512), (512, TA)):
                    mm = pe.matmul(ps[:, 2 + a // 512, 0:b - a], m.w2a2[DH:P, i * P:(i + 1) * P], xwa[DH:P, a:b], start=True, stop=True)
                mm.then_inc(s_lora, 1)
                pe.wait_ge(s_sq, i + 1)
                pe.wait_ge(s_sig, 2 * i + 1)
                for a, b in ((0, 512), (512, TA)):
                    mm = pe.matmul(ps[:, a // 512, 0:b - a], c("heads"), kk2[:, a:b], start=True, stop=True)
                mm.then_inc(s_ss, 1)

            for g in range(4):
                channel_tiles(g)
            token_tiles(4)
            lora(0)
            token_tiles(5)
            lora(1)
            token_tiles(6)
            lora(2)
            lora(3)

        @block.scalar
        def _(act):
            link = Link(act, s_a)
            act.wait_ge(s_const, 16 * len(m.consts))
            for ct in range(NCH):
                act.wait_ge(s_item, ct + 1)
                if ct == 0:
                    act.wait_ge(s_v, 1)
                if ct >= 2:
                    act.wait_ge(s_mixed, ct - 1)
                buf = cols[:, ct % 2, :]
                act.activation(buf[:, 1 + NMETA:1 + TP], ps[:, ct % 2, :], ACT.Copy)
                act.activation(buf[:, 1:1 + NMETA], ps[:, 2 + ct % 2, NB:SM], ACT.Copy)
                act.activation(buf[:, 1 + TP:1 + TA], ps[:, 2 + ct % 2, 0:NB], ACT.Copy).then_inc(s_cols, 1)
            act.wait_ge(s_mixed, NCH)
            act.activation(xwa[0:DH, :], xwa[0:DH, :], ACT.Tanh).then_inc(s_tanh, 1)
            act.activation(m.sg[:, :], xg[:, :], ACT.Sigmoid).then_inc(s_tanh, 1)

            def evac_transposes(n):
                act.wait_ge(s_tr, n + 1)
                tt = n % 5
                src = ps[:, 6 + n % 2, :].rearrange("p (h t) -> p h t", h=NH)
                if n < 4:
                    ins = act.activation(m.qT[:, :, tt * P:(tt + 1) * P], src, ACT.Copy)
                elif n == 4:
                    ins = act.activation(m.qTs[:, :, :], src[:, :, 0:NB], ACT.Copy)
                elif tt < NT:
                    ins = act.activation(m.kT[:, :, NMETA + tt * P:NMETA + (tt + 1) * P], src, ACT.Copy)
                else:
                    ins = act.activation(m.kT[:, :, 0:NMETA], src[:, :, NB:SM], ACT.Copy)
                ins.then_inc(s_trc, 1)

            def factors(i):
                act.wait_ge(s_lora, i + 1)
                if i >= 1:
                    act.wait_ge(s_Eu, 2 * i)
                z = ps[:, 0:2, :].rearrange("p a b -> p (a b)")[:, 0:TA]
                za = ps[:, 2:4, :].rearrange("p a b -> p (a b)")[:, 0:TA]
                act.activation(sgm[:, :], z, ACT.Sigmoid, bias=par("w0", i)).then_inc(s_sig, 1)
                act.activation(am[:, :], za, ACT.Sigmoid, bias=par("a0", i)).then_inc(s_sig, 1)
                act.wait_ge(s_ss, i + 1)
                act.activation(kk2[:, :], z, ACT.Sqrt).then_inc(s_rn, 1)
                act.wait_ge(s_L, i + 1)
                act.activation(E[:, :], L[:, :], ACT.Exp)
                act.activation(Ei[:, :], L[:, :], ACT.Exp, scale=-1.0)
                act.activation(Lp[:, :], Lp[:, :], ACT.Exp).then_inc(s_E, 1)

            for n in range(4):
                evac_transposes(n)
            factors(0)
            for n in range(4, 9):
                evac_transposes(n)
            factors(1)
            for tt in range(NT + 1):
                rows = P if tt < NT else SM
                act.wait_ge(s_item, 24 + tt + 1)
                act.activation(m.vtok[0:rows, tt, :], ps[0:rows, 4 + tt % 2, :], ACT.Copy).then_inc(s_val, 1)
                if tt == 0:
                    evac_transposes(9)
            factors(2)
            factors(3)

        @block.vector
        def _(dve):
            link = Link(dve, s_v)
            link(dve.memset(cols[:, :, 0:1], 0.0))
            link(dve.memset(m.zero[:, :], 0.0))
            dve.wait_ge(s_const, 16 * len(m.consts))
            link(dve.tensor_scalar(m.omka[:, :], m.params[:, PAR["k_a"]:PAR["k_a"] + HP], -1.0, 1.0, ALU.mult, ALU.add))
            dests = [rraw[:, i, :] for i in range(HP)] + [kraw[:, i, :] for i in range(HP)] + \
                    [m.vT[:, i, :] for i in range(HP)] + [xwa[:, :], xg[:, :]]
            for ct in range(NCH):
                dve.wait_ge(s_cols, ct + 1)
                buf, d = cols[:, ct % 2, :], diff[:, ct % 2, :]
                dve.tensor_tensor(d[:, 0:TP], buf[:, 0:TP], buf[:, 1:1 + TP], ALU.subtract)
                dve.tensor_copy(m.shout[:, ct, :], buf[:, TP:1 + TA])
                link(dve.tensor_tensor(d[:, TP:TA], m.shift0[:, ct, :], buf[:, 1 + TP:1 + TA], ALU.subtract))
                link(dve.scalar_tensor_tensor(dests[ct], d, par("mu", ct), buf[:, 1:1 + TA], ALU.mult, ALU.add), s_mixed)

            def rope(n):
                tt = n % 5
                rows = P if tt < NT else SM
                dve.wait_ge(s_item, 14 + n + 1)
                if n >= 3:
                    dve.wait_ge(s_tr, n - 2)
                    if n - 3 >= 5 and (n - 3) % 5 < NT:
                        dve.wait_ge(s_rot_out[n % 3], 16 * sum(1 for q in range(5, n - 2) if q % 3 == n % 3 and q % 5 < NT))
                x = ps[0:rows, 4 + n % 2, :].rearrange("p (g f) -> p g f", f=DH)
                out = rot[:, n % 3, :] if tt < NT else m.qks[0:SM, n // 5, :]
                cs = c("cos")[0:rows, tt * DH:(tt + 1) * DH].unsqueeze(1).broadcast_to([rows, 8, DH])
                sn = c("sin")[0:rows, tt * DH:(tt + 1) * DH].unsqueeze(1).broadcast_to([rows, 8, DH])
                t = rtmp[0:rows, :].rearrange("p (g f) -> p g f", f=DH)
                u = rtmp2[0:rows, :].rearrange("p (g f) -> p g f", f=DH)
                dve.tensor_tensor(t, x, cs, ALU.mult)
                dve.tensor_tensor(u[:, :, 0:32], x[:, :, 32:64], sn[:, :, 0:32], ALU.mult)
                link(dve.tensor_tensor(u[:, :, 32:64], x[:, :, 0:32], sn[:, :, 32:64], ALU.mult))
                link(dve.tensor_tensor(out, rtmp[0:rows, :], rtmp2[0:rows, :], ALU.add), s_rope)

            def squares(i):
                if i >= 1:
                    dve.wait_ge(s_ss, i)
                link(dve.tensor_scalar(kk[:, :], kraw[:, i, :], par("k_k", i), None, ALU.mult))
                link(dve.tensor_tensor(kk2[:, :], kk[:, :], kk[:, :], ALU.mult), s_sq)

            def factors(i):
                dve.wait_ge(s_sig, 2 * i + 2)
                link(dve.tensor_scalar(sgm[:, :], sgm[:, :], -math.exp(-0.5), None, ALU.mult))
                link(dve.tensor_tensor_scan(L[:, :], c("start"), sgm[:, :], 0.0, ALU.mult, ALU.add))
                link(dve.tensor_tensor(Lp[:, :], L[:, :], sgm[:, :], ALU.subtract), s_L)
                link(dve.tensor_scalar(sgm[:, :], am[:, :], par("k_a", i), m.omka[:, i:i + 1], ALU.mult, ALU.add))
                link(dve.tensor_tensor(kraw[:, i, :], kraw[:, i, :], sgm[:, :], ALU.mult), s_Eu)
                dve.wait_ge(s_rn, i + 1)
                link(dve.tensor_scalar(kk2[:, :], kk2[:, :], 1e-12, None, ALU.max))
                link(dve.reciprocal(kk2[:, :], kk2[:, :]))
                link(dve.tensor_tensor(kk[:, :], kk[:, :], kk2[:, :], ALU.mult))
                dve.wait_ge(s_E, i + 1)
                link(dve.scalar_tensor_tensor(m.rk[:, i, :], rraw[:, i, :], par("r_k", i), kraw[:, i, :], ALU.mult, ALU.mult))
                dve.tensor_tensor(m.ar[:, i, 1, :], rraw[:, i, :], E[:, :], ALU.mult)
                dve.scalar_tensor_tensor(m.ar[:, i, 0, :], kk[:, :], -1.0, Lp[:, :], ALU.mult, ALU.mult)
                dve.tensor_tensor(m.kt[:, i, :], kraw[:, i, :], Ei[:, :], ALU.mult)
                dve.tensor_copy(m.eend[:, i, 0:9], E[:, NMETA - 1:TP:CH])
                dve.tensor_copy(m.eend[:, i, 9:17], E[:, TP:TA])
                link(dve.tensor_tensor(am[:, :], kk[:, :], am[:, :], ALU.mult))
                link(dve.tensor_tensor(m.bt[:, i, :], am[:, :], Ei[:, :], ALU.mult), s_Eu)

            for n in range(5):
                rope(n)
            squares(0)
            factors(0)
            for n in range(5, 10):
                rope(n)
            squares(1)
            factors(1)
            for i in (2, 3):
                squares(i)
                factors(i)


def phase_rwkv(nc, io, m):
    ctx = ExitStack()
    with ctx:
        sb = lambda n, s, dt=F32: ctx.enter_context(nc.sbuf_tensor(n, s, dt))
        sem = lambda n: ctx.enter_context(nc.semaphore("r_" + n))
        ps, c = m.ps, m.c
        tok = sb("tok", [P, 2, 4, RWW])
        msk = sb("msk", [P, 8, 4, P])
        X = sb("X", [P, 2, HP, P])
        XT = sb("XT", [P, 2, HP, P])
        T1 = sb("T1", [P, 2, HP, P])
        AV = sb("AV", [P, RWW])
        U0 = sb("U0", [P, RWW])
        U = sb("U", [P, RWW])
        WT = sb("WT", [P, HP, P])
        St = sb("St", [P, 10, HP, DH])
        stmp = sb("stmp", [P, HP, DH])
        y = sb("y", [P, RWW])
        sq = sb("sq", [P, RWW])
        stat = sb("stat", [P, 4, 8])
        S0 = sb("S0", [P, NB, HP, DH])
        y2 = msk[0:2, 0:4].rearrange("p a x t -> p (a x t)")
        w1 = msk[:, 4:8].rearrange("p a x t -> p (a x t)").rearrange("p (b i v) -> p b i v", b=NB, i=HP)
        lnw = sb("lnxw", [P, RWW])
        lnb = sb("lnxb", [P, RWW])

        s_ld, s_st = sem("ld"), sem("st")
        s_tr, s_trc = sem("tr"), sem("trc")
        s_A, s_Am = sem("A"), sem("Am")
        s_A0, s_X = sem("A0"), sem("X")
        s_XT0 = sem("XT0")
        s_T, s_Tc, s_XX = sem("T"), sem("Tc"), sem("XX")
        s_AV, s_AVc, s_UW, s_UWc = sem("AV"), sem("AVc"), sem("UW"), sem("UWc")
        s_U, s_Uc, s_N, s_S = sem("U"), sem("Uc"), sem("N"), sem("S")
        s_Y, s_yc, s_var, s_rs = sem("Y"), sem("yc"), sem("var"), sem("rs")
        s_mix, s_mt, s_mtc = sem("mix"), sem("mt"), sem("mtc")
        s_sp, s_sc = sem("sp"), sem("sc")
        s_sr = sem("sr")
        s_y2, s_y2d = sem("y2"), sem("y2d")
        s_v, s_a, s_g = sem("v"), sem("a"), sem("g")

        tiles = [(0, NMETA, (2, 4, 8))] + [(NMETA + P * t, P, (2, 4, 8, 16, 32)) for t in range(NT)]
        NTL = len(tiles)
        levels_before = [sum(len(t[2]) for t in tiles[:i]) for i in range(NTL)]

        block = ctx.enter_context(nc.Block())

        @block.sync
        def _(sp):
            sp.dma_start(lnw[:, :], io["lnx_w"].partition_broadcast(P)).then_inc(s_ld, 16)
            sp.dma_start(lnb[:, :], io["lnx_b"].partition_broadcast(P)).then_inc(s_ld, 16)
            sp.dma_start(S0[:, :, :, :], io["state"]).then_inc(s_ld, 16)
            sp.wait_ge(s_y2, 1)
            for h2 in range(2):
                for b in range(NB):
                    sp.dma_start(y[b:b + 1, :].rearrange("b (i h v) -> b i h v", h=2, v=DH)[:, :, h2, :],
                                 y2[h2:h2 + 1, :].rearrange("o (b i v) -> o b i v", b=NB, v=DH)[:, b]).then_inc(s_y2d, 16)
            sp.wait_ge(s_sc, 3)
            sp.dma_start(io["wkv_s_out"], S0[:, :, :, :]).then_inc(s_st, 16)
            sp.wait_ge(s_S, 9)
            sp.dma_start(io["wkv_p_out"], St[:, 9, :, :]).then_inc(s_st, 16)
            sp.wait_ge(s_st, 32)

        @block.tensor
        def _(pe):
            def prepare(ti):
                p0, n, levels = tiles[ti]
                span = slice(p0, p0 + n)
                for q, src in enumerate((m.ar[:, :, 0], m.bt, m.kt, m.vT)):
                    if 4 * ti + q >= 2:
                        pe.wait_ge(s_trc, 4 * ti + q - 1)
                    if ti >= 1:
                        pe.wait_ge(s_UWc, 2 * ti)
                    for i in range(HP):
                        mm = pe.transpose(ps[0:n, q % 2, i * P:(i + 1) * P], src[:, i, span], c("ident"))
                    mm.then_inc(s_tr, 1)
                pe.wait_ge(s_trc, 4 * ti + 4)
                for hd in range(8):
                    q, i = hd // 4, hd % 4
                    rows = slice(q * DH, (q + 1) * DH)
                    j = 8 * ti + hd
                    if hd >= 2:
                        pe.wait_ge(s_Am, j - 1)
                    for w, src in enumerate((m.bt, m.kt)):
                        mm = pe.matmul(ps[0:n, hd % 2, w * 2 * n:(w + 1) * 2 * n].rearrange("s (x t) -> s x t", x=2),
                                       src[rows, i, span], m.ar[rows, i, :, span], start=True, stop=True)
                    mm.then_inc(s_A, 1)
                for q in range(2):
                    rows = slice(q * DH, (q + 1) * DH)
                    if ti >= 1:
                        pe.wait_ge(s_yc, ti)
                    for i in range(HP):
                        mm = pe.matmul(ps[0:n, 4 + q, i * n:(i + 1) * n], m.ar[rows, i, 0, span], m.bt[rows, i, span],
                                       start=True, stop=True)
                    mm.then_inc(s_A0, 1)
                for l in range(len(levels)):
                    at = 2 * (levels_before[ti] + l)
                    for q in range(2):
                        pe.wait_ge(s_X, at + q + 1 + 2 * ti)
                        if l == 0:
                            pe.wait_ge(s_XT0, 2 * ti + q + 1)
                            pe.wait_ge(s_Am, 8 * ti + 8)
                        for i in range(HP):
                            mm = pe.matmul(ps[0:n, 2 + q, i * n:(i + 1) * n], msk[0:n, 4 * q + i, 0, 0:n], X[0:n, q, i, 0:n],
                                           start=True, stop=True)
                        mm.then_inc(s_T, 1)
                    for q in range(2):
                        pe.wait_ge(s_Tc, at + q + 1)
                        for i in range(HP):
                            if l < len(levels) - 1:
                                pe.matmul(ps[0:n, 4 + q, i * n:(i + 1) * n], XT[0:n, q, i, 0:n], T1[0:n, q, i, 0:n],
                                          start=True, stop=True)
                            mm = pe.matmul(ps[0:n, 6 + q, i * n:(i + 1) * n], T1[0:n, q, i, 0:n], XT[0:n, q, i, 0:n],
                                           start=True, stop=True)
                        mm.then_inc(s_XX, 1)
                for hd in range(8):
                    h = 2 * (hd % 4) + hd // 4
                    mm = pe.matmul(ps[0:n, 0, h * DH:(h + 1) * DH], msk[0:n, hd, 2, 0:n], tok[0:n, ti % 2, 3, h * DH:(h + 1) * DH],
                                   start=True, stop=True)
                mm.then_inc(s_AV, 1)
                pe.wait_ge(s_X, 2 * (levels_before[ti] + len(levels)) + 2 * ti + 2)
                pe.wait_ge(s_AVc, ti + 1)
                for hd in range(8):
                    q, i = hd // 4, hd % 4
                    h = 2 * i + q
                    mm = pe.matmul(ps[0:n, 1, h * DH:(h + 1) * DH], XT[0:n, q, i, 0:n], AV[0:n, h * DH:(h + 1) * DH],
                                   start=True, stop=True)
                    if ti > 0:
                        mm = pe.matmul(ps[q * DH:(q + 1) * DH, 2, i * P:(i + 1) * P], tok[0:n, ti % 2, 0, h * DH:(h + 1) * DH],
                                       XT[0:n, q, i, 0:n], start=True, stop=True)
                mm.then_inc(s_UW, 1)

            def chain(ti):
                pe.wait_ge(s_UWc, 2 * ti + 2)
                for ch in range(2 if ti else 1):
                    n = CH if ti else NMETA
                    k = 2 * ti - 1 + ch if ti else 0
                    r = slice(ch * CH, ch * CH + n)
                    if ti:
                        pe.wait_ge(s_S, k)
                        for hd in range(8):
                            q, i = hd // 4, hd % 4
                            rows = slice(q * DH, (q + 1) * DH)
                            mm = pe.matmul(ps[r, 2 + q, i * DH:(i + 1) * DH], WT[rows, i, r], St[rows, k, i, :],
                                           start=True, stop=True)
                        mm.then_inc(s_U, 1)
                        pe.wait_ge(s_Uc, k)
                    u = U if ti else U0
                    for hd in range(8):
                        q, i = hd // 4, hd % 4
                        h = 2 * i + q
                        hs = slice(h * DH, (h + 1) * DH)
                        out = ps[q * DH:(q + 1) * DH, 4, i * DH:(i + 1) * DH]
                        pe.matmul(out, tok[r, ti % 2, 1, hs], u[r, hs], start=True, stop=False)
                        mm = pe.matmul(out, tok[r, ti % 2, 2, hs], tok[r, ti % 2, 3, hs], start=False, stop=True)
                    mm.then_inc(s_N, 1)

            def outputs(ti):
                p0 = tiles[ti][0]
                for hd in range(8):
                    q, i = hd // 4, hd % 4
                    h = 2 * i + q
                    hs = slice(h * DH, (h + 1) * DH)
                    rows = slice(q * DH, (q + 1) * DH)
                    for ch in range(2):
                        k = 2 * ti - 1 + ch
                        pe.matmul(ps[ch * CH:(ch + 1) * CH, 6 + q, i * DH:(i + 1) * DH],
                                  m.ar[rows, i, 1, p0 + ch * CH:p0 + (ch + 1) * CH], St[rows, k, i, :],
                                  start=True, stop=False, skip_group_check=True)
                    pe.matmul(ps[:, 6 + q, i * DH:(i + 1) * DH], msk[:, hd, 3, :], tok[:, ti % 2, 3, hs],
                              start=False, stop=False, skip_group_check=True)
                    pe.matmul(ps[:, 6 + q, i * DH:(i + 1) * DH], msk[:, hd, 1, :], U[:, hs],
                              start=False, stop=True, skip_group_check=True)
                gate(slice(p0, p0 + P), P)

            def gate(span, n):
                pe.matmul(ps[0:n, 0, :], m.sg[:, span], m.g2[:, :], start=True, stop=True)
                for i in range(HP):
                    mm = pe.matmul(ps[0:n, 1, 2 * i:2 * i + 2], m.rk[:, i, span], c("half"), start=True, stop=True)
                mm.then_inc(s_Y, 1)

            def transpose_mix(ti, n):
                pe.wait_ge(s_mix, ti + 1)
                for i in range(HP):
                    mm = pe.transpose(ps[:, 2, i * P:i * P + n], y[0:n, i * P:(i + 1) * P], c("ident")[0:n, 0:n])
                mm.then_inc(s_mt, 1)

            for ti in range(NTL):
                prepare(ti)
                chain(ti)
                if ti:
                    outputs(ti)
                    transpose_mix(ti - 1, P)
                    pe.wait_ge(s_mtc, ti)

            def sums(step, src):
                pe.wait_ge(s_sr, step)
                for j in range(4):
                    mm = pe.matmul(ps[:, 4 + j, :], c("heads"), src[:, 2 * j:2 * j + 2].rearrange("p a i v -> p (a i v)"),
                                   start=True, stop=True)
                mm.then_inc(s_sp, 1)

            sums(1, w1)
            pe.wait_ge(s_sc, 1)
            sums(2, w1)
            pe.wait_ge(s_sc, 2)
            pe.wait_ge(s_sr, 3)
            for j in range(4):
                mm = pe.matmul(ps[0:2, 4 + j, :], c("half"), w1[:, 2 * j:2 * j + 2].rearrange("p a i v -> p (a i v)"),
                               start=True, stop=True)
            mm.then_inc(s_sp, 1)
            for i in range(HP):
                mm = pe.transpose(ps[0:NB, 3, i * P:(i + 1) * P], m.vT[:, i, TP:TA], c("ident"))
            mm.then_inc(s_sp, 1)
            gate(slice(TP, TA), NB)
            transpose_mix(NT, NB)

        @block.scalar
        def _(act):
            for ti in range(NTL):
                n = tiles[ti][1]
                for q in range(4):
                    act.wait_ge(s_tr, 4 * ti + q + 1)
                    if ti >= 2:
                        act.wait_ge(s_Y, ti - 1)
                    act.activation(tok[0:n, ti % 2, q, :], ps[0:n, q % 2, :], ACT.Copy).then_inc(s_trc, 1)
                act.wait_ge(s_AV, ti + 1)
                act.activation(AV[0:n, :], ps[0:n, 0, :], ACT.Copy).then_inc(s_AVc, 1)
                act.wait_ge(s_UW, ti + 1)
                if ti:
                    act.activation(WT[:, :, :], ps[:, 2, :].rearrange("p (i t) -> p i t", i=HP), ACT.Copy).then_inc(s_UWc, 1)
                    act.wait_ge(s_var, ti)
                    act.activation(stat[:, 2, :], stat[:, 1, :], ACT.Sqrt).then_inc(s_rs, 1)
                    act.wait_ge(s_mt, ti)
                    act.activation(m.mixT[:, 0:HP, (ti - 1) * P:ti * P], ps[:, 2, :].rearrange("p (i t) -> p i t", i=HP),
                                   ACT.Copy).then_inc(s_mtc, 1)
                else:
                    act.activation(stmp[:, 0, 0:1], c("ident")[:, 0:1], ACT.Copy).then_inc(s_UWc, 1)
            act.wait_ge(s_sp, 3)
            act.activation(y2, ps[0:2, 4:8, :].rearrange("p a b -> p (a b)"), ACT.Copy).then_inc(s_y2, 1)
            act.wait_ge(s_var, NT + 1)
            act.activation(stat[0:NB, 2, :], stat[0:NB, 1, :], ACT.Sqrt).then_inc(s_rs, 1)
            act.wait_ge(s_mt, NT + 1)
            act.activation(m.mixT[:, 0:HP, SEQ:SEQ + NB], ps[:, 2, :].rearrange("p (i t) -> p i t", i=HP)[:, :, 0:NB],
                           ACT.Copy).then_inc(s_mtc, 1)

        @block.gpsimd
        def _(pool):
            for ti in range(NTL):
                n = tiles[ti][1]
                for q in range(2):
                    pool.wait_ge(s_Am, 8 * ti + 4 * q + 4)
                    if ti:
                        pool.wait_ge(s_UW, ti)
                    link_n = 4 * ti + 2 * q
                    pool.tensor_tensor(XT[0:n, q, :, 0:n], msk[0:n, 4 * q:4 * q + 4, 0, 0:n],
                                       c("firstT")[0:n, 0:n].unsqueeze(1).broadcast_to([n, 4, n]), ALU.mult).then_inc(s_g, 1)
                    pool.wait_ge(s_g, 2 * ti + q + 1)
                    pool.tensor_tensor(XT[0:n, q, :, 0:n], XT[0:n, q, :, 0:n],
                                       c("ident")[0:n, 0:n].unsqueeze(1).broadcast_to([n, 4, n]), ALU.add).then_inc(s_XT0, 1)

        @block.vector
        def _(dve):
            link = Link(dve, s_v)
            dve.wait_ge(s_ld, 48)

            def four(t):
                return t.unsqueeze(1).broadcast_to([t.shape[0], HP, t.shape[1]])

            def prepare(ti):
                p0, n, levels = tiles[ti]
                for hd in range(8):
                    dve.wait_ge(s_A, 8 * ti + hd + 1)
                    dve.tensor_tensor(msk[0:n, hd, :, 0:n], ps[0:n, hd % 2, 0:4 * n].rearrange("s (x t) -> s x t", x=4),
                                      c("mask4")[0:n].rearrange("s (x t) -> s x t", x=4)[:, :, 0:n], ALU.mult).then_inc(s_Am, 1)
                for q in range(2):
                    dve.wait_ge(s_A0, 2 * ti + q + 1)
                    link(dve.tensor_tensor(X[0:n, q, :, 0:n], ps[0:n, 4 + q, 0:4 * n].rearrange("s (x t) -> s x t", x=4),
                                           four(c("first")[0:n, 0:n]), ALU.mult))
                    link(dve.tensor_tensor(X[0:n, q, :, 0:n], X[0:n, q, :, 0:n], four(c("ident")[0:n, 0:n]), ALU.add), s_X)
                for l, lev in enumerate(levels):
                    at = 2 * (levels_before[ti] + l)
                    for q in range(2):
                        dve.wait_ge(s_T, at + q + 1)
                        link(dve.tensor_tensor(T1[0:n, q, :, 0:n], ps[0:n, 2 + q, 0:4 * n].rearrange("s (x t) -> s x t", x=4),
                                               four(c(f"lev{lev}")[0:n, 0:n]), ALU.mult), s_Tc)
                    for q in range(2):
                        dve.wait_ge(s_XX, at + q + 1)
                        if l < len(levels) - 1:
                            dve.tensor_tensor(X[0:n, q, :, 0:n], ps[0:n, 4 + q, 0:4 * n].rearrange("s (x t) -> s x t", x=4),
                                              X[0:n, q, :, 0:n], ALU.add)
                        link(dve.tensor_tensor(XT[0:n, q, :, 0:n], ps[0:n, 6 + q, 0:4 * n].rearrange("s (x t) -> s x t", x=4),
                                               XT[0:n, q, :, 0:n], ALU.add), s_X)
                dve.wait_ge(s_UW, ti + 1)
                link(dve.tensor_copy(U0[0:n, :], ps[0:n, 1, :]), s_UWc)

            def chain(ti):
                for ch in range(2 if ti else 1):
                    k = 2 * ti - 1 + ch if ti else 0
                    r = slice(ch * CH, (ch + 1) * CH)
                    if ti:
                        dve.wait_ge(s_U, k)
                        view = lambda t: t[r, :].rearrange("s (i h v) -> s h i v", h=2, v=DH)
                        link(dve.tensor_tensor(view(U), ps[r, 2:4, 0:HP * DH].rearrange("s h (i v) -> s h i v", i=HP),
                                               view(U0), ALU.add), s_Uc)
                    dve.wait_ge(s_N, k + 1)
                    new = ps[:, 4, 0:HP * DH].rearrange("p (i v) -> p i v", i=HP)
                    if ti:
                        link(dve.tensor_tensor(stmp[:, :, :], new, St[:, k, :, :], ALU.add))
                        new = stmp[:, :, :]
                    link(dve.tensor_tensor(St[:, k + 1, :, :], new, m.eend[:, :, k:k + 1].broadcast_to([P, HP, DH]), ALU.mult), s_S)

            def finish(ti, n, vals):
                y3, sq3 = (t[0:n, :].rearrange("s (h v) -> s h v", v=DH) for t in (y, sq))
                per = lambda j: stat[0:n, j, :].unsqueeze(2).broadcast_to([n, 8, DH])
                link(dve.tensor_reduce(stat[0:n, 0, :], y3, AX.X, ALU.add))
                link(dve.tensor_scalar(stat[0:n, 0, :], stat[0:n, 0, :], 1.0 / DH, None, ALU.mult))
                link(dve.tensor_tensor(y3, y3, per(0), ALU.subtract))
                link(dve.tensor_tensor(sq[0:n, :], y[0:n, :], y[0:n, :], ALU.mult))
                link(dve.tensor_reduce(stat[0:n, 1, :], sq3, AX.X, ALU.add))
                link(dve.tensor_scalar(stat[0:n, 1, :], stat[0:n, 1, :], 1.0 / DH, 64e-5, ALU.mult, ALU.add), s_var)
                dve.wait_ge(s_rs, ti + 1)
                link(dve.reciprocal(stat[0:n, 3, :], stat[0:n, 2, :]))
                link(dve.tensor_tensor(y3, y3, per(3), ALU.mult))
                link(dve.tensor_tensor(y[0:n, :], y[0:n, :], lnw[0:n, :], ALU.mult))
                link(dve.tensor_tensor(y[0:n, :], y[0:n, :], lnb[0:n, :], ALU.add))
                dve.wait_ge(s_Y, ti + 1)
                link(dve.tensor_copy(stat[0:n, 0, :], ps[0:n, 1, 0:8]))
                link(dve.tensor_tensor(sq3, vals, per(0), ALU.mult))
                link(dve.tensor_tensor(y[0:n, :], y[0:n, :], sq[0:n, :], ALU.add))
                link(dve.tensor_tensor(y[0:n, :], y[0:n, :], ps[0:n, 0, :], ALU.mult), s_mix)

            for ti in range(NTL):
                prepare(ti)
                chain(ti)
                if ti:
                    dve.wait_ge(s_Y, ti)
                    if ti >= 2:
                        dve.wait_ge(s_mt, ti - 1)
                    link(dve.tensor_copy(y[:, :].rearrange("s (i h v) -> s h i v", h=2, v=DH),
                                         ps[:, 6:8, 0:HP * DH].rearrange("s h (i v) -> s h i v", i=HP)), s_yc)
                    finish(ti - 1, P, tok[:, ti % 2, 3, :].rearrange("s (h v) -> s h v", v=DH))
                else:
                    link(dve.memset(stat[:, :, :], 0.0), s_yc)

            def over_v(t):
                return t.rearrange("p i b -> p b i").unsqueeze(3).broadcast_to([P, NB, HP, DH])

            def halves(f):
                for b in range(NB):
                    last = f(b)
                return last

            def col(t, b):
                return t[:, :, b:b + 1].broadcast_to([P, HP, DH])

            al, rr = m.ar[:, :, 0, TP:TA], m.ar[:, :, 1, TP:TA]
            bb, kk, vv = m.bt[:, :, TP:TA], m.kt[:, :, TP:TA], m.vT[:, :, TP:TA]
            dve.wait_ge(s_mt, NT)
            link(halves(lambda b: dve.tensor_tensor(w1[:, b], S0[:, b], col(al, b), ALU.mult)), s_sr)
            dve.wait_ge(s_sp, 1)
            psv = lambda b: ps[:, 4 + b // 2, (b % 2) * HP * DH:(b % 2 + 1) * HP * DH].rearrange("p (i v) -> p i v", i=HP)
            link(halves(lambda b: dve.tensor_tensor(w1[:, b], psv(b), col(bb, b), ALU.mult)))
            link(halves(lambda b: dve.tensor_tensor(S0[:, b], S0[:, b], w1[:, b], ALU.add)), s_sc)
            diag = c("diag64").unsqueeze(1).broadcast_to([P, HP, DH])
            link(halves(lambda b: dve.tensor_tensor(w1[:, b], diag, col(vv, b), ALU.mult)), s_sr)
            dve.wait_ge(s_sp, 2)
            link(halves(lambda b: dve.tensor_tensor(w1[:, b], psv(b), col(kk, b), ALU.mult)), s_sc)
            link(halves(lambda b: dve.tensor_tensor(S0[:, b], S0[:, b], w1[:, b], ALU.add)))
            link(halves(lambda b: dve.tensor_tensor(w1[:, b], S0[:, b], col(rr, b), ALU.mult)), s_sr)
            link(halves(lambda b: dve.tensor_tensor(S0[:, b], S0[:, b], col(m.eend[:, :, 9:17], b), ALU.mult)), s_sc)
            dve.wait_ge(s_sp, 4)
            link(dve.tensor_copy(U0[0:NB, :], ps[0:NB, 3, :]))
            dve.wait_ge(s_y2d, 16 * 2 * NB)
            finish(NT, NB, U0[0:NB, :].rearrange("s (h v) -> s h v", v=DH))


def phase_attention(nc, io, m):
    ctx = ExitStack()
    with ctx:
        sb = lambda n, s, dt=F32: ctx.enter_context(nc.sbuf_tensor("t_" + n, s, dt))
        sem = lambda n: ctx.enter_context(nc.semaphore("t_" + n))
        ps, c = m.ps, m.c
        RING = 3
        SCALE = DH ** -0.5
        ring = sb("ring", [P, RING, NPG + 1, RWW])
        pt = sb("pt", [P, NB * NPG], I32)
        idx = sb("idx", [P, NB * NPG], I32)
        lam4 = sb("lam4", [P, 4, DH])
        lamj = sb("lamj", [P, DH])
        lam2 = sb("lam2", [P, 2])
        nlam = sb("nlam", [P, 1])
        subw = sb("subw", [P, RWW])
        pr = sb("pr", [P, 2, TP])
        att = sb("att", [P, TP])
        attT = sb("attT", [P, NT + 1, P])
        mx = sb("mx", [P, 2])
        Z = sb("Z", [P, 2])
        rz = sb("rz", [P, 2])
        o = sb("o", [P, RWW])
        osq = sb("osq", [P, RWW])
        ost = sb("ost", [P, 3, NH])
        sc = sb("sc", [P, NPG + 1, NB * 8])
        PT = sb("PT", [NB * 8, PAST + 1])
        sst = sb("sst", [NB * 8, 8])
        attS = sb("attS", [P, NPG + 1, NB * NH])
        oT = sb("oT", [P, NH * NB])

        s_ld = sem("ld")
        s_k = [sem(f"k{i}") for i in range(RING)]
        s_kn = [sem(f"kn{i}") for i in range(RING)]
        s_ix = sem("ix")
        s_use = sem("use")
        s_lam, s_lame, s_lamd = sem("lam"), sem("lame"), sem("lamd")
        s_sc, s_mx, s_ex = sem("sc"), sem("mx"), sem("ex")
        s_at, s_tr, s_trc, s_pv = sem("at"), sem("tr"), sem("trc"), sem("pv")
        s_oc, s_ms, s_rs, s_on, s_ot, s_otc = sem("oc"), sem("ms"), sem("rs"), sem("on"), sem("ot"), sem("otc")
        s_qb, s_qbu = sem("qb"), sem("qbu")
        s_ss, s_st, s_smx, s_sex, s_sP, s_sT, s_sA, s_so, s_soc = (sem(n) for n in
            ("ss", "st2", "smx", "sex", "sP", "sT", "sA", "so", "soc"))
        s_v, s_a = sem("v"), sem("a")
        NQ = NT * NH
        width = lambda t: NMETA + P * (t + 1)

        block = ctx.enter_context(nc.Block())

        @block.sync
        def _(sp):
            sp.dma_start(pt[:, :], io["pages"].partition_broadcast(P)).then_inc(s_ld, 16)
            sp.dma_start(lam4[:, :, :], io["lams"].partition_broadcast(P)).then_inc(s_ld, 16)
            sp.dma_start(subw[:, :], io["subln_w"].partition_broadcast(P)).then_inc(s_ld, 16)
            sp.dma_start(m.w_out[:, :, :], io["w_out"].rearrange("(k p) n -> p k n", p=P)).then_inc(m.s_wout, 16)
            for j in range(2 * NB):
                b = j % NB
                if j >= RING:
                    sp.wait_ge(s_use, j - RING + 1)
                src = m.qks[b:b + 1, 1, :] if j < NB else m.vtok[b:b + 1, NT, :]
                sp.dma_start(ring[0:1, j % RING, NPG, :], src).then_inc(s_kn[j % RING], 16)

        @block.gpsimd
        def _(pool):
            pool.wait_ge(s_ix, 1)
            for j in range(2 * NB):
                b = j % NB
                if j >= RING:
                    pool.wait_ge(s_use, j - RING + 1)
                for g in range(NPG):
                    pool.indirect_dma_start(
                        out=ring[:, j % RING, g, :], out_offset=None,
                        in_=io["cache_k"] if j < NB else io["cache_v"],
                        in_offset=bass.IndirectOffsetOnAxis(ap=idx[:, b * NPG + g:b * NPG + g + 1], axis=0),
                    ).then_inc(s_k[j % RING], 16)

        def landed(eng, j):
            eng.wait_ge(s_k[j % RING], 16 * NPG * (j // RING + 1))
            eng.wait_ge(s_kn[j % RING], 16 * (j // RING + 1))

        @block.tensor
        def _(pe):
            def scores(n):
                t, h = divmod(n, NH)
                w = width(t)
                if n >= 1:
                    pe.wait_ge(s_ex, n)
                for x in range(2):
                    rows = slice(x * DH, (x + 1) * DH)
                    out = ps[:, 2 * x:2 * x + 2, :].rearrange("p a b -> p (a b)")
                    cuts = [(0, min(w, 512))] + ([(512, w)] if w > 512 else [])
                    for a, b in cuts:
                        pe.matmul(out[:, a:b], m.qT[rows, h, t * P:(t + 1) * P], m.kT[rows, h, a:b],
                                  start=True, stop=False)
                        lo = max(a, w - P)
                        mm = pe.matmul(out[:, lo:b], c("ident"), c("causal")[:, lo - (w - P):b - (w - P)],
                                       start=False, stop=True)
                mm.then_inc(s_sc, 1)

            def values(n):
                t, h = divmod(n, NH)
                hs = slice(h * DV, (h + 1) * DV)
                pe.wait_ge(s_at, n + 1)
                if n >= 1:
                    pe.wait_ge(s_trc, n)
                for j in range(t + 1):
                    pe.transpose(ps[:, 4, j * P:(j + 1) * P], att[:, NMETA + j * P:NMETA + (j + 1) * P], c("ident"))
                pe.transpose(ps[0:NMETA, 5, 0:P], att[:, 0:NMETA], c("ident")).then_inc(s_tr, 1)

            def weigh(n):
                t, h = divmod(n, NH)
                hs = slice(h * DV, (h + 1) * DV)
                pe.wait_ge(s_trc, n + 1)
                if h == 0 and t:
                    pe.wait_ge(s_oc, t)
                pe.matmul(ps[:, 6, hs], attT[0:NMETA, NT, :], m.vmeta[:, hs], start=True, stop=False)
                for j in range(t + 1):
                    mm = pe.matmul(ps[:, 6, hs], attT[:, j, :], m.vtok[:, j, hs], start=False, stop=(j == t))
                mm.then_inc(s_pv, 1)

            def transpose_out(t, n):
                pe.wait_ge(s_on, t + 1)
                for i in range(NH):
                    mm = pe.transpose(ps[:, 5, i * P:i * P + n], o[0:n, i * P:(i + 1) * P], c("ident")[0:n, 0:n])
                mm.then_inc(s_ot, 1)

            def query(b):
                if b >= 1:
                    pe.wait_ge(s_qbu, b)
                pe.matmul(ps[:, 7, :], c("one8")[0:NB, b:b + 1].broadcast_to([NB, P]), m.qks[0:NB, 0, :],
                          start=True, stop=True).then_inc(s_qb, 1)

            scores(0)
            for n in range(NQ):
                if n + 1 < NQ:
                    scores(n + 1)
                values(n)
                weigh(n)
                if n % NH == NH - 1:
                    transpose_out(n // NH, P)
                    pe.wait_ge(s_otc, n // NH + 1)
                if n % 2 == 1:
                    query(n // 2)
            pe.wait_ge(s_ss, NB)
            for g in range(NPG):
                pe.transpose(ps[0:NB * 8, g // 4, (g % 4) * P:(g % 4 + 1) * P], sc[:, g, :], c("ident"))
            pe.transpose(ps[0:NB * 8, 2, 0:1], sc[0:1, NPG, :], c("ident")[0:1, 0:1]).then_inc(s_st, 1)
            pe.wait_ge(s_sP, 1)
            for g in range(NPG):
                pe.transpose(ps[:, 3, g * NB * 8:(g + 1) * NB * 8], PT[:, g * P:(g + 1) * P], c("ident")[0:NB * 8, 0:NB * 8])
            pe.transpose(ps[0:1, 4, 0:NB * 8], PT[:, PAST:PAST + 1], c("ident")[0:NB * 8, 0:NB * 8]).then_inc(s_sT, 1)
            pe.wait_ge(s_sA, 1)
            for b in range(NB):
                landed(pe, NB + b)
                slot = (NB + b) % RING
                for h in range(NH):
                    out = ps[:, 6, h * NB + b:h * NB + b + 1]
                    for g in range(NPG):
                        pe.matmul(out, ring[:, slot, g, h * DV:(h + 1) * DV], attS[:, g, b * NH + h:b * NH + h + 1],
                                  start=(g == 0), stop=False)
                    mm = pe.matmul(out, ring[0:1, slot, NPG, h * DV:(h + 1) * DV], attS[0:1, NPG, b * NH + h:b * NH + h + 1],
                                   start=False, stop=True)
                mm.then_inc(s_so, 1)
            pe.wait_ge(s_soc, 1)
            for h in range(NH):
                mm = pe.transpose(ps[0:NB, 7, h * DV:(h + 1) * DV], oT[:, h * NB:(h + 1) * NB], c("ident"))
            mm.then_inc(s_pv, 1)
            transpose_out(NT, NB)

        @block.scalar
        def _(act):
            act.wait_ge(s_lam, 1)
            act.activation(lam2[:, :], lam2[:, :], ACT.Exp).then_inc(s_lame, 1)

            def root(t, n):
                act.wait_ge(s_ms, t + 1)
                act.activation(ost[0:n, 1, :], ost[0:n, 0, :], ACT.Sqrt).then_inc(s_rs, 1)
                act.wait_ge(s_ot, t + 1)
                act.activation(m.mixT[:, HP:2 * HP, t * P:t * P + n], ps[:, 5, :].rearrange("p (i t) -> p i t", i=NH)[:, :, 0:n],
                               ACT.Copy).then_inc(s_otc, 1)

            for n in range(NQ):
                t, h = divmod(n, NH)
                w = width(t)
                act.wait_ge(s_mx, n + 1)
                if n >= 1:
                    act.wait_ge(s_at, n)
                for x in range(2):
                    last = act.activation(pr[:, x, 0:w], ps[:, 2 * x:2 * x + 2, :].rearrange("p a b -> p (a b)")[:, 0:w],
                                          ACT.Exp, bias=mx[:, x:x + 1], scale=SCALE, accum_out=Z[:, x:x + 1])
                last.then_inc(s_ex, 1)
                act.wait_ge(s_tr, n + 1)
                if n >= 1:
                    act.wait_ge(s_pv, n)
                act.activation(attT[:, 0:t + 1, :], ps[:, 4, 0:(t + 1) * P].rearrange("p (j q) -> p j q", q=P), ACT.Copy)
                act.activation(attT[0:NMETA, NT, :], ps[0:NMETA, 5, 0:P], ACT.Copy).then_inc(s_trc, 1)
                if h == NH - 1:
                    root(t, P)
            act.wait_ge(s_smx, 1)
            act.activation(PT[:, 0:PAST], ps[0:NB * 8, 0:2, :].rearrange("p a b -> p (a b)"), ACT.Exp,
                           bias=sst[:, 2:3], scale=SCALE, accum_out=sst[:, 3:4])
            act.activation(PT[:, PAST:PAST + 1], ps[0:NB * 8, 2, 0:1], ACT.Exp, bias=sst[:, 2:3], scale=SCALE).then_inc(s_sex, 1)
            act.wait_ge(s_so, NB)
            act.activation(oT[:, :], ps[:, 6, 0:NH * NB], ACT.Copy).then_inc(s_soc, 1)
            root(NT, NB)

        @block.vector
        def _(dve):
            link = Link(dve, s_v)
            dve.wait_ge(s_ld, 48)
            link(dve.tensor_scalar(idx[:, :], pt[:, :], float(PAGE), c("rowid"), ALU.mult, ALU.add), s_ix)
            for a in range(2):
                link(dve.tensor_tensor(lamj[:, :], lam4[:, 2 * a, :], lam4[:, 2 * a + 1, :], ALU.mult))
                ins = dve.tensor_reduce(lam2[:, a:a + 1], lamj[:, :], AX.X, ALU.add)
                link(ins, s_lam if a else None)
            dve.wait_ge(s_lame, 1)
            link(dve.tensor_tensor(nlam[:, :], lam2[:, 1:2], lam2[:, 0:1], ALU.subtract))
            link(dve.tensor_scalar(nlam[:, :], nlam[:, :], -LAM_INIT, None, ALU.add))
            link(dve.tensor_scalar(subw[:, :], subw[:, :], 1.0 - LAM_INIT, None, ALU.mult))

            def soft(n):
                t, h = divmod(n, NH)
                w = width(t)
                dve.wait_ge(s_sc, n + 1)
                s = ps[:, 0:4, :].rearrange("p (x a) b -> p x (a b)", x=2)[:, :, 0:w]
                link(dve.tensor_reduce(mx[:, :], s, AX.X, ALU.max))
                link(dve.tensor_scalar(mx[:, :], mx[:, :], -SCALE, None, ALU.mult), s_mx)

            def combine(n):
                t, h = divmod(n, NH)
                w = width(t)
                dve.wait_ge(s_ex, n + 1)
                if n >= 1:
                    dve.wait_ge(s_tr, n)
                link(dve.reciprocal(rz[:, :], Z[:, :]))
                link(dve.tensor_tensor(rz[:, 1:2], rz[:, 1:2], nlam[:, :], ALU.mult))
                link(dve.tensor_scalar(pr[:, 1, 0:w], pr[:, 1, 0:w], rz[:, 1:2], None, ALU.mult))
                link(dve.scalar_tensor_tensor(att[:, 0:w], pr[:, 0, 0:w], rz[:, 0:1], pr[:, 1, 0:w], ALU.mult, ALU.add), s_at)

            def finish(t, n, bank):
                dve.wait_ge(s_pv, NH * (t + 1) if t < NT else NQ + 1)
                if t >= 1:
                    dve.wait_ge(s_ot, t)
                o3, q3 = (x[0:n, :].rearrange("p (h v) -> p h v", h=NH) for x in (o, osq))
                link(dve.tensor_copy(o[0:n, :], ps[0:n, bank, :]), s_oc)
                link(dve.tensor_tensor(osq[0:n, :], o[0:n, :], o[0:n, :], ALU.mult))
                link(dve.tensor_reduce(ost[0:n, 0, :], q3, AX.X, ALU.add))
                link(dve.tensor_scalar(ost[0:n, 0, :], ost[0:n, 0, :], 1.0 / DV, 1e-5, ALU.mult, ALU.add), s_ms)
                dve.wait_ge(s_rs, t + 1)
                link(dve.reciprocal(ost[0:n, 2, :], ost[0:n, 1, :]))
                link(dve.tensor_tensor(o3, o3, ost[0:n, 2, :].unsqueeze(2).broadcast_to([n, NH, DV]), ALU.mult))
                link(dve.tensor_tensor(o[0:n, :], o[0:n, :], subw[0:n, :], ALU.mult), s_on)

            def sample_scores(b):
                dve.wait_ge(s_qb, b + 1)
                landed(dve, b)
                slot = b % RING
                k = ring[:, slot, 0:NPG, :]
                dve.tensor_tensor(k, k, ps[:, 7, :].unsqueeze(1).broadcast_to([P, NPG, RWW]), ALU.mult)
                kn = ring[0:1, slot, NPG, :]
                link(dve.tensor_tensor(kn, kn, ps[0:1, 7, :], ALU.mult), s_qbu)
                dve.tensor_reduce(sc[:, 0:NPG, b * 8:(b + 1) * 8], k.rearrange("p g (x d) -> p g x d", d=DH), AX.X, ALU.add)
                link(dve.tensor_reduce(sc[0:1, NPG, b * 8:(b + 1) * 8], kn.rearrange("p (x d) -> p x d", d=DH), AX.X, ALU.add), s_ss)
                dve.engine_nop().then_inc(s_use, 1)

            soft(0)
            for n in range(NQ):
                combine(n)
                if n + 1 < NQ:
                    soft(n + 1)
                if n % NH == NH - 1:
                    finish(n // NH, P, 6)
                if n % 2 == 1:
                    sample_scores(n // 2)
            dve.wait_ge(s_st, 1)
            link(dve.tensor_reduce(sst[:, 0:1], ps[0:NB * 8, 0:2, :].rearrange("p a b -> p (a b)"), AX.X, ALU.max))
            link(dve.tensor_tensor(sst[:, 1:2], sst[:, 0:1], ps[0:NB * 8, 2, 0:1], ALU.max))
            link(dve.tensor_scalar(sst[:, 2:3], sst[:, 1:2], -SCALE, None, ALU.mult), s_smx)
            dve.wait_ge(s_sex, 1)
            link(dve.tensor_tensor(sst[:, 4:5], sst[:, 3:4], PT[:, PAST:PAST + 1], ALU.add))
            link(dve.reciprocal(sst[:, 5:6], sst[:, 4:5]))
            link(dve.scalar_tensor_tensor(sst[:, 6:7], c("map")[0:NB * 8, 1:2], nlam[0:NB * 8, :], c("map")[0:NB * 8, 0:1], ALU.mult, ALU.add))
            link(dve.tensor_tensor(sst[:, 7:8], sst[:, 6:7], sst[:, 5:6], ALU.mult))
            link(dve.tensor_scalar(PT[:, :], PT[:, :], sst[:, 7:8], None, ALU.mult), s_sP)
            dve.wait_ge(s_sT, 1)
            dve.tensor_reduce(attS[:, 0:NPG, :], ps[:, 3, :].rearrange("p (g x y) -> p g x y", g=NPG, y=2), AX.X, ALU.add)
            link(dve.tensor_reduce(attS[0:1, NPG, :], ps[0:1, 4, 0:NB * 8].rearrange("p (x y) -> p x y", y=2), AX.X, ALU.add), s_sA)
            for b in range(NB):
                dve.wait_ge(s_so, b + 1)
                dve.engine_nop().then_inc(s_use, 1)
            finish(NT, NB, 7)


def phase_peer(nc, io, m):
    ctx = ExitStack()
    with ctx:
        sb = lambda n, s, dt=F32: ctx.enter_context(nc.sbuf_tensor("p_" + n, s, dt))
        sem = lambda n: ctx.enter_context(nc.semaphore("p_" + n))
        ps, c = m.ps, m.c
        G = 4
        W2 = 2 * G
        PARTS = PKH
        ITERS = TOPK // W2
        PASSES = SLOTS // W2
        NTT = NT + 1
        w_out = m.w_out
        wq = sb("wq", [P, KT, D])
        skT = sb("skT", [P, PKH, NKEY])
        ln = sb("ln", [P, 4, D])
        xin = sb("xin", [P, D])
        junk = sb("junk", [P, D])
        x1 = sb("x1", [P, 2, D])
        x1T = sb("x1T", [P, KT, P])
        qT = xin[:, :].rearrange("p (k t) -> p k t", k=KT)
        st = sb("st", [P, 2, 8])
        s = sb("s", [P, 2 * PKH, NKEY])
        work = sb("work", [P, 256])
        vals = sb("vals", [P, 2, TOPK])
        ix = sb("ix", [P, 2, TOPK], U32)
        ixf = sb("ixf", [P, 2, TOPK])
        cand = sb("cand", [P, TOPK, TOPK])
        eq = sb("eq", [P, TOPK, TOPK])
        tv = sb("tv", [P, 2, TOPK])
        sel = sb("sel", [P, TOPK], U32)
        sab = sb("sab", [P, 2, TOPK], U32)
        sabf = sb("sabf", [P, 2, TOPK])
        ia = sb("ia", [P, 2, TOPK])
        nmax = sb("nmax", [P, 2])
        gex = sb("gex", [P, 2, TOPK])
        gz = sb("gz", [P, 2])
        gr = sb("gr", [P, 1])
        idx = sb("idx", [P, 2, SLOTS], I32)
        gate = sb("gate", [P, 2, SLOTS])
        Ur = sb("Ur", [P, W2, D])
        Vr = sb("Vr", [P, W2, D])
        idxu = sb("idxu", [P, W2], I32)
        idxv = sb("idxv", [P, W2], I32)
        dot = sb("dot", [P, W2])
        gel = sb("gel", [P, W2])
        wgt = sb("wgt", [P, W2])
        dg = sb("dg", [P, G, P])
        idr = sb("idr", [P, PKH], I32)
        gtr = sb("gtr", [P, PKH])
        wsel = sb("wsel", [P, PKH, NB])

        s_ld, s_wq = sem("ld"), sem("wq")
        s_x = sem("x")
        s_op = sem("op")
        s_res = sem("res")
        s_xr = sem("xr")
        s_vr, s_rt = [sem(f"vr{i}") for i in range(2)], [sem(f"rt{i}") for i in range(2)]
        s_x1, s_tr, s_trc = sem("x1"), sem("tr"), sem("trc")
        s_q, s_qc, s_sc, s_scc = sem("q"), sem("qc"), sem("sc"), sem("scc")
        s_tv, s_ge = sem("tv"), sem("ge")
        s_idx = sem("idx")
        s_gate = sem("gate")
        s_u = [sem(f"u{i}") for i in range(W2)]
        s_vv = [sem(f"v{i}") for i in range(W2)]
        s_turn = sem("turn")
        s_iu, s_iv = sem("iu"), sem("iv")
        s_dot = sem("dot")
        s_gel, s_w, s_dg = sem("gel"), sem("w"), sem("dg")
        s_vu = sem("vu")
        s_acc = sem("acc")
        s_y, s_yo = sem("y"), sem("yo")
        s_rs, s_rep, s_repc, s_ws = sem("rs"), sem("rep"), sem("repc"), sem("ws")
        s_v, s_a = sem("v"), sem("a")
        rows_of = lambda t: P if t < NT else NB

        def schedule(eng_gather, eng_finish, eng_head, eng_prep):
            for stage in range(5):
                eng_prep(0, stage)
            for h in range(2):
                eng_head(0, h)
            for t in range(NT):
                for part in range(PARTS):
                    eng_gather(t, part)
                    if part < 2 and t:
                        eng_finish(t - 1, part)
                    if part < 6:
                        eng_head(t, part + 2)
                        if part:
                            eng_prep(t + 1, part - 1)
                    elif t + 1 < NT:
                        eng_head(t + 1, part - 6)
                    else:
                        for h in range(4 * (part - 6), 4 * (part - 5)):
                            eng_head(NT, h)

        block = ctx.enter_context(nc.Block())

        @block.sync
        def _(sp):
            sp.dma_start(wq[:, :, :], io["pk_wq"].rearrange("(k p) n -> p k n", p=P)).then_inc(s_wq, 16)
            sp.dma_start(skT[:, :, :], io["skT"]).then_inc(s_ld, 16)
            for j, n in enumerate(("ln1_w", "ln1_b", "ln2_w", "ln2_b")):
                sp.dma_start(ln[:, j, :], io[n].partition_broadcast(P)).then_inc(s_ld, 16)
            for t in range(NTT):
                n = rows_of(t)
                if t:
                    sp.wait_ge(s_sc, t)
                sp.dma_start(xin[0:n, :], io["x_tok"][t * P:t * P + n, :]).then_inc(s_x, 16)
                if t >= 2:
                    sp.wait_ge(s_y, t - 1)
                    sp.dma_start(io["y_out"][(t - 2) * P:(t - 1) * P, :], x1[:, t % 2, :]).then_inc(s_yo, 16)
            sp.wait_ge(s_idx, PKH * NTT)
            for b in range(NB):
                sp.dma_start(idr[b * TOPK:(b + 1) * TOPK, :], idx[b:b + 1, NT % 2, :].rearrange("o (w h) -> o w h", h=PKH)
                             ).then_inc(s_rs, 16)
            sp.wait_ge(s_gate, PKH * NTT)
            for b in range(NB):
                sp.dma_start(gtr[b * TOPK:(b + 1) * TOPK, :], gate[b:b + 1, NT % 2, :].rearrange("o (w h) -> o w h", h=PKH)
                             ).then_inc(s_rs, 16)
            for t in range(NTT - 2, NTT):
                sp.wait_ge(s_y, t + 1)
                n = rows_of(t)
                sp.dma_start(io["y_out"][t * P:t * P + n, :], x1[0:n, t % 2, :]).then_inc(s_yo, 16)
            sp.wait_ge(s_yo, 16 * NTT)

        @block.gpsimd
        def _(pool):
            def row(table, dst, at, s_to):
                pool.indirect_dma_start(out=dst, out_offset=None, in_=io[table],
                                        in_offset=bass.IndirectOffsetOnAxis(ap=at, axis=0)).then_inc(s_to, 16)

            for t in range(NT):
                for part in range(PARTS):
                    pool.wait_ge(s_idx, PKH * t + part + 1)
                    it0 = ITERS * part
                    done = 2 * (PASSES * t + it0)
                    with pool.Fori(0, ITERS) as i:
                        for half in range(2):
                            col = idx[:, t % 2, bass.ds(W2 * i + (W2 * it0 + half * G), G)]
                            hs = slice(half * G, (half + 1) * G)
                            pool.wait_ge(s_dot, 2 * i + (done + half + 1))
                            pool.sem_inc(s_turn, 1)
                            pool.tensor_copy(idxu[:, hs], col).then_inc(s_iu, 1)
                            pool.wait_ge(s_iu, 2 * i + (done + half + 1))
                            pool.sem_inc(s_turn, 1)
                            for q in range(half * G, (half + 1) * G):
                                row("peer_u", Ur[:, q, :], idxu[:, q:q + 1], s_u[q])
                            pool.wait_ge(s_vu, 2 * i + (done + half + 1))
                            pool.sem_inc(s_turn, 1)
                            pool.tensor_copy(idxv[:, hs], col).then_inc(s_iv, 1)
                            pool.wait_ge(s_iv, 2 * i + (done + half + 1))
                            pool.sem_inc(s_turn, 1)
                            for q in range(half * G, (half + 1) * G):
                                row("peer_v", Vr[:, q, :], idxv[:, q:q + 1], s_vv[q])
            pool.wait_ge(s_rs, 16 * 2 * NB)
            done = 2 * (PASSES * NT)
            for half in range(2):
                pool.wait_ge(s_dot, done + half + 1)
                for h in range(half * G, (half + 1) * G):
                    row("peer_u", Ur[:, h, :], idr[:, h:h + 1], s_u[h])
                pool.wait_ge(s_vu, done + half + 1)
                for h in range(half * G, (half + 1) * G):
                    row("peer_v", Vr[:, h, :], idr[:, h:h + 1], s_vv[h])

        @block.tensor
        def _(pe):
            def prep(t, stage):
                n = rows_of(t)
                if stage == 0:
                    if t:
                        pe.wait_ge(s_scc, 4 * t)
                    else:
                        pe.wait_ge(m.s_wout, 16)
                    for a in range(2):
                        for k in range(KT):
                            mm = pe.matmul(ps[0:n, a, :], m.mixT[:, k, t * P:t * P + n], w_out[:, k, a * 512:(a + 1) * 512],
                                           start=(k == 0), stop=(k == KT - 1))
                    mm.then_inc(s_op, 1)
                if stage == 3:
                    pe.wait_ge(s_x1, t + 1)
                    for a in range(2):
                        for k in range(4 * a, 4 * a + 4):
                            mm = pe.transpose(ps[:, 2 + a, (k % 4) * P:(k % 4) * P + n], x1[0:n, t % 2, k * P:(k + 1) * P],
                                              c("ident")[0:n, 0:n])
                        mm.then_inc(s_tr, 1)
                    pe.wait_ge(s_trc, 2 * t + 2)
                    pe.wait_ge(s_wq, 16)
                    for a in range(2):
                        for f in range(4 * a, 4 * a + 4):
                            for k in range(KT):
                                mm = pe.matmul(ps[:, a, (f % 4) * P:(f % 4) * P + n], wq[:, k, f * P:(f + 1) * P], x1T[:, k, 0:n],
                                               start=(k == 0), stop=(k == KT - 1))
                        mm.then_inc(s_q, 1)
                if stage == 4:
                    pe.wait_ge(s_qc, 2 * t + 2)
                    pe.wait_ge(s_ld, 16 * 5)
                    for x in range(2):
                        for h in range(PKH):
                            mm = pe.matmul(ps[0:n, 2 * x + h // 4, (h % 4) * P:(h % 4 + 1) * P], qT[x * DH:(x + 1) * DH, h, 0:n],
                                           skT[x * DH:(x + 1) * DH, h, :], start=True, stop=True)
                    mm.then_inc(s_sc, 1)

            def gather(t, part):
                acc = ps[:, 4 + 2 * (t % 2):6 + 2 * (t % 2), :]
                if part == 0:
                    if t >= 2:
                        pe.wait_ge(s_res, t - 1)
                    for a in range(2):
                        pe.matmul(acc[:, a, :], m.zero[0:1, :], wq[0:1, 0, 0:512], start=True, stop=False, skip_group_check=True)
                it0 = ITERS * part
                done = 2 * (PASSES * t + it0)
                with pe.Fori(0, ITERS) as i:
                    for half in range(2):
                        for q in range(half * G, (half + 1) * G):
                            pe.wait_ge(s_dg, W2 * i + (G * done + q + 1))
                            pe.wait_ge(s_vv[q], 16 * i + (8 * done + 16))
                            for a in range(2):
                                mm = pe.matmul(acc[:, a, :], dg[:, q % G, :], Vr[:, q, a * 512:(a + 1) * 512],
                                               start=False, stop=False, skip_group_check=True)
                        mm.then_inc(s_vu, 1)
                if part == PARTS - 1:
                    for a in range(2):
                        mm = pe.matmul(acc[:, a, :], m.zero[0:1, :], wq[0:1, 0, 0:512], start=False, stop=True, skip_group_check=True)
                    mm.then_inc(s_acc, 1)

            schedule(gather, lambda t, x: None, lambda t, h: None, prep)
            pe.wait_ge(s_scc, 4 * NTT)
            for a in range(2):
                mm = pe.matmul(ps[:, a, :], c("spread")[0:NB, :], x1[0:NB, NT % 2, a * 512:(a + 1) * 512], start=True, stop=True)
            mm.then_inc(s_rep, 1)
            pe.wait_ge(s_ws, 1)
            for h in range(PKH):
                pe.wait_ge(s_vv[h], 16 * (PASSES * NT + 1))
                for a in range(2):
                    mm = pe.matmul(ps[0:NB, 4 + a, :], wsel[:, h, :], Vr[:, h, a * 512:(a + 1) * 512],
                                   start=(h == 0), stop=(h == PKH - 1), skip_group_check=True)
            mm.then_inc(s_acc, 1)

        @block.scalar
        def _(act):
            def root(which, k, n):
                act.wait_ge(s_vr[which], k)
                act.activation(st[0:n, which, 4:5], st[0:n, which, 3:4], ACT.Sqrt).then_inc(s_rt[which], 1)

            def finish(t, x):
                if x == 0:
                    root(1, t + 1, rows_of(t))

            def head(t, h):
                n = rows_of(t)
                k = PKH * t + h
                act.wait_ge(s_tv, k + 1)
                act.activation(gex[0:n, h % 2, :], tv[0:n, h % 2, :], ACT.Exp, bias=nmax[0:n, h % 2:h % 2 + 1],
                               accum_out=gz[0:n, h % 2:h % 2 + 1]).then_inc(s_ge, 1)

            def prep(t, stage):
                n = rows_of(t)
                if stage == 1:
                    root(0, t + 1, n)
                if stage == 3:
                    for a in range(2):
                        act.wait_ge(s_tr, 2 * t + a + 1)
                        act.activation(x1T[:, 4 * a:4 * a + 4, 0:n], ps[:, 2 + a, :].rearrange("p (k t) -> p k t", k=4)[:, :, 0:n],
                                       ACT.Copy).then_inc(s_trc, 1)
                    for a in range(2):
                        act.wait_ge(s_q, 2 * t + a + 1)
                        act.activation(qT[:, 4 * a:4 * a + 4, 0:n], ps[:, a, :].rearrange("p (k t) -> p k t", k=4)[:, :, 0:n],
                                       ACT.Copy).then_inc(s_qc, 1)
                if stage == 4:
                    act.wait_ge(s_sc, t + 1)
                    if t:
                        act.wait_ge(s_idx, PKH * t)
                    for a in range(4):
                        act.activation(s[0:n, 4 * a:4 * a + 4, :], ps[0:n, a, :].rearrange("p (k t) -> p k t", k=4),
                                       ACT.Copy).then_inc(s_scc, 1)

            def gather(t, part):
                done = 2 * (PASSES * t + ITERS * part)
                with act.Fori(0, ITERS) as i:
                    for half in range(2):
                        hs = slice(half * G, (half + 1) * G)
                        act.wait_ge(s_dot, 2 * i + (done + half + 3))
                        act.activation(gel[:, hs], dot[:, hs], ACT.Gelu).then_inc(s_gel, 1)
                        act.wait_ge(s_w, 2 * i + (done + half + 1))
                        act.wait_ge(s_vu, 2 * i + (done + half + 2))
                        for q in range(half * G, (half + 1) * G):
                            act.activation(dg[:, q % G, :], c("ident"), ACT.Copy, scale=wgt[:, q:q + 1]).then_inc(s_dg, 1)

            schedule(gather, finish, head, prep)
            root(1, NT, P)
            act.wait_ge(s_rep, 1)
            act.activation(xin[:, :], ps[:, 0:2, :].rearrange("p a b -> p (a b)"), ACT.Copy).then_inc(s_repc, 1)
            act.wait_ge(s_dot, 2 * (PASSES * NT) + 3)
            act.activation(gel[:, :], dot[:, :], ACT.Gelu).then_inc(s_gel, 1)
            root(1, NTT, NB)

        @block.vector
        def _(dve):
            link = Link(dve, s_v)

            def spread(which, x, add, xin_, n, s_read):
                v = lambda j: st[0:n, which, j:j + 1]
                for a in range(2):
                    cs = slice(a * 512, (a + 1) * 512)
                    last = dve.scalar_tensor_tensor(x[:, cs], xin_[:, cs], ALPHA, add[:, a, :], ALU.mult, ALU.add, accum_out=v(a))
                link(last, s_read)
                link(dve.tensor_scalar(v(2), v(0), v(1), -1.0 / D, ALU.add, ALU.mult))
                link(dve.tensor_scalar(x, x, v(2), None, ALU.add))
                link(dve.tensor_tensor_reduce(junk[0:n, :], x, x, 1.0, 0.0, ALU.mult, ALU.add, v(5)))
                link(dve.tensor_scalar(v(3), v(5), 1.0 / D, 1e-5, ALU.mult, ALU.add), s_vr[which])

            def scale(which, k, x, n, s_to):
                v = lambda j: st[0:n, which, j:j + 1]
                dve.wait_ge(s_rt[which], k)
                if k == 1:
                    dve.wait_ge(s_ld, 16 * 5)
                link(dve.reciprocal(v(6), v(4)))
                link(dve.scalar_tensor_tensor(x, x, v(6), ln[0:n, 2 * which, :], ALU.mult, ALU.mult))
                link(dve.tensor_tensor(x, x, ln[0:n, 2 * which + 1, :], ALU.add), s_to)

            def top16(val, ind, src, n):
                w = work[0:n, 0:src.shape[1]]
                link(dve.max(val[:, 0:8], src))
                dve.max_index(ind[:, 0:8], val[:, 0:8], src)
                link(dve.match_replace(w, val[:, 0:8], src, -3.0e38))
                link(dve.max(val[:, 8:16], w))
                return dve.max_index(ind[:, 8:16], val[:, 8:16], w)

            def gates(t, h):
                n = rows_of(t)
                k = PKH * t + h
                dve.wait_ge(s_ge, k + 1)
                link(dve.reciprocal(gr[0:n, :], gz[0:n, h % 2:h % 2 + 1]))
                link(dve.tensor_scalar(gate[0:n, t % 2, TOPK * h:TOPK * (h + 1)], gex[0:n, h % 2, :], gr[0:n, :], None,
                                       ALU.mult), s_gate)

            def head(t, h):
                n = rows_of(t)
                if h:
                    gates(t, h - 1)
                elif t:
                    gates(t - 1, PKH - 1)
                if h == 0:
                    dve.wait_ge(s_scc, 4 * t + 4)
                for x in range(2):
                    link(top16(vals[0:n, x, :], ix[0:n, x, :], s[0:n, x * PKH + h, :], n))
                link(dve.tensor_copy(ixf[0:n], ix[0:n]))
                link(dve.tensor_tensor(cand[0:n], vals[0:n, 0, :].unsqueeze(2).broadcast_to([n, TOPK, TOPK]),
                                       vals[0:n, 1, :].unsqueeze(1).broadcast_to([n, TOPK, TOPK]), ALU.add))
                link(top16(tv[0:n, h % 2, :], sel[0:n, :], cand[0:n].rearrange("p a b -> p (a b)"), n))
                link(dve.tensor_scalar(nmax[0:n, h % 2:h % 2 + 1], tv[0:n, h % 2, 0:1], -1.0, None, ALU.mult), s_tv)
                dve.tensor_scalar(sab[0:n, 0, :], sel[0:n, :], 4, None, ALU.logical_shift_right)
                link(dve.tensor_scalar(sab[0:n, 1, :], sel[0:n, :], 15, None, ALU.bitwise_and))
                link(dve.tensor_copy(sabf[0:n], sab[0:n]))
                for x in range(2):
                    link(dve.tensor_tensor(eq[0:n], sabf[0:n, x, :].unsqueeze(2).broadcast_to([n, TOPK, TOPK]),
                                           c("iota16")[0:n].unsqueeze(1).broadcast_to([n, TOPK, TOPK]), ALU.is_equal))
                    link(dve.tensor_tensor(eq[0:n], eq[0:n], ixf[0:n, x, :].unsqueeze(1).broadcast_to([n, TOPK, TOPK]), ALU.mult))
                    link(dve.tensor_reduce(ia[0:n, x, :], eq[0:n], AX.X, ALU.add))
                link(dve.scalar_tensor_tensor(idx[0:n, t % 2, TOPK * h:TOPK * (h + 1)], ia[0:n, 0, :], float(NKEY), ia[0:n, 1, :],
                                              ALU.mult, ALU.add), s_idx)

            def prep(t, stage):
                n = rows_of(t)
                x = x1[0:n, t % 2, :]
                if stage == 1:
                    dve.wait_ge(s_op, t + 1)
                    dve.wait_ge(s_x, 16 * (t + 1))
                    if t >= 2:
                        dve.wait_ge(s_yo, 16 * (t - 1))
                    spread(0, x, ps[0:n, 0:2, :], xin[0:n, :], n, s_xr)
                if stage == 2:
                    scale(0, t + 1, x, n, s_x1)

            def gather(t, part):
                it0 = ITERS * part
                done = 2 * (PASSES * t + it0)
                with dve.Fori(0, ITERS) as i:
                    for half in range(2):
                        for q in range(half * G, (half + 1) * G):
                            dve.wait_ge(s_u[q], 16 * i + (8 * done + 16))
                            ins = dve.tensor_tensor_reduce(Ur[:, q, :], Ur[:, q, :], x1[:, t % 2, :], 1.0, 0.0, ALU.mult, ALU.add,
                                                           dot[:, q:q + 1])
                        ins.then_inc(s_dot, 1)
                        hs = slice(half * G, (half + 1) * G)
                        dve.wait_ge(s_gel, 2 * i + (done + half + 1))
                        dve.tensor_tensor(wgt[:, hs], gel[:, hs], gate[:, t % 2, bass.ds(W2 * i + (W2 * it0 + half * G), G)],
                                          ALU.mult).then_inc(s_w, 1)

            def finish(t, step):
                n = rows_of(t)
                x = x1[0:n, t % 2, :]
                bank = 4 + 2 * (t % 2)
                if step == 0:
                    dve.wait_ge(s_acc, t + 1)
                    spread(1, x, ps[0:n, bank:bank + 2, :], x, n, s_res)
                else:
                    scale(1, t + 1, x, n, s_y)

            for q in (s_dot, s_vu):
                for _ in range(2):
                    dve.engine_nop().then_inc(q, 1)
            schedule(gather, finish, head, prep)
            gates(NT, PKH - 1)
            for step in range(2):
                finish(NT - 1, step)
            dve.wait_ge(s_repc, 1)
            for h in range(PKH):
                dve.wait_ge(s_u[h], 16 * (PASSES * NT + 1))
                ins = dve.tensor_tensor_reduce(Ur[:, h, :], Ur[:, h, :], xin[:, :], 1.0, 0.0, ALU.mult, ALU.add, dot[:, h:h + 1])
            ins.then_inc(s_dot, 1)
            dve.wait_ge(s_gel, 2 * (PASSES * NT) + 1)
            dve.wait_ge(s_rs, 16 * 2 * NB)
            link(dve.tensor_tensor(wgt[:, :], gel[:, :], gtr[:, :], ALU.mult))
            link(dve.tensor_tensor(wsel[:, :, :], wgt[:, :].unsqueeze(2).broadcast_to([P, PKH, NB]),
                                   c("gather").unsqueeze(1).broadcast_to([P, PKH, NB]), ALU.mult), s_ws)
            for step in range(2):
                finish(NT, step)


class Mem:
    pass


def build(nc, io, upto=9, debug=None):
    root = ExitStack()
    with root:
        m = Mem()
        sb0 = lambda n, s, dt=F32: root.enter_context(nc.sbuf_tensor(n, s, dt))
        m.ps = root.enter_context(nc.psum_tensor("ps", [P, 8, 512], F32))
        tables = [sb0("table_long", TABLES[0].shape)]
        m.params = sb0("params", [P, NPAR])
        m.par = lambda n, i: m.params[:, PAR[n] + i:PAR[n] + i + 1]
        m.c = lambda n: tables[WHERE[n][0]][:, WHERE[n][1]:WHERE[n][1] + WHERE[n][2]]
        m.mixT = sb0("mixT", [P, KT, SEQ + NB])
        m.omka = sb0("omka", [P, HP])
        m.zero = sb0("zero", [1, P])
        m.w_out = sb0("w_out", [P, KT, D])
        m.s_wout = root.enter_context(nc.semaphore("s_wout"))
        lent = m.w_out[:, :, :].rearrange("p k n -> p (k n)")
        m.ar = lent[:, 0:HP * 2 * TA].rearrange("p (i x t) -> p i x t", i=HP, x=2)
        m.bt = lent[:, HP * 2 * TA:HP * 3 * TA].rearrange("p (i t) -> p i t", i=HP)
        mid = ExitStack()
        with mid:
            sb = lambda n, s, dt=F32: mid.enter_context(nc.sbuf_tensor(n, s, dt))
            tables.append(sb("table_short", TABLES[1].shape))
            m.w2a2 = sb("w2a2", [P, RWW])
            m.g2 = sb("g2", [P, RWW])
            m.shift0 = sb("shift0", [P, NCH, NB])
            m.shout = sb("shout", [P, NCH, 1 + NB])
            m.qT = sb("qT", [P, NH, SEQ])
            m.qTs = sb("qTs", [P, NH, NB])
            m.kT = sb("kT", [P, NH, TP])
            m.vtok = sb("vtok", [P, NT + 1, RWW])
            m.vmeta = sb("vmeta", [NMETA, RWW])
            m.qks = sb("qks", [SM, 2, RWW])
            m.kt = sb("kt", [P, HP, TA])
            m.rk = sb("rk", [P, HP, TA])
            m.vT = sb("vT", [P, HP, TA])
            m.sg = sb("sg", [P, TA])
            m.eend = sb("eend", [P, HP, 17])
            m.consts = [(tables[0][:, :], io["table0"]), (tables[1][:, :], io["table1"]), (m.params[:, :], io["params"]), (m.w2a2[:, :], io["w2a2"]),
                        (m.g2[:, :], io["g2"]), (m.shift0[:, :, :], io["shift0"])]
            phase_project(nc, io, m)
            if debug:
                debug(nc, m, 1)
            if upto <= 1:
                return
            phase_rwkv(nc, io, m)
            if debug:
                debug(nc, m, 2)
            if upto <= 2:
                return
            phase_attention(nc, io, m)
            if debug:
                debug(nc, m, 3)
            if upto <= 3:
                return
        phase_peer(nc, io, m)


def arrange(x):
    a = {}
    chan = lambda v: np.asarray(v).reshape(-1, P).T
    a["table0"], a["table1"] = TABLES
    a["params"] = np.concatenate([chan(x["mu_shift"][0]), chan(x["w0"][0]), chan(x["a0"][0]), chan(x["k_k"][0]),
                                  chan(x["k_a"][0]), chan(x["r_k"][0])], 1)
    a["w2a2"] = np.concatenate([x["w2_decay"][0], x["a2"][0]], 0)
    a["g2"] = x["g2"][0]
    a["shift0"] = np.asarray(x["state_shift"][0]).reshape(NB, NCH, P).transpose(2, 1, 0)
    a["xT"] = np.concatenate([x["x_prompt"][0], x["x_sample"][:, 0], x["meta_tokens"]], 0).T
    a["w_in"] = x["w_in"][0]
    a["lnx_w"], a["lnx_b"] = x["lnx_w"][0], x["lnx_b"][0]
    a["state"] = np.asarray(x["state_wkv"][0]).reshape(NB, HP, 2, DH, DH).transpose(2, 4, 0, 1, 3).reshape(P, NB, HP, DH)
    a["w_out"], a["pk_wq"] = x["w_out"][0], x["pk_wq"][0]
    a["peer_u"], a["peer_v"] = x["peer_u"][0], x["peer_v"][0]
    for n in ("ln1_w", "ln1_b", "ln2_w", "ln2_b"):
        a[n] = x[n][0]
    a["skT"] = np.asarray(x["pk_subkeys"][0]).transpose(1, 3, 0, 2).reshape(P, PKH, NKEY)
    a["x_tok"] = np.concatenate([x["x_prompt"][0], x["x_sample"][:, 0]], 0)
    a["pages"] = np.asarray(x["page_table"]).reshape(-1)
    a["lams"] = np.stack([x["lam_q1"][0], x["lam_k1"][0], x["lam_q2"][0], x["lam_k2"][0]])
    a["subln_w"] = x["subln_w"][0]
    a["cache_k"] = np.asarray(x["cache_k"][0]).reshape(-1, RWW)
    a["cache_v"] = np.asarray(x["cache_v"][0]).reshape(-1, RWW)
    return {k: np.ascontiguousarray(v) for k, v in a.items()}


_OUTS = {
    "y_out": (SEQ + NB, D), "k_out": (TA, RWW), "v_out": (TA, RWW), "shift_out": (P, NCH, 1 + NB),
    "wkv_p_out": (P, HP, DH), "wkv_s_out": (P, NB, HP, DH),
}


def returned(r):
    y = r["y_out"]
    tokens = lambda a: np.concatenate([a[SEQ + NB:], a[:SEQ]], 0)
    k, v = r["k_out"], r["v_out"]
    sh = r["shift_out"].transpose(2, 1, 0).reshape(1 + NB, RWC)
    wp = r["wkv_p_out"].reshape(2, DH, HP, DH).transpose(2, 0, 3, 1).reshape(1, 1, 2 * HP, DH, DH)
    ws = r["wkv_s_out"].reshape(2, DH, NB, HP, DH).transpose(2, 3, 0, 4, 1).reshape(1, NB, 2 * HP, DH, DH)
    out = (y[None, :SEQ], y[SEQ:, None], tokens(k).reshape(1, 1, TP, NH, 2, DH), tokens(v).reshape(1, 1, TP, NH, DV),
           wp, sh[None, 0:1], k[SEQ:SEQ + NB].reshape(1, NB, 1, NH, 2, DH), v[SEQ:SEQ + NB].reshape(1, NB, 1, NH, DV),
           ws, sh[None, 1:])
    return tuple(np.ascontiguousarray(a) for a in out)


def kernel(**inputs):
    import concourse.bacc as bacc
    from concourse.bass_utils import run_bass_kernel_spmd

    nc = bacc.Bacc("TRN2", target_bir_lowering=False, num_devices=1)
    arrays, io = {}, {}
    for n, a in arrange({k: np.asarray(v) for k, v in inputs.items()}).items():
        arrays[f"in_{n}_dram"] = a
        io[n] = nc.dram_tensor(f"in_{n}_dram", a.shape, mybir.dt.from_np(a.dtype), kind="ExternalInput").ap()
    for n, shape in _OUTS.items():
        io[n] = nc.dram_tensor(f"out_{n}_dram", shape, F32, kind="ExternalOutput").ap()
    build(nc, io)
    r = run_bass_kernel_spmd(nc, [arrays], core_ids=[0])
    return returned({n: r.results[0][f"out_{n}_dram"] for n in _OUTS})
```

```python
import math

import numpy as np
import concourse.bass as bass
from concourse import mybir
from concourse.alu_op_type import AluOpType as ALU
from contextlib import ExitStack

F32 = mybir.dt.float32
I32 = mybir.dt.int32
U32 = mybir.dt.uint32
ACT = mybir.ActivationFunctionType
AX = mybir.AxisListType

P = 128
D = 1024
KT = D // P
NMETA, SEQ, NB = 16, 512, 8
NT = SEQ // P
TP = NMETA + SEQ
TA = TP + NB
SM = NB + NMETA
RWW, RWC = 512, 1792
NCH = RWC // P
HP = 4
DH = 64
NH, DV = 4, 128
PAST, PAGE = 1024, 128
NPG = PAST // PAGE
PKH, NKEY, TOPK = 8, 128, 16
NEXP = NKEY * NKEY
SLOTS = PKH * TOPK
CH = 64
LAM_INIT = 0.8 - 0.6 * math.exp(-0.3 * 0)
ALPHA = 2.0 ** 0.25
BIG = 1.0e30


class Link:

    def __init__(self, eng, own):
        self.eng, self.own, self.n = eng, own, {}

    def __call__(self, ins, sem=None):
        s = sem if sem is not None else self.own
        k = s.name
        self.n[k] = self.n.get(k, 0) + 1
        ins.then_inc(s, 1)
        self.eng.wait_ge(s, self.n[k])


def constant_table():
    t, s = np.arange(P)[:, None], np.arange(P)[None, :]
    same = (t // CH) == (s // CH)
    parts = {}
    parts["ident"] = (t == s)
    strict_up = same & (t < s)
    incl_up = same & (t <= s)
    parts["mask4"] = np.concatenate([strict_up, incl_up, strict_up, incl_up], 1)

    def level(l):
        return (t // (2 * l) == s // (2 * l)) & ((t // l) % 2 == 1) & ((s // l) % 2 == 0)

    parts["first"] = level(1)
    parts["firstT"] = level(1).T
    for l in (2, 4, 8, 16, 32):
        parts[f"lev{l}"] = level(l)
    parts["heads"] = (t // DH == s // DH)
    parts["half"] = (t // DH == np.arange(2)[None, :])
    parts["diag64"] = (t % DH == np.arange(DH)[None, :])
    parts["causal"] = np.where(s > t, -BIG, 0.0)
    parts["one8"] = (t == np.arange(NB)[None, :])
    parts["spread"] = (t == s // TOPK)
    parts["gather"] = (t // TOPK == np.arange(NB)[None, :])
    parts["pick"] = np.concatenate([(t // DH == h) & (np.arange(2 * NB - 1)[None, :] == NB - 1) for h in range(2)], 1)
    parts["rows4"] = (t // NH == np.arange(NB)[None, :])
    parts["own4"] = (t % NH == np.arange(NH)[None, :])
    parts["iota16"] = np.broadcast_to(np.arange(16)[None, :], (P, 16))
    parts["rowid"] = t
    parts["map"] = np.concatenate([t % 2 == 0, t % 2 == 1], 1)
    half = 32
    inv = (np.float32(10000.0) ** (-np.arange(half, dtype=np.float32) / np.float32(half))).astype(np.float32)
    pos = np.zeros((P, NT + 1), np.float32)
    for tt in range(NT):
        pos[:, tt] = NMETA + P * tt + np.arange(P)
    pos[:NB, NT] = PAST
    pos[NB:SM, NT] = np.arange(NMETA)
    ang = pos[:, :, None] * inv[None, None, :]
    c, sn = np.cos(ang), np.sin(ang)
    parts["cos"] = np.concatenate([c, c], 2).reshape(P, -1)
    parts["sin"] = np.concatenate([-sn, sn], 2).reshape(P, -1)
    start = np.ones((P, TA))
    start[:, 0] = 0
    start[:, NMETA:TP:CH] = 0
    start[:, TP:] = 0
    parts["start"] = start
    keep = ("ident", "spread", "gather", "iota16")
    where, tables = {}, []
    for which in (True, False):
        at, here = 0, []
        for n, a in parts.items():
            if (n in keep) == which:
                where[n] = (len(tables), at, a.shape[1])
                at += a.shape[1]
                here.append(np.asarray(a, np.float32))
        tables.append(np.concatenate(here, 1))
    return where, tables


WHERE, TABLES = constant_table()
PAR = {}
_at = 0
for _n, _c in (("mu", NCH), ("w0", HP), ("a0", HP), ("k_k", HP), ("k_a", HP), ("r_k", HP)):
    PAR[_n] = _at
    _at += _c
NPAR = _at


def phase_project(nc, io, m):
    ctx = ExitStack()
    with ctx:
        sb = lambda n, s, dt=F32: ctx.enter_context(nc.sbuf_tensor(n, s, dt))
        sem = lambda n: ctx.enter_context(nc.semaphore(n))
        ps = m.ps
        xT = sb("xT", [P, KT, TA])
        wr = sb("w_ring", [P, 2, KT, 512])
        cols = sb("cols", [P, 2, TA + 1])
        diff = sb("diff", [P, 2, TA])
        rraw = m.ar[:, :, 1, :]
        kraw = m.kt
        xwa = sb("xwa", [P, TA])
        xg = sb("xg", [P, TA])
        kk = sb("kk", [P, TA])
        kk2 = sb("kk2", [P, TA])
        sgm = sb("sgm", [P, TA])
        am = sb("am", [P, TA])
        L = sb("L", [P, TA])
        E = sb("E", [P, TA])
        Ei = sb("Ei", [P, TA])
        Lp = sb("Lp", [P, TA])
        lent = m.mixT[:, :, :].rearrange("p k n -> p (k n)")
        rot = lent[:, 0:1536].rearrange("p (a n) -> p a n", a=3)
        rtmp, rtmp2 = lent[:, 1536:2048], lent[:, 2048:2560]
        c = m.c
        par = m.par

        XPARTS = 4
        s_const = sem("s_const")
        s_x = [sem(f"s_x{i}") for i in range(XPARTS)]
        s_wfirst = sem("s_wfirst")
        s_w = [sem(f"s_w{i}") for i in range(2)]
        s_item = sem("s_item")
        s_cols = sem("s_cols")
        s_mixed = sem("s_mixed")
        s_rope = sem("s_rope")
        s_val = sem("s_val")
        s_tr = sem("s_tr")
        s_trc = sem("s_trc")
        s_rot_out = [sem(f"s_rot_out{i}") for i in range(3)]
        s_tanh = sem("s_tanh")
        s_sq = sem("s_sq")
        s_lora = sem("s_lora")
        s_sig = sem("s_sig")
        s_ss = sem("s_ss")
        s_rn = sem("s_rn")
        s_L = sem("s_L")
        s_E = sem("s_E")
        s_Eu = sem("s_Eu")
        s_v = sem("s_v")
        s_a = sem("s_a")
        s_out = sem("s_out")

        NG = 7
        GW = [4, 4, 4, 2, 4, 4, 4]
        chan = list(range(NCH))
        done_group = [4, 8, 12, 14, 19, 24, 29]

        block = ctx.enter_context(nc.Block())

        @block.sync
        def _(sp):
            x_in, w_first = (a.rearrange("(k p) n -> p k n", p=P) for a in (io["xT"], io["w_in"][:, 0:GW[0] * P]))
            sp.dma_start(wr[:, 0, :, 0:P], w_first[:, :, 0:P]).then_inc(s_wfirst, 16)
            for q in range(XPARTS):
                ks = slice(q * KT // XPARTS, (q + 1) * KT // XPARTS)
                sp.dma_start(xT[:, ks, :], x_in[:, ks, :]).then_inc(s_x[q], 16)
            sp.dma_start(wr[:, 0, :, P:GW[0] * P], w_first[:, :, P:]).then_inc(s_w[0], 16)
            for n in m.consts:
                sp.dma_start(n[0], n[1]).then_inc(s_const, 16)
            for g in range(1, NG):
                if g >= 2:
                    sp.wait_ge(s_item, done_group[g - 2])
                w = GW[g] * P
                sp.dma_start(wr[:, g % 2, :, 0:w],
                             io["w_in"][:, g * 512 - (256 if g > 3 else 0):][:, 0:w].rearrange("(k p) n -> p k n", p=P)
                             ).then_inc(s_w[g % 2], 16)
            n_out = 0
            for n in range(10):
                tt = n % 5
                if n >= 5:
                    sp.wait_ge(s_rope, n + 1)
                    if tt < NT:
                        sp.dma_start(io["k_out"][tt * P:(tt + 1) * P, :], rot[:, n % 3, :]).then_inc(s_rot_out[n % 3], 16)
                    else:
                        sp.dma_start(io["k_out"][SEQ:, :], m.qks[0:SM, 1, :]).then_inc(s_out, 16)
                        n_out += 1
            sp.dma_start(m.q_rows, m.qks[0:NB, 0, :]).then_inc(s_out, 16)
            n_out += 1
            sp.wait_ge(s_val, 4)
            sp.dma_start(io["v_out"][0:SEQ, :].rearrange("(t p) n -> p t n", p=P), m.vtok[:, 0:NT, :]).then_inc(s_out, 16)
            sp.wait_ge(s_val, 5)
            sp.dma_start(io["v_out"][SEQ:, :], m.vtok[0:SM, NT, :]).then_inc(s_out, 16)
            sp.dma_start(m.vmeta[:, :], m.vtok[NB:SM, NT, :]).then_inc(s_out, 16)
            sp.wait_ge(s_mixed, NCH)
            sp.dma_start(io["shift_out"], m.shout[:, :, :]).then_inc(s_out, 16)
            n_out += 4
            sp.wait_ge(s_out, 16 * n_out)
            for i, k in ((0, 1), (1, 1), (2, 2)):
                sp.wait_ge(s_rot_out[i], 16 * sum(1 for n in range(5, 9) if n % 3 == i))

        @block.tensor
        def _(pe):
            def arrived(g):
                pe.wait_ge(s_w[g % 2], 16 * (g // 2 + 1))

            def channel_tiles(g):
                if g:
                    arrived(g)
                for mt in range(GW[g]):
                    ct = 4 * g + mt
                    if ct == 0:
                        pe.wait_ge(s_wfirst, 16)
                    if ct == 1:
                        arrived(0)
                    if ct >= 2:
                        pe.wait_ge(s_cols, ct - 1)
                    for k in range(KT):
                        if ct == 0 and k * XPARTS % KT == 0:
                            pe.wait_ge(s_x[k * XPARTS // KT], 16)
                        w = wr[:, g % 2, k, mt * P:(mt + 1) * P]
                        pe.matmul(ps[:, ct % 2, :], w, xT[:, k, 0:SEQ], start=(k == 0), stop=(k == KT - 1))
                        mm = pe.matmul(ps[:, 2 + ct % 2, 0:SM], w, xT[:, k, SEQ:TA], start=(k == 0), stop=(k == KT - 1))
                    mm.then_inc(s_item, 1)

            def token_tiles(g):
                arrived(g)
                for tt in range(NT + 1):
                    n = 5 * (g - 4) + tt
                    rows = P if tt < NT else SM
                    if n >= 2:
                        pe.wait_ge(s_rope, min(n - 1, 10))
                        if n - 1 > 10:
                            pe.wait_ge(s_val, n - 11)
                    for k in range(KT):
                        mm = pe.matmul(ps[0:rows, 4 + n % 2, :], xT[:, k, tt * P:tt * P + rows], wr[:, g % 2, k, :],
                                       start=(k == 0), stop=(k == KT - 1))
                    mm.then_inc(s_item, 1)
                    if 1 <= n <= 10:
                        transposes(n - 1)

            def transposes(n):
                if n == 0:
                    pe.wait_ge(s_const, 16 * len(m.consts))
                rows = P if n % 5 < NT else SM
                src = rot[:, n % 3, :] if n % 5 < NT else m.qks[0:SM, n // 5, :]
                pe.wait_ge(s_rope, n + 1)
                if n >= 2:
                    pe.wait_ge(s_trc, n - 1)
                for h in range(NH):
                    mm = pe.transpose(ps[:, 6 + n % 2, h * P:h * P + rows], src[:, h * P:(h + 1) * P], c("ident")[0:rows, 0:rows])
                mm.then_inc(s_tr, 1)

            def lora(i):
                pe.wait_ge(s_tanh, 1)
                if i >= 1:
                    pe.wait_ge(s_rn, i)
                    pe.wait_ge(s_sig, 2 * i)
                else:
                    pe.wait_ge(s_cols, NCH)
                for a, b in ((0, 512), (512, TA)):
                    pe.matmul(ps[:, a // 512, 0:b - a], m.w2a2[0:DH, i * P:(i + 1) * P], xwa[0:DH, a:b], start=True, stop=True)
                for a, b in ((0, 512), (512, TA)):
                    mm = pe.matmul(ps[:, 2 + a // 512, 0:b - a], m.w2a2[DH:P, i * P:(i + 1) * P], xwa[DH:P, a:b], start=True, stop=True)
                mm.then_inc(s_lora, 1)
                pe.wait_ge(s_sq, i + 1)
                pe.wait_ge(s_sig, 2 * i + 1)
                for a, b in ((0, 512), (512, TA)):
                    mm = pe.matmul(ps[:, a // 512, 0:b - a], c("heads"), kk2[:, a:b], start=True, stop=True)
                mm.then_inc(s_ss, 1)

            for g in range(4):
                channel_tiles(g)
            token_tiles(4)
            lora(0)
            token_tiles(5)
            lora(1)
            token_tiles(6)
            lora(2)
            lora(3)

        @block.scalar
        def _(act):
            link = Link(act, s_a)
            act.wait_ge(s_const, 16 * len(m.consts))
            for ct in range(NCH):
                act.wait_ge(s_item, ct + 1)
                if ct == 0:
                    act.wait_ge(s_v, 1)
                if ct >= 2:
                    act.wait_ge(s_mixed, ct - 1)
                buf = cols[:, ct % 2, :]
                act.activation(buf[:, 1 + NMETA:1 + TP], ps[:, ct % 2, :], ACT.Copy)
                act.activation(buf[:, 1:1 + NMETA], ps[:, 2 + ct % 2, NB:SM], ACT.Copy)
                act.activation(buf[:, 1 + TP:1 + TA], ps[:, 2 + ct % 2, 0:NB], ACT.Copy).then_inc(s_cols, 1)
            act.wait_ge(s_mixed, NCH)
            act.activation(xwa[0:DH, :], xwa[0:DH, :], ACT.Tanh).then_inc(s_tanh, 1)
            act.activation(m.sg[:, :], xg[:, :], ACT.Sigmoid).then_inc(s_tanh, 1)

            def evac_transposes(n):
                act.wait_ge(s_tr, n + 1)
                tt = n % 5
                src = ps[:, 6 + n % 2, :].rearrange("p (h t) -> p h t", h=NH)
                if n < 4:
                    ins = act.activation(m.qT[:, :, tt * P:(tt + 1) * P], src, ACT.Copy)
                elif n == 4:
                    ins = act.activation(m.qTs[:, :, :], src[:, :, 0:NB], ACT.Copy)
                elif tt < NT:
                    ins = act.activation(m.kT[:, :, NMETA + tt * P:NMETA + (tt + 1) * P], src, ACT.Copy)
                else:
                    ins = act.activation(m.kT[:, :, 0:NMETA], src[:, :, NB:SM], ACT.Copy)
                ins.then_inc(s_trc, 1)

            def factors(i):
                act.wait_ge(s_lora, i + 1)
                if i >= 1:
                    act.wait_ge(s_Eu, 2 * i)
                z = ps[:, 0:2, :].rearrange("p a b -> p (a b)")[:, 0:TA]
                za = ps[:, 2:4, :].rearrange("p a b -> p (a b)")[:, 0:TA]
                act.activation(sgm[:, :], z, ACT.Sigmoid, bias=par("w0", i)).then_inc(s_sig, 1)
                act.activation(am[:, :], za, ACT.Sigmoid, bias=par("a0", i)).then_inc(s_sig, 1)
                act.wait_ge(s_ss, i + 1)
                act.activation(kk2[:, :], z, ACT.Sqrt).then_inc(s_rn, 1)
                act.wait_ge(s_L, i + 1)
                act.activation(E[:, :], L[:, :], ACT.Exp)
                act.activation(Ei[:, :], L[:, :], ACT.Exp, scale=-1.0)
                act.activation(Lp[:, :], Lp[:, :], ACT.Exp).then_inc(s_E, 1)

            for n in range(4):
                evac_transposes(n)
            factors(0)
            for n in range(4, 9):
                evac_transposes(n)
            factors(1)
            for tt in range(NT + 1):
                rows = P if tt < NT else SM
                act.wait_ge(s_item, 24 + tt + 1)
                act.activation(m.vtok[0:rows, tt, :], ps[0:rows, 4 + tt % 2, :], ACT.Copy).then_inc(s_val, 1)
                if tt == 0:
                    evac_transposes(9)
            factors(2)
            factors(3)

        @block.vector
        def _(dve):
            link = Link(dve, s_v)
            link(dve.memset(cols[:, :, 0:1], 0.0))
            link(dve.memset(m.zero[:, :], 0.0))
            dve.wait_ge(s_const, 16 * len(m.consts))
            link(dve.tensor_scalar(m.omka[:, :], m.params[:, PAR["k_a"]:PAR["k_a"] + HP], -1.0, 1.0, ALU.mult, ALU.add))
            link(dve.tensor_scalar(m.idx[:, :], m.pt[:, :], float(PAGE), c("rowid"), ALU.mult, ALU.add))
            dests = [rraw[:, i, :] for i in range(HP)] + [kraw[:, i, :] for i in range(HP)] + \
                    [m.vT[:, i, :] for i in range(HP)] + [xwa[:, :], xg[:, :]]
            for ct in range(NCH):
                dve.wait_ge(s_cols, ct + 1)
                buf, d = cols[:, ct % 2, :], diff[:, ct % 2, :]
                dve.tensor_tensor(d[:, 0:TP], buf[:, 0:TP], buf[:, 1:1 + TP], ALU.subtract)
                dve.tensor_copy(m.shout[:, ct, :], buf[:, TP:1 + TA])
                link(dve.tensor_tensor(d[:, TP:TA], m.shift0[:, ct, :], buf[:, 1 + TP:1 + TA], ALU.subtract))
                link(dve.scalar_tensor_tensor(dests[ct], d, par("mu", ct), buf[:, 1:1 + TA], ALU.mult, ALU.add), s_mixed)

            def rope(n):
                tt = n % 5
                rows = P if tt < NT else SM
                dve.wait_ge(s_item, 14 + n + 1)
                if n >= 3:
                    dve.wait_ge(s_tr, n - 2)
                    if n - 3 >= 5 and (n - 3) % 5 < NT:
                        dve.wait_ge(s_rot_out[n % 3], 16 * sum(1 for q in range(5, n - 2) if q % 3 == n % 3 and q % 5 < NT))
                x = ps[0:rows, 4 + n % 2, :].rearrange("p (g f) -> p g f", f=DH)
                out = rot[:, n % 3, :] if tt < NT else m.qks[0:SM, n // 5, :]
                cs = c("cos")[0:rows, tt * DH:(tt + 1) * DH].unsqueeze(1).broadcast_to([rows, 8, DH])
                sn = c("sin")[0:rows, tt * DH:(tt + 1) * DH].unsqueeze(1).broadcast_to([rows, 8, DH])
                t = rtmp[0:rows, :].rearrange("p (g f) -> p g f", f=DH)
                u = rtmp2[0:rows, :].rearrange("p (g f) -> p g f", f=DH)
                dve.tensor_tensor(t, x, cs, ALU.mult)
                dve.tensor_tensor(u[:, :, 0:32], x[:, :, 32:64], sn[:, :, 0:32], ALU.mult)
                link(dve.tensor_tensor(u[:, :, 32:64], x[:, :, 0:32], sn[:, :, 32:64], ALU.mult))
                link(dve.tensor_tensor(out, rtmp[0:rows, :], rtmp2[0:rows, :], ALU.add), s_rope)

            def squares(i):
                if i >= 1:
                    dve.wait_ge(s_ss, i)
                link(dve.tensor_scalar(kk[:, :], kraw[:, i, :], par("k_k", i), None, ALU.mult))
                link(dve.tensor_tensor(kk2[:, :], kk[:, :], kk[:, :], ALU.mult), s_sq)

            def factors(i):
                dve.wait_ge(s_sig, 2 * i + 2)
                link(dve.tensor_scalar(sgm[:, :], sgm[:, :], -math.exp(-0.5), None, ALU.mult))
                link(dve.tensor_tensor_scan(L[:, :], c("start"), sgm[:, :], 0.0, ALU.mult, ALU.add))
                link(dve.tensor_tensor(Lp[:, :], L[:, :], sgm[:, :], ALU.subtract), s_L)
                link(dve.tensor_scalar(sgm[:, :], am[:, :], par("k_a", i), m.omka[:, i:i + 1], ALU.mult, ALU.add))
                link(dve.tensor_tensor(kraw[:, i, :], kraw[:, i, :], sgm[:, :], ALU.mult), s_Eu)
                dve.wait_ge(s_rn, i + 1)
                link(dve.tensor_scalar(kk2[:, :], kk2[:, :], 1e-12, None, ALU.max))
                link(dve.reciprocal(kk2[:, :], kk2[:, :]))
                link(dve.tensor_tensor(kk[:, :], kk[:, :], kk2[:, :], ALU.mult))
                dve.wait_ge(s_E, i + 1)
                link(dve.scalar_tensor_tensor(m.rk[:, i, :], rraw[:, i, :], par("r_k", i), kraw[:, i, :], ALU.mult, ALU.mult))
                dve.tensor_tensor(m.ar[:, i, 1, :], rraw[:, i, :], E[:, :], ALU.mult)
                dve.scalar_tensor_tensor(m.ar[:, i, 0, :], kk[:, :], -1.0, Lp[:, :], ALU.mult, ALU.mult)
                dve.tensor_tensor(m.kt[:, i, :], kraw[:, i, :], Ei[:, :], ALU.mult)
                dve.tensor_copy(m.eend[:, i, 0:9], E[:, NMETA - 1:TP:CH])
                dve.tensor_copy(m.eend[:, i, 9:17], E[:, TP:TA])
                link(dve.tensor_tensor(am[:, :], kk[:, :], am[:, :], ALU.mult))
                link(dve.tensor_tensor(m.bt[:, i, :], am[:, :], Ei[:, :], ALU.mult), s_Eu)

            for n in range(5):
                rope(n)
            squares(0)
            factors(0)
            for n in range(5, 10):
                rope(n)
            squares(1)
            factors(1)
            for i in (2, 3):
                squares(i)
                factors(i)


def phase_rwkv(nc, io, m):
    ctx = ExitStack()
    with ctx:
        sb = lambda n, s, dt=F32: ctx.enter_context(nc.sbuf_tensor(n, s, dt))
        sem = lambda n: ctx.enter_context(nc.semaphore("r_" + n))
        ps, c = m.ps, m.c
        tok = sb("tok", [P, 2, 4, RWW])
        msk = sb("msk", [P, 8, 4, P])
        X = sb("X", [P, 2, HP, P])
        XT = sb("XT", [P, 2, HP, P])
        T1 = sb("T1", [P, 2, HP, P])
        AV = sb("AV", [P, RWW])
        U0 = sb("U0", [P, RWW])
        U = sb("U", [P, RWW])
        WT = sb("WT", [P, HP, P])
        St = sb("St", [P, 10, HP, DH])
        stmp = sb("stmp", [P, HP, DH])
        y = sb("y", [P, RWW])
        sq = sb("sq", [P, RWW])
        stat = sb("stat", [P, 4, 8])
        S0 = sb("S0", [P, NB, HP, DH])
        w1, w2 = (msk[:, a:a + 4].rearrange("p a x t -> p (a x t)").rearrange("p (b i v) -> p b i v", b=NB, i=HP) for a in (4, 0))
        KR = 4
        kr = m.mixT[:, HP:2 * HP, :].rearrange("p k n -> p (k n)")[:, 0:KR * RWW].rearrange("p (j n) -> p j n", j=KR)
        free = m.w_out[:, :, :].rearrange("p k n -> p (k n)")[:, HP * 3 * TA:]
        qb = free[:, 0:2 * RWW].rearrange("p (j n) -> p j n", j=2)
        lnw = sb("lnxw", [P, RWW])
        lnb = free[:, 2 * RWW:3 * RWW]

        s_ld, s_st = sem("ld"), sem("st")
        s_tr, s_trc = sem("tr"), sem("trc")
        s_A, s_Am = sem("A"), sem("Am")
        s_A0, s_X = sem("A0"), sem("X")
        s_XT0 = sem("XT0")
        s_T, s_Tc, s_XX = sem("T"), sem("Tc"), sem("XX")
        s_AV, s_AVc, s_UW, s_UWc = sem("AV"), sem("AVc"), sem("UW"), sem("UWc")
        s_U, s_Uc, s_N, s_S = sem("U"), sem("Uc"), sem("N"), sem("S")
        s_Y, s_yc, s_var, s_rs = sem("Y"), sem("yc"), sem("var"), sem("rs")
        s_mix, s_mt, s_mtc = sem("mix"), sem("mt"), sem("mtc")
        s_sp, s_sc = sem("sp"), sem("sc")
        s_sr = sem("sr")
        s_vd = sem("vd")
        s_v, s_a, s_g = sem("v"), sem("a"), sem("g")
        s_kp = sem("kp")
        s_km, s_ks = sem("km"), sem("ks")
        s_qb = [sem(f"qb{i}") for i in range(2)]

        tiles = [(0, NMETA, (2, 4, 8))] + [(NMETA + P * t, P, (2, 4, 8, 16, 32)) for t in range(NT)]
        NTL = len(tiles)
        FSTEPS = 6
        levels_before = [sum(len(t[2]) for t in tiles[:i]) for i in range(NTL)]

        block = ctx.enter_context(nc.Block())

        @block.sync
        def _(sp):
            sp.dma_start(lnw[:, :], io["lnx_w"].partition_broadcast(P)).then_inc(s_ld, 16)
            sp.dma_start(lnb[:, :], io["lnx_b"].partition_broadcast(P)).then_inc(s_ld, 16)
            sp.dma_start(S0[:, :, :, :], io["state"]).then_inc(s_ld, 16)
            for b in range(NB):
                if b >= 2:
                    sp.wait_ge(s_ks, NPG // 2 * (b - 1))
                sp.dma_start(qb[:, b % 2, :], m.q_rows[b, :].partition_broadcast(P)).then_inc(s_qb[b % 2], 16)
            sp.wait_ge(s_sc, 1)
            sp.dma_start(io["wkv_s_out"], S0[:, :, :, :]).then_inc(s_st, 16)
            sp.wait_ge(s_S, 9)
            sp.dma_start(io["wkv_p_out"], St[:, 9, :, :]).then_inc(s_st, 16)
            sp.wait_ge(s_st, 32)

        @block.tensor
        def _(pe):
            def token_major(ti, q):
                p0, n, _ = tiles[ti]
                if 4 * ti + q >= 2:
                    pe.wait_ge(s_trc, 4 * ti + q - 1)
                src = (m.ar[:, :, 0], m.bt, m.kt, m.vT)[q]
                for i in range(HP):
                    mm = pe.transpose(ps[0:n, q % 2, i * P:(i + 1) * P], src[:, i, p0:p0 + n], c("ident"))
                mm.then_inc(s_tr, 1)

            def prepare(ti):
                p0, n, levels = tiles[ti]
                span = slice(p0, p0 + n)
                pe.wait_ge(s_trc, 4 * ti + 4)
                if ti >= 1:
                    pe.wait_ge(s_UWc, 2 * ti)
                for hd in range(8):
                    q, i = hd // 4, hd % 4
                    rows = slice(q * DH, (q + 1) * DH)
                    j = 8 * ti + hd
                    if hd >= 2:
                        pe.wait_ge(s_Am, j - 1)
                    for w, src in enumerate((m.bt, m.kt)):
                        mm = pe.matmul(ps[0:n, hd % 2, w * 2 * n:(w + 1) * 2 * n].rearrange("s (x t) -> s x t", x=2),
                                       src[rows, i, span], m.ar[rows, i, :, span], start=True, stop=True)
                    mm.then_inc(s_A, 1)
                if ti >= 2:
                    transpose_mix(ti - 2, P)
                for q in range(2):
                    rows = slice(q * DH, (q + 1) * DH)
                    if ti >= 1:
                        pe.wait_ge(s_yc, ti)
                    for i in range(HP):
                        mm = pe.matmul(ps[0:n, 4 + q, i * n:(i + 1) * n], m.ar[rows, i, 0, span], m.bt[rows, i, span],
                                       start=True, stop=True)
                    mm.then_inc(s_A0, 1)
                for l in range(len(levels)):
                    at = 2 * (levels_before[ti] + l)
                    for q in range(2):
                        pe.wait_ge(s_X, at + q + 1 + 2 * ti)
                        if l == 0:
                            pe.wait_ge(s_XT0, 2 * ti + q + 1)
                            pe.wait_ge(s_Am, 8 * ti + 8)
                            if ti >= 2:
                                pe.wait_ge(s_mtc, ti - 1)
                        for i in range(HP):
                            mm = pe.matmul(ps[0:n, 2 + q, i * n:(i + 1) * n], msk[0:n, 4 * q + i, 0, 0:n], X[0:n, q, i, 0:n],
                                           start=True, stop=True)
                        mm.then_inc(s_T, 1)
                    for q in range(4):
                        if ti + 1 < NTL and l == min(q, len(levels) - 2):
                            token_major(ti + 1, q)
                    if l == len(levels) - 1:
                        if ti + 1 < NTL:
                            pe.wait_ge(s_trc, 4 * ti + 8)
                        for hd in range(8):
                            h = 2 * (hd % 4) + hd // 4
                            mm = pe.matmul(ps[0:n, 0, h * DH:(h + 1) * DH], msk[0:n, hd, 2, 0:n],
                                           tok[0:n, ti % 2, 3, h * DH:(h + 1) * DH], start=True, stop=True)
                        mm.then_inc(s_AV, 1)
                    for q in range(2):
                        pe.wait_ge(s_Tc, at + q + 1)
                        for i in range(HP):
                            if l < len(levels) - 1:
                                pe.matmul(ps[0:n, 4 + q, i * n:(i + 1) * n], XT[0:n, q, i, 0:n], T1[0:n, q, i, 0:n],
                                          start=True, stop=True)
                            mm = pe.matmul(ps[0:n, 6 + q, i * n:(i + 1) * n], T1[0:n, q, i, 0:n], XT[0:n, q, i, 0:n],
                                           start=True, stop=True)
                        mm.then_inc(s_XX, 1)
                pe.wait_ge(s_X, 2 * (levels_before[ti] + len(levels)) + 2 * ti + 2)
                pe.wait_ge(s_AVc, ti + 1)
                for hd in range(8):
                    q, i = hd // 4, hd % 4
                    h = 2 * i + q
                    mm = pe.matmul(ps[0:n, 1, h * DH:(h + 1) * DH], XT[0:n, q, i, 0:n], AV[0:n, h * DH:(h + 1) * DH],
                                   start=True, stop=True)
                    if ti > 0:
                        mm = pe.matmul(ps[q * DH:(q + 1) * DH, 2, i * P:(i + 1) * P], tok[0:n, ti % 2, 0, h * DH:(h + 1) * DH],
                                       XT[0:n, q, i, 0:n], start=True, stop=True)
                mm.then_inc(s_UW, 1)

            def chain(ti):
                pe.wait_ge(s_UWc, 2 * ti + 2)
                for ch in range(2 if ti else 1):
                    n = CH if ti else NMETA
                    k = 2 * ti - 1 + ch if ti else 0
                    r = slice(ch * CH, ch * CH + n)
                    if ti:
                        pe.wait_ge(s_S, k)
                        for hd in range(8):
                            q, i = hd // 4, hd % 4
                            rows = slice(q * DH, (q + 1) * DH)
                            mm = pe.matmul(ps[r, 2 + q, i * DH:(i + 1) * DH], WT[rows, i, r], St[rows, k, i, :],
                                           start=True, stop=True)
                        mm.then_inc(s_U, 1)
                        pe.wait_ge(s_Uc, k)
                    u = U if ti else U0
                    for hd in range(8):
                        q, i = hd // 4, hd % 4
                        h = 2 * i + q
                        hs = slice(h * DH, (h + 1) * DH)
                        out = ps[q * DH:(q + 1) * DH, 4, i * DH:(i + 1) * DH]
                        pe.matmul(out, tok[r, ti % 2, 1, hs], u[r, hs], start=True, stop=False)
                        mm = pe.matmul(out, tok[r, ti % 2, 2, hs], tok[r, ti % 2, 3, hs], start=False, stop=True)
                    mm.then_inc(s_N, 1)

            def outputs(ti):
                p0 = tiles[ti][0]
                for hd in range(8):
                    q, i = hd // 4, hd % 4
                    h = 2 * i + q
                    hs = slice(h * DH, (h + 1) * DH)
                    rows = slice(q * DH, (q + 1) * DH)
                    for ch in range(2):
                        k = 2 * ti - 1 + ch
                        pe.matmul(ps[ch * CH:(ch + 1) * CH, 6 + q, i * DH:(i + 1) * DH],
                                  m.ar[rows, i, 1, p0 + ch * CH:p0 + (ch + 1) * CH], St[rows, k, i, :],
                                  start=True, stop=False, skip_group_check=True)
                    pe.matmul(ps[:, 6 + q, i * DH:(i + 1) * DH], msk[:, hd, 3, :], tok[:, ti % 2, 3, hs],
                              start=False, stop=False, skip_group_check=True)
                    pe.matmul(ps[:, 6 + q, i * DH:(i + 1) * DH], msk[:, hd, 1, :], U[:, hs],
                              start=False, stop=True, skip_group_check=True)
                gate(slice(p0, p0 + P), P)

            def gate(span, n):
                pe.matmul(ps[0:n, 2, :], m.sg[:, span], m.g2[:, :], start=True, stop=True)
                for i in range(HP):
                    mm = pe.matmul(ps[0:n, 3, 2 * i:2 * i + 2], m.rk[:, i, span], c("half"), start=True, stop=True)
                mm.then_inc(s_Y, 1)

            def transpose_mix(ti, n):
                pe.wait_ge(s_mix, ti + 1)
                for i in range(HP):
                    mm = pe.transpose(ps[:, 2, i * P:i * P + n], y[0:n, i * P:(i + 1) * P], c("ident")[0:n, 0:n])
                mm.then_inc(s_mt, 1)

            for q in range(4):
                token_major(0, q)
            for ti in range(NTL):
                prepare(ti)
                chain(ti)
                if ti:
                    outputs(ti)

            def sums(src, bank):
                for j in range(4):
                    mm = pe.matmul(ps[:, bank + j, :], c("heads"), src[:, 2 * j:2 * j + 2].rearrange("p a i v -> p (a i v)"),
                                   start=True, stop=True)
                mm.then_inc(s_sp, 1)

            pe.wait_ge(s_sr, 1)
            sums(w1, 4)
            transpose_mix(NT - 1, P)
            pe.wait_ge(s_mtc, NT)
            pe.wait_ge(s_vd, 1)
            sums(w2, 0)
            pe.wait_ge(s_sr, 2)
            for h in range(2):
                for b in range(NB):
                    at = h * (2 * NB - 1) + NB - 1 - b
                    mm = pe.matmul(ps[0:NB, 4 + h, 0:HP * DH], c("pick")[:, at:at + NB], w1[:, b].rearrange("p i v -> p (i v)"),
                                   start=(b == 0), stop=(b == NB - 1))
            mm.then_inc(s_sp, 1)
            for i in range(HP):
                mm = pe.transpose(ps[0:NB, 1, i * P:(i + 1) * P], m.vT[:, i, TP:TA], c("ident"))
            mm.then_inc(s_sp, 1)
            gate(slice(TP, TA), NB)
            transpose_mix(NT, NB)

        @block.scalar
        def _(act):
            def mixed(ti):
                act.wait_ge(s_var, ti)
                act.activation(stat[:, 2, :], stat[:, 1, :], ACT.Sqrt).then_inc(s_rs, 1)
                act.wait_ge(s_mt, ti)
                act.activation(m.mixT[:, 0:HP, (ti - 1) * P:ti * P], ps[:, 2, :].rearrange("p (i t) -> p i t", i=HP),
                               ACT.Copy).then_inc(s_mtc, 1)

            def token_major(ti):
                n = tiles[ti][1]
                for q in range(4):
                    act.wait_ge(s_tr, 4 * ti + q + 1)
                    act.activation(tok[0:n, ti % 2, q, :], ps[0:n, q % 2, :], ACT.Copy).then_inc(s_trc, 1)

            token_major(0)
            for ti in range(NTL):
                n = tiles[ti][1]
                if ti >= 2:
                    mixed(ti - 1)
                if ti + 1 < NTL:
                    token_major(ti + 1)
                act.wait_ge(s_AV, ti + 1)
                act.activation(AV[0:n, :], ps[0:n, 0, :], ACT.Copy).then_inc(s_AVc, 1)
                act.wait_ge(s_UW, ti + 1)
                if ti:
                    act.activation(WT[:, :, :], ps[:, 2, :].rearrange("p (i t) -> p i t", i=HP), ACT.Copy).then_inc(s_UWc, 1)
                else:
                    act.activation(stmp[:, 0, 0:1], c("ident")[:, 0:1], ACT.Copy).then_inc(s_UWc, 1)
            mixed(NT)
            act.wait_ge(s_var, NT + 1)
            act.activation(stat[0:NB, 2, :], stat[0:NB, 1, :], ACT.Sqrt).then_inc(s_rs, 1)
            act.wait_ge(s_mt, NT + 1)
            act.activation(m.mixT[:, 0:HP, SEQ:SEQ + NB], ps[:, 2, :].rearrange("p (i t) -> p i t", i=HP)[:, :, 0:NB],
                           ACT.Copy).then_inc(s_mtc, 1)

        @block.gpsimd
        def _(pool):
            def score(v):
                if v:
                    pool.wait_ge(s_ks, KR // 2 * v)
                for k in range(KR):
                    j = KR * v + k
                    pool.indirect_dma_start(out=kr[:, k, :], out_offset=None, in_=io["cache_k"],
                                            in_offset=bass.IndirectOffsetOnAxis(ap=m.idx[:, j:j + 1], axis=0)
                                            ).then_inc(s_kp, 16)
                b = KR * v // NPG
                pool.wait_ge(s_qb[b % 2], 16 * (b // 2 + 1))
                pool.wait_ge(s_kp, 16 * KR * (v + 1))
                for k in range(KR):
                    ins = pool.tensor_tensor(kr[:, k, :], kr[:, k, :], qb[:, b % 2, :], ALU.mult)
                ins.then_inc(s_km, 1)

            for ti in range(NTL):
                n = tiles[ti][1]
                if ti:
                    score(4 * ti - 4)
                for q in range(2):
                    pool.wait_ge(s_Am, 8 * ti + 4 * q + 4)
                    if ti:
                        pool.wait_ge(s_UW, ti)
                    pool.tensor_tensor(XT[0:n, q, :, 0:n], msk[0:n, 4 * q:4 * q + 4, 0, 0:n],
                                       c("firstT")[0:n, 0:n].unsqueeze(1).broadcast_to([n, 4, n]), ALU.mult).then_inc(s_g, 1)
                    pool.wait_ge(s_g, 2 * ti + q + 1)
                    pool.tensor_tensor(XT[0:n, q, :, 0:n], XT[0:n, q, :, 0:n],
                                       c("ident")[0:n, 0:n].unsqueeze(1).broadcast_to([n, 4, n]), ALU.add).then_inc(s_XT0, 1)
                if ti:
                    for v in range(4 * ti - 3, 4 * ti):
                        score(v)
            pool.wait_ge(s_Y, NT)
            for b in range(NB):
                ins = pool.tensor_tensor(w2[:, b], c("diag64").unsqueeze(1).broadcast_to([P, HP, DH]),
                                         m.vT[:, :, TP + b:TP + b + 1].broadcast_to([P, HP, DH]), ALU.mult)
            ins.then_inc(s_vd, 1)

        @block.vector
        def _(dve):
            link = Link(dve, s_v)
            dve.wait_ge(s_ld, 48)

            def four(t):
                return t.unsqueeze(1).broadcast_to([t.shape[0], HP, t.shape[1]])

            def sum_scores(j):
                b, g = divmod(2 * j, NPG)
                k = 2 * j % KR
                if k == 0:
                    dve.wait_ge(s_km, 2 * j // KR + 1)
                dve.tensor_reduce(m.sc[:, g:g + 2, b * 8:(b + 1) * 8], kr[:, k:k + 2, :].rearrange("p g (x d) -> p g x d", d=DH),
                                  AX.X, ALU.add).then_inc(s_ks, 1)

            def prepare(ti):
                p0, n, levels = tiles[ti]
                for hd in range(8):
                    dve.wait_ge(s_A, 8 * ti + hd + 1)
                    dve.tensor_tensor(msk[0:n, hd, :, 0:n], ps[0:n, hd % 2, 0:4 * n].rearrange("s (x t) -> s x t", x=4),
                                      c("mask4")[0:n].rearrange("s (x t) -> s x t", x=4)[:, :, 0:n], ALU.mult).then_inc(s_Am, 1)
                    if ti >= 2 and hd < FSTEPS:
                        finish(ti - 2, P, values_of(ti - 1), hd)
                if ti:
                    for j in range(2):
                        sum_scores(8 * (ti - 1) + j)
                for q in range(2):
                    dve.wait_ge(s_A0, 2 * ti + q + 1)
                    link(dve.tensor_tensor(X[0:n, q, :, 0:n], ps[0:n, 4 + q, 0:4 * n].rearrange("s (x t) -> s x t", x=4),
                                           four(c("first")[0:n, 0:n]), ALU.mult))
                    link(dve.tensor_tensor(X[0:n, q, :, 0:n], X[0:n, q, :, 0:n], four(c("ident")[0:n, 0:n]), ALU.add), s_X)
                for l, lev in enumerate(levels):
                    at = 2 * (levels_before[ti] + l)
                    for q in range(2):
                        dve.wait_ge(s_T, at + q + 1)
                        link(dve.tensor_tensor(T1[0:n, q, :, 0:n], ps[0:n, 2 + q, 0:4 * n].rearrange("s (x t) -> s x t", x=4),
                                               four(c(f"lev{lev}")[0:n, 0:n]), ALU.mult), s_Tc)
                    if ti and l in (1, 2, 4):
                        sum_scores(8 * (ti - 1) + {1: 2, 2: 3, 4: 4}[l])
                    for q in range(2):
                        dve.wait_ge(s_XX, at + q + 1)
                        if l < len(levels) - 1:
                            dve.tensor_tensor(X[0:n, q, :, 0:n], ps[0:n, 4 + q, 0:4 * n].rearrange("s (x t) -> s x t", x=4),
                                              X[0:n, q, :, 0:n], ALU.add)
                        link(dve.tensor_tensor(XT[0:n, q, :, 0:n], ps[0:n, 6 + q, 0:4 * n].rearrange("s (x t) -> s x t", x=4),
                                               XT[0:n, q, :, 0:n], ALU.add), s_X)
                dve.wait_ge(s_UW, ti + 1)
                link(dve.tensor_copy(U0[0:n, :], ps[0:n, 1, :]), s_UWc)
                if ti:
                    sum_scores(8 * (ti - 1) + 5)

            def chain(ti):
                for ch in range(2 if ti else 1):
                    k = 2 * ti - 1 + ch if ti else 0
                    r = slice(ch * CH, (ch + 1) * CH)
                    if ti:
                        dve.wait_ge(s_U, k)
                        view = lambda t: t[r, :].rearrange("s (i h v) -> s h i v", h=2, v=DH)
                        link(dve.tensor_tensor(view(U), ps[r, 2:4, 0:HP * DH].rearrange("s h (i v) -> s h i v", i=HP),
                                               view(U0), ALU.add), s_Uc)
                    dve.wait_ge(s_N, k + 1)
                    new = ps[:, 4, 0:HP * DH].rearrange("p (i v) -> p i v", i=HP)
                    if ti:
                        link(dve.tensor_tensor(stmp[:, :, :], new, St[:, k, :, :], ALU.add))
                        new = stmp[:, :, :]
                    link(dve.tensor_tensor(St[:, k + 1, :, :], new, m.eend[:, :, k:k + 1].broadcast_to([P, HP, DH]), ALU.mult), s_S)

            values_of = lambda ti: tok[:, ti % 2, 3, :].rearrange("s (h v) -> s h v", v=DH)

            def finish(ti, n, vals, step):
                y3, sq3 = (t[0:n, :].rearrange("s (h v) -> s h v", v=DH) for t in (y, sq))
                per = lambda j: stat[0:n, j, :].unsqueeze(2).broadcast_to([n, 8, DH])
                if step == 0:
                    link(dve.tensor_reduce(stat[0:n, 0, :], y3, AX.X, ALU.add))
                    link(dve.tensor_scalar(stat[0:n, 0, :], stat[0:n, 0, :], 1.0 / DH, None, ALU.mult))
                    link(dve.tensor_tensor(y3, y3, per(0), ALU.subtract))
                if step == 1:
                    link(dve.tensor_tensor(sq[0:n, :], y[0:n, :], y[0:n, :], ALU.mult))
                    link(dve.tensor_reduce(stat[0:n, 1, :], sq3, AX.X, ALU.add))
                    link(dve.tensor_scalar(stat[0:n, 1, :], stat[0:n, 1, :], 1.0 / DH, 64e-5, ALU.mult, ALU.add), s_var)
                if step == 2:
                    dve.wait_ge(s_rs, ti + 1)
                    link(dve.reciprocal(stat[0:n, 3, :], stat[0:n, 2, :]))
                    link(dve.tensor_tensor(y3, y3, per(3), ALU.mult))
                if step == 3:
                    link(dve.tensor_tensor(y[0:n, :], y[0:n, :], lnw[0:n, :], ALU.mult))
                    link(dve.tensor_tensor(y[0:n, :], y[0:n, :], lnb[0:n, :], ALU.add))
                if step == 4:
                    link(dve.tensor_copy(stat[0:n, 0, :], ps[0:n, 3, 0:8]))
                    link(dve.tensor_tensor(sq3, vals, per(0), ALU.mult))
                if step == 5:
                    link(dve.tensor_tensor(y[0:n, :], y[0:n, :], sq[0:n, :], ALU.add))
                    link(dve.tensor_tensor(y[0:n, :], y[0:n, :], ps[0:n, 2, :], ALU.mult), s_mix)

            for ti in range(NTL):
                prepare(ti)
                chain(ti)
                if ti:
                    for j in (6, 7):
                        sum_scores(8 * (ti - 1) + j)
                    dve.wait_ge(s_Y, ti)
                    if ti >= 2:
                        dve.wait_ge(s_mt, ti - 1)
                    link(dve.tensor_copy(y[:, :].rearrange("s (i h v) -> s h i v", h=2, v=DH),
                                         ps[:, 6:8, 0:HP * DH].rearrange("s h (i v) -> s h i v", i=HP)), s_yc)
                else:
                    link(dve.memset(stat[:, :, :], 0.0), s_yc)
            def halves(f):
                for b in range(NB):
                    last = f(b)
                return last

            def col(t, b):
                return t[:, :, b:b + 1].broadcast_to([P, HP, DH])

            al, rr = m.ar[:, :, 0, TP:TA], m.ar[:, :, 1, TP:TA]
            bb, kk = m.bt[:, :, TP:TA], m.kt[:, :, TP:TA]
            psv = lambda b, bank: ps[:, bank + b // 2, (b % 2) * HP * DH:(b % 2 + 1) * HP * DH].rearrange("p (i v) -> p i v", i=HP)
            link(halves(lambda b: dve.tensor_tensor(w1[:, b], S0[:, b], col(al, b), ALU.mult)), s_sr)
            for step in range(FSTEPS):
                finish(NT - 1, P, values_of(NT), step)
            dve.wait_ge(s_sp, 1)
            link(halves(lambda b: dve.tensor_tensor(w1[:, b], psv(b, 4), col(bb, b), ALU.mult)))
            link(halves(lambda b: dve.tensor_tensor(S0[:, b], S0[:, b], w1[:, b], ALU.add)))
            dve.wait_ge(s_sp, 2)
            link(halves(lambda b: dve.tensor_tensor(w1[:, b], psv(b, 0), col(kk, b), ALU.mult)))
            link(halves(lambda b: dve.tensor_tensor(S0[:, b], S0[:, b], w1[:, b], ALU.add)))
            link(halves(lambda b: dve.tensor_tensor(w1[:, b], S0[:, b], col(rr, b), ALU.mult)), s_sr)
            link(halves(lambda b: dve.tensor_tensor(S0[:, b], S0[:, b], col(m.eend[:, :, 9:17], b), ALU.mult)), s_sc)
            dve.wait_ge(s_sp, 4)
            dve.wait_ge(s_mt, NT)
            link(dve.tensor_copy(y[0:NB, :].rearrange("s (i h v) -> s h i v", h=2, v=DH),
                                 ps[0:NB, 4:6, 0:HP * DH].rearrange("s h (i v) -> s h i v", i=HP)))
            link(dve.tensor_copy(U0[0:NB, :], ps[0:NB, 1, :]))
            dve.wait_ge(s_Y, NT + 1)
            for step in range(FSTEPS):
                finish(NT, NB, U0[0:NB, :].rearrange("s (h v) -> s h v", v=DH), step)


def phase_attention(nc, io, m):
    ctx = ExitStack()
    with ctx:
        sb = lambda n, s, dt=F32: ctx.enter_context(nc.sbuf_tensor("t_" + n, s, dt))
        sem = lambda n: ctx.enter_context(nc.semaphore("t_" + n))
        ps, c = m.ps, m.c
        RING = 3
        SCALE = DH ** -0.5
        ring = sb("ring", [P, RING, NPG, RWW])
        idx, sc = m.idx, m.sc
        qk = sb("qk", [NB, RWW])
        qks = sb("qks2", [NB, 8])
        qkd = sb("qkd", [NB, NB, 8])
        attN = sb("attN", [NB, NB * NH])
        attD = sb("attD", [NB, NB, NH])
        lam4 = sb("lam4", [P, 4, DH])
        lamj = sb("lamj", [P, DH])
        lam2 = sb("lam2", [P, 2])
        nlam = sb("nlam", [P, 1])
        subw = sb("subw", [P, RWW])
        pr = sb("pr", [P, 2, TP])
        att = sb("att", [P, TP])
        attT = sb("attT", [P, NT + 1, P])
        mx = sb("mx", [P, 2])
        Z = sb("Z", [P, 2])
        rz = sb("rz", [P, 2])
        o = sb("o", [P, RWW])
        osq = sb("osq", [P, RWW])
        ost = sb("ost", [P, 3, NH])
        PT = sb("PT", [NB * 8, PAST + 1])
        sst = sb("sst", [NB * 8, 8])
        attS = sb("attS", [P, NPG, NB * NH])
        attB = m.kt[:, :, :].rearrange("p i t -> p (i t)")[:, 0:NB * NPG * NB * NH].rearrange("p (b g r) -> p b g r", b=NB, g=NPG)
        osum = sb("osum", [NB * NH, RWW])

        s_ld = sem("ld")
        s_k = [sem(f"k{i}") for i in range(RING)]
        s_nk = sem("nk")
        s_use = sem("use")
        s_lam, s_lame = sem("lam"), sem("lame")
        s_sc, s_mx, s_ex = sem("sc"), sem("mx"), sem("ex")
        s_at, s_tr, s_trc, s_pv = sem("at"), sem("tr"), sem("trc"), sem("pv")
        s_oc, s_ms, s_rs, s_on, s_ot, s_otc = sem("oc"), sem("ms"), sem("rs"), sem("on"), sem("ot"), sem("otc")
        s_st, s_smx, s_sex, s_sP, s_sT, s_sA = (sem(n) for n in ("st2", "smx", "sex", "sP", "sT", "sA"))
        s_so, s_soc = sem("so"), sem("soc")
        s_v, s_a = sem("v"), sem("a")
        NQ = NT * NH
        width = lambda t: NMETA + P * (t + 1)

        block = ctx.enter_context(nc.Block())

        @block.sync
        def _(sp):
            sp.dma_start(lam4[:, :, :], io["lams"].partition_broadcast(P)).then_inc(s_ld, 16)
            sp.dma_start(subw[:, :], io["subln_w"].partition_broadcast(P)).then_inc(s_ld, 16)
            sp.dma_start(m.w_out[:, :, :], io["w_out"].rearrange("(k p) n -> p k n", p=P)).then_inc(m.s_wout, 16)

        @block.gpsimd
        def _(pool):
            for b in range(NB):
                if b >= RING:
                    pool.wait_ge(s_use, b - RING + 1)
                for g in range(NPG):
                    pool.indirect_dma_start(
                        out=ring[:, b % RING, g, :], out_offset=None, in_=io["cache_v"],
                        in_offset=bass.IndirectOffsetOnAxis(ap=idx[:, b * NPG + g:b * NPG + g + 1], axis=0),
                    ).then_inc(s_k[b % RING], 16)

        def landed(eng, j):
            eng.wait_ge(s_k[j % RING], 16 * NPG * (j // RING + 1))

        @block.tensor
        def _(pe):
            def scores(n):
                t, h = divmod(n, NH)
                w = width(t)
                for x in range(2):
                    if n >= 1:
                        pe.wait_ge(s_ex, 2 * n + x - 1)
                    rows = slice(x * DH, (x + 1) * DH)
                    out = ps[:, 2 * x:2 * x + 2, :].rearrange("p a b -> p (a b)")
                    cuts = [(0, min(w, 512))] + ([(512, w)] if w > 512 else [])
                    for a, b in cuts:
                        pe.matmul(out[:, a:b], m.qT[rows, h, t * P:(t + 1) * P], m.kT[rows, h, a:b],
                                  start=True, stop=False)
                        lo = max(a, w - P)
                        mm = pe.matmul(out[:, lo:b], c("ident"), c("causal")[:, lo - (w - P):b - (w - P)],
                                       start=False, stop=True)
                    mm.then_inc(s_sc, 1)

            def values(n):
                t, h = divmod(n, NH)
                hs = slice(h * DV, (h + 1) * DV)
                pe.wait_ge(s_at, n + 1)
                if n >= 1:
                    pe.wait_ge(s_trc, n)
                if n > NH and h == 1:
                    pe.wait_ge(s_otc, t)
                for j in range(t + 1):
                    pe.transpose(ps[:, 4, j * P:(j + 1) * P], att[:, NMETA + j * P:NMETA + (j + 1) * P], c("ident"))
                pe.transpose(ps[0:NMETA, 5, 0:P], att[:, 0:NMETA], c("ident")).then_inc(s_tr, 1)

            def weigh(n):
                t, h = divmod(n, NH)
                hs = slice(h * DV, (h + 1) * DV)
                pe.wait_ge(s_trc, n + 1)
                if h == 0 and t:
                    pe.wait_ge(s_oc, t)
                pe.matmul(ps[:, 6, hs], attT[0:NMETA, NT, :], m.vmeta[:, hs], start=True, stop=False)
                for j in range(t + 1):
                    mm = pe.matmul(ps[:, 6, hs], attT[:, j, :], m.vtok[:, j, hs], start=False, stop=(j == t))
                mm.then_inc(s_pv, 1)

            def transpose_out(t, n):
                pe.wait_ge(s_on, t + 1)
                pe.wait_ge(s_trc, min(NH * (t + 1) + 1, NQ))
                for i in range(NH):
                    mm = pe.transpose(ps[:, 5, i * P:i * P + n], o[0:n, i * P:(i + 1) * P], c("ident")[0:n, 0:n])
                mm.then_inc(s_ot, 1)

            def sample_scores():
                pe.wait_ge(s_nk, 1)
                for g in range(NPG):
                    pe.transpose(ps[0:NB * 8, g // 4, (g % 4) * P:(g % 4 + 1) * P], sc[:, g, :], c("ident"))
                pe.matmul(ps[0:NB * 8, 2, 0:1], qkd[:, :, :].rearrange("r b x -> r (b x)"), c("heads")[0:NB, 0:1],
                          start=True, stop=True).then_inc(s_st, 1)
                pe.wait_ge(s_sP, 1)
                for g in range(NPG):
                    pe.transpose(ps[:, 3, g * NB * 8:(g + 1) * NB * 8], PT[:, g * P:(g + 1) * P], c("ident")[0:NB * 8, 0:NB * 8])
                pe.matmul(ps[0:NB, 7, 0:NB * 8], PT[:, PAST:PAST + 1].broadcast_to([NB * 8, NB]), c("ident")[0:NB * 8, 0:NB * 8],
                          start=True, stop=True).then_inc(s_sT, 1)
                pe.wait_ge(s_sA, 1)

            def sample_values(n):
                b = n // 2
                if n % 2 == 0:
                    landed(pe, b)
                for g in range(n % 2 * NPG // 2, (n % 2 + 1) * NPG // 2):
                    mm = pe.matmul(ps[0:NB * NH, 7, :], attB[:, b, g, :], ring[:, b % RING, g, :],
                                   start=(b == 0 and g == 0), stop=False)
                if n % 2 == 1:
                    mm.then_inc(s_use, 1)

            def project(a):
                if a == 0:
                    pe.wait_ge(m.s_wout, 16)
                    pe.wait_ge(s_otc, 1)
                    pe.wait_ge(s_ex, 2 * NQ)
                for k in range(KT):
                    mm = pe.matmul(ps[:, a, :], m.mixT[:, k, 0:P], m.w_out[:, k, a * 512:(a + 1) * 512],
                                   start=(k == 0), stop=(k == KT - 1))
                mm.then_inc(m.s_op, 1)

            sample_scores()
            scores(0)
            for n in range(NQ):
                if n + 1 < NQ:
                    scores(n + 1)
                if n >= 1:
                    weigh(n - 1)
                values(n)
                if n % NH == 0 and n:
                    transpose_out(n // NH - 1, P)
                sample_values(n)
            pe.matmul(ps[0:NB * NH, 7, :], attD[:, :, :].rearrange("r b h -> r (b h)"), m.vtok[0:NB, NT, :],
                      start=False, stop=True).then_inc(s_so, 1)
            weigh(NQ - 1)
            project(0)
            transpose_out(NT - 1, P)
            pe.wait_ge(s_soc, 1)
            pe.matmul(ps[0:NB, 7, :], c("rows4")[0:NB * NH], osum[:, :], start=True, stop=True).then_inc(s_pv, 1)
            project(1)
            pe.wait_ge(s_otc, NT)
            transpose_out(NT, NB)

        @block.scalar
        def _(act):
            act.wait_ge(s_lam, 1)
            act.activation(lam2[:, :], lam2[:, :], ACT.Exp).then_inc(s_lame, 1)

            def root(t, n):
                act.wait_ge(s_ms, t + 1)
                act.activation(ost[0:n, 1, :], ost[0:n, 0, :], ACT.Sqrt).then_inc(s_rs, 1)

            def mixed(t, n):
                act.wait_ge(s_ot, t + 1)
                act.activation(m.mixT[:, HP:2 * HP, t * P:t * P + n], ps[:, 5, :].rearrange("p (i t) -> p i t", i=NH)[:, :, 0:n],
                               ACT.Copy).then_inc(s_otc, 1)

            act.wait_ge(s_smx, 1)
            act.activation(PT[:, 0:PAST], ps[0:NB * 8, 0:2, :].rearrange("p a b -> p (a b)"), ACT.Exp,
                           bias=sst[:, 2:3], scale=SCALE, accum_out=sst[:, 3:4])
            act.activation(PT[:, PAST:PAST + 1], ps[0:NB * 8, 2, 0:1], ACT.Exp, bias=sst[:, 2:3], scale=SCALE).then_inc(s_sex, 1)
            for n in range(NQ):
                t, h = divmod(n, NH)
                w = width(t)
                if n >= 1:
                    act.wait_ge(s_at, n)
                for x in range(2):
                    act.wait_ge(s_mx, 2 * n + x + 1)
                    act.activation(pr[:, x, 0:w], ps[:, 2 * x:2 * x + 2, :].rearrange("p a b -> p (a b)")[:, 0:w],
                                          ACT.Exp, bias=mx[:, x:x + 1], scale=SCALE,
                                   accum_out=Z[:, x:x + 1]).then_inc(s_ex, 1)
                act.wait_ge(s_tr, n + 1)
                if n >= 1:
                    act.wait_ge(s_pv, n)
                act.activation(attT[:, 0:t + 1, :], ps[:, 4, 0:(t + 1) * P].rearrange("p (j q) -> p j q", q=P), ACT.Copy)
                act.activation(attT[0:NMETA, NT, :], ps[0:NMETA, 5, 0:P], ACT.Copy).then_inc(s_trc, 1)
                if h == 0 and t:
                    root(t - 1, P)
                    mixed(t - 1, P)
            root(NT - 1, P)
            mixed(NT - 1, P)
            root(NT, NB)
            mixed(NT, NB)

        @block.vector
        def _(dve):
            link = Link(dve, s_v)
            dve.memset(attB[:, :, :, :], 0.0)
            link(dve.tensor_tensor(qk[:, :], m.qks[0:NB, 0, :], m.qks[0:NB, 1, :], ALU.mult))
            link(dve.tensor_reduce(qks[:, :], qk[:, :].rearrange("p (x d) -> p x d", d=DH), AX.X, ALU.add))
            own = c("one8")[0:NB].unsqueeze(2)
            link(dve.tensor_tensor(qkd[:, :, :], qks[:, :].unsqueeze(1).broadcast_to([NB, NB, 8]), own.broadcast_to([NB, NB, 8]),
                                   ALU.mult), s_nk)
            dve.wait_ge(s_ld, 32)
            for a in range(2):
                link(dve.tensor_tensor(lamj[:, :], lam4[:, 2 * a, :], lam4[:, 2 * a + 1, :], ALU.mult))
                ins = dve.tensor_reduce(lam2[:, a:a + 1], lamj[:, :], AX.X, ALU.add)
                link(ins, s_lam if a else None)
            dve.wait_ge(s_lame, 1)
            link(dve.tensor_tensor(nlam[:, :], lam2[:, 1:2], lam2[:, 0:1], ALU.subtract))
            link(dve.tensor_scalar(nlam[:, :], nlam[:, :], -LAM_INIT, None, ALU.add))
            link(dve.tensor_scalar(subw[:, :], subw[:, :], 1.0 - LAM_INIT, None, ALU.mult))

            def soft(n):
                t, h = divmod(n, NH)
                w = width(t)
                for x in range(2):
                    dve.wait_ge(s_sc, 2 * n + x + 1)
                    link(dve.tensor_reduce(mx[:, x:x + 1], ps[:, 2 * x:2 * x + 2, :].rearrange("p a b -> p (a b)")[:, 0:w],
                                           AX.X, ALU.max))
                    link(dve.tensor_scalar(mx[:, x:x + 1], mx[:, x:x + 1], -SCALE, None, ALU.mult), s_mx)

            def combine(n):
                t, h = divmod(n, NH)
                w = width(t)
                dve.wait_ge(s_ex, 2 * n + 2)
                if n >= 1:
                    dve.wait_ge(s_tr, n)
                link(dve.reciprocal(rz[:, :], Z[:, :]))
                link(dve.tensor_tensor(rz[:, 1:2], rz[:, 1:2], nlam[:, :], ALU.mult))
                link(dve.tensor_scalar(pr[:, 1, 0:w], pr[:, 1, 0:w], rz[:, 1:2], None, ALU.mult))
                link(dve.scalar_tensor_tensor(att[:, 0:w], pr[:, 0, 0:w], rz[:, 0:1], pr[:, 1, 0:w], ALU.mult, ALU.add), s_at)

            def finish(t, n, bank):
                dve.wait_ge(s_pv, NH * (t + 1) if t < NT else NQ + 1)
                if t >= 1:
                    dve.wait_ge(s_ot, t)
                o3, q3 = (x[0:n, :].rearrange("p (h v) -> p h v", h=NH) for x in (o, osq))
                link(dve.tensor_copy(o[0:n, :], ps[0:n, bank, :]), s_oc)
                link(dve.tensor_tensor(osq[0:n, :], o[0:n, :], o[0:n, :], ALU.mult))
                link(dve.tensor_reduce(ost[0:n, 0, :], q3, AX.X, ALU.add))
                link(dve.tensor_scalar(ost[0:n, 0, :], ost[0:n, 0, :], 1.0 / DV, 1e-5, ALU.mult, ALU.add), s_ms)
                dve.wait_ge(s_rs, t + 1)
                link(dve.reciprocal(ost[0:n, 2, :], ost[0:n, 1, :]))
                link(dve.tensor_tensor(o3, o3, ost[0:n, 2, :].unsqueeze(2).broadcast_to([n, NH, DV]), ALU.mult))
                link(dve.tensor_tensor(o[0:n, :], o[0:n, :], subw[0:n, :], ALU.mult), s_on)

            dve.wait_ge(s_st, 1)
            link(dve.tensor_reduce(sst[:, 0:1], ps[0:NB * 8, 0:2, :].rearrange("p a b -> p (a b)"), AX.X, ALU.max))
            link(dve.tensor_tensor(sst[:, 1:2], sst[:, 0:1], ps[0:NB * 8, 2, 0:1], ALU.max))
            link(dve.tensor_scalar(sst[:, 2:3], sst[:, 1:2], -SCALE, None, ALU.mult), s_smx)
            dve.wait_ge(s_sex, 1)
            link(dve.tensor_tensor(sst[:, 4:5], sst[:, 3:4], PT[:, PAST:PAST + 1], ALU.add))
            link(dve.reciprocal(sst[:, 5:6], sst[:, 4:5]))
            link(dve.scalar_tensor_tensor(sst[:, 6:7], c("map")[0:NB * 8, 1:2], nlam[0:NB * 8, :], c("map")[0:NB * 8, 0:1], ALU.mult, ALU.add))
            link(dve.tensor_tensor(sst[:, 7:8], sst[:, 6:7], sst[:, 5:6], ALU.mult))
            link(dve.tensor_scalar(PT[:, :], PT[:, :], sst[:, 7:8], None, ALU.mult), s_sP)
            dve.wait_ge(s_sT, 1)
            dve.tensor_reduce(attS[:, :, :], ps[:, 3, :].rearrange("p (g x y) -> p g x y", g=NPG, y=2), AX.X, ALU.add)
            link(dve.tensor_reduce(attN[:, :], ps[0:NB, 7, 0:NB * 8].rearrange("p (x y) -> p x y", y=2), AX.X, ALU.add))
            link(dve.tensor_tensor(attD[:, :, :], attN[:, :].rearrange("r (b h) -> r b h", h=NH), own.broadcast_to([NB, NB, NH]),
                                   ALU.mult))
            for b in range(NB):
                link(dve.tensor_copy(attB[:, b, :, b * NH:(b + 1) * NH], attS[:, :, b * NH:(b + 1) * NH]), s_sA if b == NB - 1 else None)
            soft(0)
            for n in range(NQ):
                combine(n)
                if n + 1 < NQ:
                    soft(n + 1)
                if n % NH == 0 and n:
                    finish(n // NH - 1, P, 6)
            finish(NT - 1, P, 6)
            dve.wait_ge(s_so, 1)
            link(dve.tensor_tensor(osum[:, :].rearrange("r (h v) -> r h v", h=NH), ps[0:NB * NH, 7, :].rearrange("r (h v) -> r h v", h=NH),
                                   c("own4")[0:NB * NH].unsqueeze(2).broadcast_to([NB * NH, NH, DV]), ALU.mult), s_soc)
            finish(NT, NB, 7)


def phase_peer(nc, io, m):
    ctx = ExitStack()
    with ctx:
        sb = lambda n, s, dt=F32: ctx.enter_context(nc.sbuf_tensor("p_" + n, s, dt))
        sem = lambda n: ctx.enter_context(nc.semaphore("p_" + n))
        ps, c = m.ps, m.c
        G = 4
        W2 = 2 * G
        PARTS = PKH
        ITERS = TOPK // W2
        PASSES = SLOTS // W2
        NTT = NT + 1
        w_out = m.w_out
        wq = sb("wq", [P, KT, D])
        skT = sb("skT", [P, PKH, NKEY])
        ln = sb("ln", [P, 4, D])
        xin = sb("xin", [P, D])
        junk = sb("junk", [P, D])
        x1 = sb("x1", [P, 2, D])
        x1T = sb("x1T", [P, KT, P])
        qT = xin[:, :].rearrange("p (k t) -> p k t", k=KT)
        st = sb("st", [P, 2, 8])
        s = sb("s", [P, 2 * PKH, NKEY])
        work = sb("work", [P, 256])
        vals = sb("vals", [P, 2, TOPK])
        ix = sb("ix", [P, 2, TOPK], U32)
        ixf = sb("ixf", [P, 2, TOPK])
        cand = sb("cand", [P, TOPK, TOPK])
        eq = sb("eq", [P, TOPK, TOPK])
        tv = sb("tv", [P, 2, TOPK])
        sel = sb("sel", [P, TOPK], U32)
        sab = sb("sab", [P, 2, TOPK], U32)
        sabf = sb("sabf", [P, 2, TOPK])
        ia = sb("ia", [P, 2, TOPK])
        nmax = sb("nmax", [P, 2])
        gex = sb("gex", [P, 2, TOPK])
        gz = sb("gz", [P, 2])
        gr = sb("gr", [P, 1])
        idx = sb("idx", [P, 2, SLOTS], I32)
        gate = sb("gate", [P, 2, SLOTS])
        Ur = sb("Ur", [P, W2, D])
        Vr = sb("Vr", [P, W2, D])
        idxu = sb("idxu", [P, W2], I32)
        idxv = sb("idxv", [P, W2], I32)
        dot = sb("dot", [P, W2])
        gel = sb("gel", [P, W2])
        wgt = sb("wgt", [P, W2])
        dg = sb("dg", [P, G, P])
        idr = sb("idr", [P, PKH], I32)
        gtr = sb("gtr", [P, PKH])
        wsel = sb("wsel", [P, PKH, NB])

        s_ln, s_ld, s_wq = sem("ln"), sem("ld"), sem("wq")
        s_x = sem("x")
        s_op = m.s_op
        s_res = sem("res")
        s_xr = sem("xr")
        s_vr, s_rt = [sem(f"vr{i}") for i in range(2)], [sem(f"rt{i}") for i in range(2)]
        s_x1, s_tr, s_trc = sem("x1"), sem("tr"), sem("trc")
        s_q, s_qc, s_sc, s_scc = sem("q"), sem("qc"), sem("sc"), sem("scc")
        s_tv, s_ge = sem("tv"), sem("ge")
        s_idx = sem("idx")
        s_gate = sem("gate")
        s_u = [sem(f"u{i}") for i in range(W2)]
        s_vv = [sem(f"v{i}") for i in range(W2)]
        s_turn = sem("turn")
        s_iu, s_iv = sem("iu"), sem("iv")
        s_dot = sem("dot")
        s_gel, s_w, s_dg = sem("gel"), sem("w"), sem("dg")
        s_vu = sem("vu")
        s_acc = sem("acc")
        s_y, s_yo = sem("y"), sem("yo")
        s_rs, s_rep, s_repc, s_ws = sem("rs"), sem("rep"), sem("repc"), sem("ws")
        s_v, s_a = sem("v"), sem("a")
        rows_of = lambda t: P if t < NT else NB
        qz = junk[:, 0:PKH * (NB * PKH + 1)]
        qz_in = qz.rearrange("p (h r) -> p h r", h=PKH)[:, :, 0:NB * PKH:PKH]
        qz_of = lambda h: qz[:, NB * PKH * h:NB * PKH * (h + 1)]
        rows_at = lambda t: P if t < NT else NB * PKH

        def schedule(eng_gather, eng_finish, eng_head, eng_prep):
            for stage in range(6):
                eng_prep(0, stage)
            for h in range(2):
                eng_head(0, h)
            for t in range(NT):
                for part in range(PARTS):
                    if t == NT - 1 and part == PARTS - 1:
                        eng_head(NT, 1)
                    eng_gather(t, part)
                    if part < 2 and t:
                        eng_finish(t - 1, part)
                    if part < 5:
                        eng_prep(t + 1, part)
                    if part < 6:
                        eng_head(t, part + 2)
                    elif t + 1 < NT or part == 6:
                        eng_head(t + 1, part - 6)
                    if part == 5:
                        eng_prep(t + 1, part)

        block = ctx.enter_context(nc.Block())

        @block.sync
        def _(sp):
            sp.dma_start(xin[:, :], io["x_tok"][0:P, :]).then_inc(s_x, 16)
            for j, n in enumerate(("ln1_w", "ln1_b")):
                sp.dma_start(ln[:, j, :], io[n].partition_broadcast(P)).then_inc(s_ln, 16)
            sp.dma_start(wq[:, :, :], io["pk_wq"].rearrange("(k p) n -> p k n", p=P)).then_inc(s_wq, 16)
            sp.dma_start(skT[:, :, :], io["skT"]).then_inc(s_ld, 16)
            for j, n in enumerate(("ln2_w", "ln2_b")):
                sp.dma_start(ln[:, 2 + j, :], io[n].partition_broadcast(P)).then_inc(s_ld, 16)
            for t in range(1, NTT):
                n = rows_of(t)
                sp.wait_ge(s_sc, 2 * t)
                sp.dma_start(xin[0:n, :], io["x_tok"][t * P:t * P + n, :]).then_inc(s_x, 16)
                if t >= 2:
                    sp.wait_ge(s_y, t - 1)
                    sp.dma_start(io["y_out"][(t - 2) * P:(t - 1) * P, :], x1[:, t % 2, :]).then_inc(s_yo, 16)
            own = lambda a: a[0:NB * PKH, NT % 2, 0:TOPK].rearrange("r (a w) -> r a w", a=2)
            sp.wait_ge(s_idx, PKH * NT + 1)
            sp.dma_start(idr[:, :], own(idx)).then_inc(s_rs, 16)
            sp.wait_ge(s_rs, 16)
            sp.wait_ge(s_gate, PKH * NT + 1)
            sp.dma_start(gtr[:, :], own(gate)).then_inc(s_rs, 16)
            for t in range(NTT - 2, NTT):
                sp.wait_ge(s_y, t + 1)
                n = rows_of(t)
                sp.dma_start(io["y_out"][t * P:t * P + n, :], x1[0:n, t % 2, :]).then_inc(s_yo, 16)
            sp.wait_ge(s_yo, 16 * NTT)

        @block.gpsimd
        def _(pool):
            def row(table, dst, at, s_to):
                pool.indirect_dma_start(out=dst, out_offset=None, in_=io[table],
                                        in_offset=bass.IndirectOffsetOnAxis(ap=at, axis=0)).then_inc(s_to, 16)

            for t in range(NT):
                for part in range(PARTS):
                    pool.wait_ge(s_idx, PKH * t + part + 1)
                    it0 = ITERS * part
                    done = 2 * (PASSES * t + it0)
                    with pool.Fori(0, ITERS) as i:
                        for half in range(2):
                            col = idx[:, t % 2, bass.ds(W2 * i + (W2 * it0 + half * G), G)]
                            hs = slice(half * G, (half + 1) * G)
                            pool.wait_ge(s_dot, 2 * i + (done + half + 1))
                            pool.sem_inc(s_turn, 1)
                            pool.tensor_copy(idxu[:, hs], col).then_inc(s_iu, 1)
                            pool.wait_ge(s_iu, 2 * i + (done + half + 1))
                            pool.sem_inc(s_turn, 1)
                            for q in range(half * G, (half + 1) * G):
                                row("peer_u", Ur[:, q, :], idxu[:, q:q + 1], s_u[q])
                            pool.wait_ge(s_vu, 2 * i + (done + half + 1))
                            pool.sem_inc(s_turn, 1)
                            pool.tensor_copy(idxv[:, hs], col).then_inc(s_iv, 1)
                            pool.wait_ge(s_iv, 2 * i + (done + half + 1))
                            pool.sem_inc(s_turn, 1)
                            for q in range(half * G, (half + 1) * G):
                                row("peer_v", Vr[:, q, :], idxv[:, q:q + 1], s_vv[q])
            pool.wait_ge(s_rs, 16)
            done = 2 * (PASSES * NT)
            for half in range(2):
                pool.wait_ge(s_dot, done + half + 1)
                for h in range(half * G, (half + 1) * G):
                    row("peer_u", Ur[:, h, :], idr[:, h:h + 1], s_u[h])
                pool.wait_ge(s_vu, done + half + 1)
                for h in range(half * G, (half + 1) * G):
                    row("peer_v", Vr[:, h, :], idr[:, h:h + 1], s_vv[h])

        @block.tensor
        def _(pe):
            def prep(t, stage):
                n = rows_of(t)
                if stage < 2 and t:
                    if stage == 0:
                        pe.wait_ge(s_scc, 4 * t)
                    for k in range(KT):
                        mm = pe.matmul(ps[0:n, stage, :], m.mixT[:, k, t * P:t * P + n], w_out[:, k, stage * 512:(stage + 1) * 512],
                                       start=(k == 0), stop=(k == KT - 1))
                    mm.then_inc(s_op, 1)
                if stage == 3:
                    pe.wait_ge(s_x1, t + 1)
                    for a in range(2):
                        for k in range(4 * a, 4 * a + 4):
                            mm = pe.transpose(ps[:, 2 + a, (k % 4) * P:(k % 4) * P + n], x1[0:n, t % 2, k * P:(k + 1) * P],
                                              c("ident")[0:n, 0:n])
                        mm.then_inc(s_tr, 1)
                    pe.wait_ge(s_trc, 2 * t + 2)
                    if t == 0:
                        pe.wait_ge(s_wq, 16)
                if stage == 3 or stage == 4:
                    a = stage - 3
                    for f in range(4 * a, 4 * a + 4):
                        for k in range(KT):
                            mm = pe.matmul(ps[:, a, (f % 4) * P:(f % 4) * P + n], wq[:, k, f * P:(f + 1) * P], x1T[:, k, 0:n],
                                           start=(k == 0), stop=(k == KT - 1))
                    mm.then_inc(s_q, 1)
                if t == 0 and stage == 3:
                    scores(t, 0)
                if stage == 5:
                    if t < NT:
                        for part in range(2) if t else (1,):
                            scores(t, part)
                    else:
                        pe.wait_ge(s_qc, 2 * t + 2)
                        for x in range(2):
                            half = slice(x * DH, (x + 1) * DH)
                            for h in range(PKH):
                                mm = pe.matmul(ps[0:NB * PKH, 2 * x, 0:NKEY], qz_of(h)[half], skT[half, h, :],
                                               start=(h == 0), stop=(h == PKH - 1))
                        mm.then_inc(s_sc, 2)

            def scores(t, part):
                pe.wait_ge(s_qc, 2 * t + 1 + part)
                if t == 0 and part == 0:
                    pe.wait_ge(s_ld, 48)
                for x in range(2):
                    half = slice(x * DH, (x + 1) * DH)
                    for h in range(4 * part, 4 * part + 4):
                        mm = pe.matmul(ps[:, 2 * x + part, (h % 4) * P:(h % 4 + 1) * P], qT[half, h, :], skT[half, h, :],
                                       start=True, stop=True)
                mm.then_inc(s_sc, 1)

            def head(t, h):
                if t == NT and h == 1:
                    pe.wait_ge(s_scc, 4 * NT + 1)
                    for a in range(2):
                        mm = pe.matmul(ps[:, a, :], c("spread")[0:NB, :], x1[0:NB, NT % 2, a * 512:(a + 1) * 512], start=True, stop=True)
                    mm.then_inc(s_rep, 1)

            def gather(t, part):
                acc = ps[:, 4 + 2 * (t % 2):6 + 2 * (t % 2), :]
                if part == 0:
                    if t >= 2:
                        pe.wait_ge(s_res, t - 1)
                    for a in range(2):
                        pe.matmul(acc[:, a, :], m.zero[0:1, :], wq[0:1, 0, 0:512], start=True, stop=False, skip_group_check=True)
                it0 = ITERS * part
                done = 2 * (PASSES * t + it0)
                with pe.Fori(0, ITERS) as i:
                    for half in range(2):
                        for q in range(half * G, (half + 1) * G):
                            pe.wait_ge(s_dg, W2 * i + (G * done + q + 1))
                            pe.wait_ge(s_vv[q], 16 * i + (8 * done + 16))
                            for a in range(2):
                                mm = pe.matmul(acc[:, a, :], dg[:, q % G, :], Vr[:, q, a * 512:(a + 1) * 512],
                                               start=False, stop=False, skip_group_check=True)
                        mm.then_inc(s_vu, 1)
                if part == PARTS - 1:
                    for a in range(2):
                        mm = pe.matmul(acc[:, a, :], m.zero[0:1, :], wq[0:1, 0, 0:512], start=False, stop=True, skip_group_check=True)
                    mm.then_inc(s_acc, 1)

            schedule(gather, lambda t, x: None, head, prep)
            for h in range(PKH):
                if h % G == 0:
                    pe.wait_ge(s_ws, h // G + 1)
                pe.wait_ge(s_vv[h], 16 * (PASSES * NT + 1))
                for a in range(2):
                    mm = pe.matmul(ps[0:NB, 4 + a, :], wsel[:, h, :], Vr[:, h, a * 512:(a + 1) * 512],
                                   start=(h == 0), stop=(h == PKH - 1), skip_group_check=True)
            mm.then_inc(s_acc, 1)

        @block.scalar
        def _(act):
            def root(which, k, n):
                act.wait_ge(s_vr[which], k)
                act.activation(st[0:n, which, 4:5], st[0:n, which, 3:4], ACT.Sqrt).then_inc(s_rt[which], 1)

            def finish(t, x):
                if x == 0:
                    root(1, t + 1, rows_of(t))

            def head(t, h):
                n = rows_at(t)
                if t == NT and h == 1:
                    act.wait_ge(s_rep, 1)
                    act.activation(xin[:, :], ps[:, 0:2, :].rearrange("p a b -> p (a b)"), ACT.Copy).then_inc(s_repc, 1)
                    return
                k = PKH * t + h
                act.wait_ge(s_tv, k + 1)
                act.activation(gex[0:n, h % 2, :], tv[0:n, h % 2, :], ACT.Exp, bias=nmax[0:n, h % 2:h % 2 + 1],
                               accum_out=gz[0:n, h % 2:h % 2 + 1]).then_inc(s_ge, 1)

            def prep(t, stage):
                n = rows_of(t)
                if stage == 2:
                    root(0, t + 1, n)
                if stage == 3:
                    for a in range(2):
                        act.wait_ge(s_tr, 2 * t + a + 1)
                        act.activation(x1T[:, 4 * a:4 * a + 4, 0:n], ps[:, 2 + a, :].rearrange("p (k t) -> p k t", k=4)[:, :, 0:n],
                                       ACT.Copy).then_inc(s_trc, 1)
                if stage == 3 or stage == 4:
                    a = stage - 3
                    act.wait_ge(s_q, 2 * t + a + 1)
                    to = (qT if t < NT else qz_in)[:, 4 * a:4 * a + 4, 0:n]
                    act.activation(to, ps[:, a, :].rearrange("p (k t) -> p k t", k=4)[:, :, 0:n], ACT.Copy).then_inc(s_qc, 1)
                if t == 0 and stage == 3:
                    scores(t, 0)
                if stage == 5:
                    if t:
                        act.wait_ge(s_idx, PKH * t)
                    if t < NT:
                        for part in range(2) if t else (1,):
                            scores(t, part)
                    else:
                        act.wait_ge(s_sc, 2 * t + 2)
                        act.activation(s[0:NB * PKH, 0:2, :], ps[0:NB * PKH, 0:4, :].rearrange("p (x a) k -> p x a k", a=2)[:, :, 0, 0:NKEY],
                                       ACT.Copy).then_inc(s_scc, 1)

            def scores(t, part):
                act.wait_ge(s_sc, 2 * t + part + 1)
                for x in range(2):
                    a = 2 * x + part
                    act.activation(s[:, 4 * a:4 * a + 4, :], ps[:, a, :].rearrange("p (k t) -> p k t", k=4), ACT.Copy).then_inc(s_scc, 1)

            def gather(t, part):
                done = 2 * (PASSES * t + ITERS * part)
                with act.Fori(0, ITERS) as i:
                    for half in range(2):
                        hs = slice(half * G, (half + 1) * G)
                        act.wait_ge(s_dot, 2 * i + (done + half + 3))
                        act.activation(gel[:, hs], dot[:, hs], ACT.Gelu).then_inc(s_gel, 1)
                        act.wait_ge(s_w, 2 * i + (done + half + 1))
                        act.wait_ge(s_vu, 2 * i + (done + half + 2))
                        for q in range(half * G, (half + 1) * G):
                            act.activation(dg[:, q % G, :], c("ident"), ACT.Copy, scale=wgt[:, q:q + 1]).then_inc(s_dg, 1)

            schedule(gather, finish, head, prep)
            for half in range(2):
                hs = slice(half * G, (half + 1) * G)
                act.wait_ge(s_dot, 2 * (PASSES * NT) + half + 3)
                act.activation(gel[:, hs], dot[:, hs], ACT.Gelu).then_inc(s_gel, 1)
            root(1, NT, P)
            root(1, NTT, NB)

        @block.vector
        def _(dve):
            link = Link(dve, s_v)

            def spread(which, x, add, xin_, n, s_read):
                v = lambda j: st[0:n, which, j:j + 1]
                for a in range(2):
                    cs = slice(a * 512, (a + 1) * 512)
                    last = dve.scalar_tensor_tensor(x[:, cs], xin_[:, cs], ALPHA, add[:, a, :], ALU.mult, ALU.add, accum_out=v(a))
                link(last, s_read)
                link(dve.tensor_scalar(v(2), v(0), v(1), -1.0 / D, ALU.add, ALU.mult))
                link(dve.tensor_scalar(x, x, v(2), None, ALU.add))
                link(dve.tensor_tensor_reduce(junk[0:n, :], x, x, 1.0, 0.0, ALU.mult, ALU.add, v(5)))
                link(dve.tensor_scalar(v(3), v(5), 1.0 / D, 1e-5, ALU.mult, ALU.add), s_vr[which])

            def scale(which, k, x, n, s_to):
                v = lambda j: st[0:n, which, j:j + 1]
                dve.wait_ge(s_rt[which], k)
                if k == 1:
                    dve.wait_ge(*((s_ln, 32), (s_ld, 48))[which])
                link(dve.reciprocal(v(6), v(4)))
                link(dve.scalar_tensor_tensor(x, x, v(6), ln[0:n, 2 * which, :], ALU.mult, ALU.mult))
                link(dve.tensor_tensor(x, x, ln[0:n, 2 * which + 1, :], ALU.add), s_to)

            def top16(val, ind, src, n):
                w = work[0:n, 0:src.shape[1]]
                link(dve.max(val[:, 0:8], src))
                dve.max_index(ind[:, 0:8], val[:, 0:8], src)
                link(dve.match_replace(w, val[:, 0:8], src, -3.0e38))
                link(dve.max(val[:, 8:16], w))
                return dve.max_index(ind[:, 8:16], val[:, 8:16], w)

            def gates(t, h):
                n = rows_at(t)
                k = PKH * t + h
                dve.wait_ge(s_ge, k + 1)
                link(dve.reciprocal(gr[0:n, :], gz[0:n, h % 2:h % 2 + 1]))
                link(dve.tensor_scalar(gate[0:n, t % 2, TOPK * h:TOPK * (h + 1)], gex[0:n, h % 2, :], gr[0:n, :], None,
                                       ALU.mult), s_gate)

            def head(t, h):
                n = rows_at(t)
                if h:
                    gates(t, h - 1)
                elif t:
                    gates(t - 1, PKH - 1)
                if t == NT and h == 1:
                    return
                if h == 0 or (h == 4 and t < NT):
                    dve.wait_ge(s_scc, 4 * t + (h // 2 + 2 if t < NT else 1))
                for x in range(2):
                    link(top16(vals[0:n, x, :], ix[0:n, x, :], s[0:n, x * PKH + h if t < NT else x, :], n))
                link(dve.tensor_copy(ixf[0:n], ix[0:n]))
                link(dve.tensor_tensor(cand[0:n], vals[0:n, 0, :].unsqueeze(2).broadcast_to([n, TOPK, TOPK]),
                                       vals[0:n, 1, :].unsqueeze(1).broadcast_to([n, TOPK, TOPK]), ALU.add))
                link(top16(tv[0:n, h % 2, :], sel[0:n, :], cand[0:n].rearrange("p a b -> p (a b)"), n))
                link(dve.tensor_scalar(nmax[0:n, h % 2:h % 2 + 1], tv[0:n, h % 2, 0:1], -1.0, None, ALU.mult), s_tv)
                dve.tensor_scalar(sab[0:n, 0, :], sel[0:n, :], 4, None, ALU.logical_shift_right)
                link(dve.tensor_scalar(sab[0:n, 1, :], sel[0:n, :], 15, None, ALU.bitwise_and))
                link(dve.tensor_copy(sabf[0:n], sab[0:n]))
                for x in range(2):
                    link(dve.tensor_tensor(eq[0:n], sabf[0:n, x, :].unsqueeze(2).broadcast_to([n, TOPK, TOPK]),
                                           c("iota16")[0:n].unsqueeze(1).broadcast_to([n, TOPK, TOPK]), ALU.is_equal))
                    link(dve.tensor_tensor(eq[0:n], eq[0:n], ixf[0:n, x, :].unsqueeze(1).broadcast_to([n, TOPK, TOPK]), ALU.mult))
                    link(dve.tensor_reduce(ia[0:n, x, :], eq[0:n], AX.X, ALU.add))
                link(dve.scalar_tensor_tensor(idx[0:n, t % 2, TOPK * h:TOPK * (h + 1)], ia[0:n, 0, :], float(NKEY), ia[0:n, 1, :],
                                              ALU.mult, ALU.add), s_idx)

            def prep(t, stage):
                n = rows_of(t)
                x = x1[0:n, t % 2, :]
                if stage == 2:
                    dve.wait_ge(s_op, 2 * t + 2)
                    dve.wait_ge(s_x, 16 * (t + 1))
                    if t >= 2:
                        dve.wait_ge(s_yo, 16 * (t - 1))
                    spread(0, x, ps[0:n, 0:2, :], xin[0:n, :], n, s_xr)
                if stage == 3:
                    if t == NT:
                        dve.memset(qz, 0.0)
                    scale(0, t + 1, x, n, s_x1)

            def gather(t, part):
                it0 = ITERS * part
                done = 2 * (PASSES * t + it0)
                with dve.Fori(0, ITERS) as i:
                    for half in range(2):
                        for q in range(half * G, (half + 1) * G):
                            dve.wait_ge(s_u[q], 16 * i + (8 * done + 16))
                            ins = dve.tensor_tensor_reduce(Ur[:, q, :], Ur[:, q, :], x1[:, t % 2, :], 1.0, 0.0, ALU.mult, ALU.add,
                                                           dot[:, q:q + 1])
                        ins.then_inc(s_dot, 1)
                        hs = slice(half * G, (half + 1) * G)
                        dve.wait_ge(s_gel, 2 * i + (done + half + 1))
                        dve.tensor_tensor(wgt[:, hs], gel[:, hs], gate[:, t % 2, bass.ds(W2 * i + (W2 * it0 + half * G), G)],
                                          ALU.mult).then_inc(s_w, 1)

            def finish(t, step):
                n = rows_of(t)
                x = x1[0:n, t % 2, :]
                bank = 4 + 2 * (t % 2)
                if step == 0:
                    dve.wait_ge(s_acc, t + 1)
                    spread(1, x, ps[0:n, bank:bank + 2, :], x, n, s_res)
                else:
                    scale(1, t + 1, x, n, s_y)

            for q in (s_dot, s_vu):
                for _ in range(2):
                    dve.engine_nop().then_inc(q, 1)
            schedule(gather, finish, head, prep)
            dve.wait_ge(s_repc, 1)
            for half in range(2):
                hs = slice(half * G, (half + 1) * G)
                for h in range(half * G, (half + 1) * G):
                    dve.wait_ge(s_u[h], 16 * (PASSES * NT + 1))
                    ins = dve.tensor_tensor_reduce(Ur[:, h, :], Ur[:, h, :], xin[:, :], 1.0, 0.0, ALU.mult, ALU.add, dot[:, h:h + 1])
                ins.then_inc(s_dot, 1)
                dve.wait_ge(s_gel, 2 * (PASSES * NT) + half + 1)
                if half == 0:
                    dve.wait_ge(s_rs, 32)
                link(dve.tensor_tensor(wgt[:, hs], gel[:, hs], gtr[:, hs], ALU.mult))
                link(dve.tensor_tensor(wsel[:, hs, :], wgt[:, hs].unsqueeze(2).broadcast_to([P, G, NB]),
                                       c("gather").unsqueeze(1).broadcast_to([P, G, NB]), ALU.mult), s_ws)
            for t in range(NT - 1, NTT):
                for step in range(2):
                    finish(t, step)


class Mem:
    pass


def build(nc, io, upto=9, debug=None):
    root = ExitStack()
    with root:
        m = Mem()
        sb0 = lambda n, s, dt=F32: root.enter_context(nc.sbuf_tensor(n, s, dt))
        m.ps = root.enter_context(nc.psum_tensor("ps", [P, 8, 512], F32))
        tables = [sb0("table_long", TABLES[0].shape)]
        m.params = sb0("params", [P, NPAR])
        m.par = lambda n, i: m.params[:, PAR[n] + i:PAR[n] + i + 1]
        m.c = lambda n: tables[WHERE[n][0]][:, WHERE[n][1]:WHERE[n][1] + WHERE[n][2]]
        m.mixT = sb0("mixT", [P, KT, SEQ + NB])
        m.omka = sb0("omka", [P, HP])
        m.zero = sb0("zero", [1, P])
        m.w_out = sb0("w_out", [P, KT, D])
        m.s_wout = root.enter_context(nc.semaphore("s_wout"))
        m.s_op = root.enter_context(nc.semaphore("s_op"))
        lent = m.w_out[:, :, :].rearrange("p k n -> p (k n)")
        m.ar = lent[:, 0:HP * 2 * TA].rearrange("p (i x t) -> p i x t", i=HP, x=2)
        m.bt = lent[:, HP * 2 * TA:HP * 3 * TA].rearrange("p (i t) -> p i t", i=HP)
        mid = ExitStack()
        with mid:
            sb = lambda n, s, dt=F32: mid.enter_context(nc.sbuf_tensor(n, s, dt))
            tables.append(sb("table_short", TABLES[1].shape))
            m.w2a2 = sb("w2a2", [P, RWW])
            m.g2 = sb("g2", [P, RWW])
            m.shift0 = sb("shift0", [P, NCH, NB])
            m.shout = sb("shout", [P, NCH, 1 + NB])
            m.pt = sb("pt", [P, NB * NPG], I32)
            m.idx = sb("idx", [P, NB * NPG], I32)
            m.sc = sb("sc", [P, NPG, NB * 8])
            m.q_rows = nc.dram_tensor("q_rows", (NB, RWW), F32, kind="Internal").ap()
            m.qT = sb("qT", [P, NH, SEQ])
            m.qTs = sb("qTs", [P, NH, NB])
            m.kT = sb("kT", [P, NH, TP])
            m.vtok = sb("vtok", [P, NT + 1, RWW])
            m.vmeta = sb("vmeta", [NMETA, RWW])
            m.qks = sb("qks", [SM, 2, RWW])
            m.kt = sb("kt", [P, HP, TA])
            m.rk = sb("rk", [P, HP, TA])
            m.vT = sb("vT", [P, HP, TA])
            m.sg = sb("sg", [P, TA])
            m.eend = sb("eend", [P, HP, 17])
            m.consts = [(tables[0][:, :], io["table0"]), (tables[1][:, :], io["table1"]), (m.params[:, :], io["params"]), (m.w2a2[:, :], io["w2a2"]),
                        (m.g2[:, :], io["g2"]), (m.pt[:, :], io["pages"].partition_broadcast(P)),
                        (m.shift0[:, :, :], io["shift0"])]
            phase_project(nc, io, m)
            if debug:
                debug(nc, m, 1)
            if upto <= 1:
                return
            phase_rwkv(nc, io, m)
            if debug:
                debug(nc, m, 2)
            if upto <= 2:
                return
            phase_attention(nc, io, m)
            if debug:
                debug(nc, m, 3)
            if upto <= 3:
                return
        phase_peer(nc, io, m)


def arrange(x):
    a = {}
    chan = lambda v: np.asarray(v).reshape(-1, P).T
    a["table0"], a["table1"] = TABLES
    a["params"] = np.concatenate([chan(x["mu_shift"][0]), chan(x["w0"][0]), chan(x["a0"][0]), chan(x["k_k"][0]),
                                  chan(x["k_a"][0]), chan(x["r_k"][0])], 1)
    a["w2a2"] = np.concatenate([x["w2_decay"][0], x["a2"][0]], 0)
    a["g2"] = x["g2"][0]
    a["shift0"] = np.asarray(x["state_shift"][0]).reshape(NB, NCH, P).transpose(2, 1, 0)
    a["xT"] = np.concatenate([x["x_prompt"][0], x["x_sample"][:, 0], x["meta_tokens"]], 0).T
    a["w_in"] = x["w_in"][0]
    a["lnx_w"], a["lnx_b"] = x["lnx_w"][0], x["lnx_b"][0]
    a["state"] = np.asarray(x["state_wkv"][0]).reshape(NB, HP, 2, DH, DH).transpose(2, 4, 0, 1, 3).reshape(P, NB, HP, DH)
    a["w_out"], a["pk_wq"] = x["w_out"][0], x["pk_wq"][0]
    a["peer_u"], a["peer_v"] = x["peer_u"][0], x["peer_v"][0]
    for n in ("ln1_w", "ln1_b", "ln2_w", "ln2_b"):
        a[n] = x[n][0]
    a["skT"] = np.asarray(x["pk_subkeys"][0]).transpose(1, 3, 0, 2).reshape(P, PKH, NKEY)
    a["x_tok"] = np.concatenate([x["x_prompt"][0], x["x_sample"][:, 0]], 0)
    a["pages"] = np.asarray(x["page_table"]).reshape(-1)
    a["lams"] = np.stack([x["lam_q1"][0], x["lam_k1"][0], x["lam_q2"][0], x["lam_k2"][0]])
    a["subln_w"] = x["subln_w"][0]
    a["cache_k"] = np.asarray(x["cache_k"][0]).reshape(-1, RWW)
    a["cache_v"] = np.asarray(x["cache_v"][0]).reshape(-1, RWW)
    return {k: np.ascontiguousarray(v) for k, v in a.items()}


_OUTS = {
    "y_out": (SEQ + NB, D), "k_out": (TA, RWW), "v_out": (TA, RWW), "shift_out": (P, NCH, 1 + NB),
    "wkv_p_out": (P, HP, DH), "wkv_s_out": (P, NB, HP, DH),
}


def returned(r):
    y = r["y_out"]
    tokens = lambda a: np.concatenate([a[SEQ + NB:], a[:SEQ]], 0)
    k, v = r["k_out"], r["v_out"]
    sh = r["shift_out"].transpose(2, 1, 0).reshape(1 + NB, RWC)
    wp = r["wkv_p_out"].reshape(2, DH, HP, DH).transpose(2, 0, 3, 1).reshape(1, 1, 2 * HP, DH, DH)
    ws = r["wkv_s_out"].reshape(2, DH, NB, HP, DH).transpose(2, 3, 0, 4, 1).reshape(1, NB, 2 * HP, DH, DH)
    out = (y[None, :SEQ], y[SEQ:, None], tokens(k).reshape(1, 1, TP, NH, 2, DH), tokens(v).reshape(1, 1, TP, NH, DV),
           wp, sh[None, 0:1], k[SEQ:SEQ + NB].reshape(1, NB, 1, NH, 2, DH), v[SEQ:SEQ + NB].reshape(1, NB, 1, NH, DV),
           ws, sh[None, 1:])
    return tuple(np.ascontiguousarray(a) for a in out)


def kernel(**inputs):
    import concourse.bacc as bacc
    from concourse.bass_utils import run_bass_kernel_spmd

    nc = bacc.Bacc("TRN2", target_bir_lowering=False, num_devices=1)
    arrays, io = {}, {}
    for n, a in arrange({k: np.asarray(v) for k, v in inputs.items()}).items():
        arrays[f"in_{n}_dram"] = a
        io[n] = nc.dram_tensor(f"in_{n}_dram", a.shape, mybir.dt.from_np(a.dtype), kind="ExternalInput").ap()
    for n, shape in _OUTS.items():
        io[n] = nc.dram_tensor(f"out_{n}_dram", shape, F32, kind="ExternalOutput").ap()
    build(nc, io)
    r = run_bass_kernel_spmd(nc, [arrays], core_ids=[0])
    return returned({n: r.results[0][f"out_{n}_dram"] for n in _OUTS})
```
